# Optimizing a Trainium2 kernel written in Bass

```python
import math
import jax, jax.numpy as jnp
from jax import lax
import numpy as np

D_MODEL = 1024
BATCH = 1
SEQ = 2048
DEPTH = 1

CTX_LEN = 256
GRID_W = 64
D_MIX = D_MODEL
D_MLSTM = D_MIX // 2
D_HYENA = D_MIX - D_MLSTM
MLSTM_HEADS = 4
MLSTM_HEAD_DIM = D_MLSTM // MLSTM_HEADS
MLSTM_CHUNK = 64
N_GATES = 4 * MLSTM_HEADS
SHORT_CONV = 3
HYENA_ORDER = 2
FILTER_BANDS = 8
FILTER_EMB = 1 + 2 * FILTER_BANDS
FILTER_HIDDEN = 64
DECAY_TARGET = 1e-2
FAST_DECAY_PCT = 0.3
SLOW_DECAY_PCT = 1.5
MIN_DECAY = math.log(DECAY_TARGET) / SLOW_DECAY_PCT
MAX_DECAY = math.log(DECAY_TARGET) / FAST_DECAY_PCT
RMS_EPS = 1e-6
SPLIT_SIZES = [2 * D_MLSTM, D_MLSTM, D_MLSTM, D_MLSTM, N_GATES, (HYENA_ORDER + 1) * D_HYENA, D_HYENA]
D_IN = sum(SPLIT_SIZES)

kernel_name = "hybrid_mlstm_hyena_prefix_dit"

def rms_norm(x, g):
    xf = x.astype(jnp.float32)
    y = xf * lax.rsqrt(jnp.mean(xf * xf, axis=-1, keepdims=True) + RMS_EPS)
    return (y * g.astype(jnp.float32)).astype(x.dtype)

def _conv3(u, w, b):
    p = jnp.pad(u, [(0, 0)] * (u.ndim - 2) + [(1, 1), (0, 0)])
    return p[..., :-2, :] * w[0] + p[..., 1:-1, :] * w[1] + p[..., 2:, :] * w[2] + b

def short_conv(u, w, b, rows):
    if rows is None:
        return _conv3(u, w, b)
    bsz, L, ch = u.shape
    return _conv3(u.reshape(bsz, rows, GRID_W, ch), w, b).reshape(bsz, L, ch)

def mlstm_chunkwise(q, k, v, i_pre, f_pre, state):
    bsz, nh, L, d = q.shape
    nc = L // MLSTM_CHUNK

    def to_chunks(a):
        a = a.reshape((bsz, nh, nc, MLSTM_CHUNK) + a.shape[3:])
        return jnp.moveaxis(a, 2, 0)

    logf = jax.nn.log_sigmoid(f_pre)
    lower = jnp.tril(jnp.ones((MLSTM_CHUNK, MLSTM_CHUNK), dtype=bool))

    def step(carry, inp):
        C, n, m = carry
        qc, kc, vc, ic, fc = inp
        bcum = jnp.cumsum(fc, axis=-1)
        dmat = bcum[..., :, None] - bcum[..., None, :] + ic[..., None, :]
        dmat = jnp.where(lower, dmat, -jnp.inf)
        inter = bcum + m[..., None]
        m_t = jnp.maximum(inter, jnp.max(dmat, axis=-1))
        s = jnp.einsum('bhtd,bhsd->bhts', qc, kc) * jnp.exp(dmat - m_t[..., None])
        w_inter = jnp.exp(inter - m_t)
        num = jnp.einsum('bhts,bhsv->bhtv', s, vc) + w_inter[..., None] * jnp.einsum('bhtk,bhkv->bhtv', qc, C)
        den = jnp.sum(s, axis=-1) + w_inter * jnp.einsum('bhtk,bhk->bht', qc, n)
        h = num / jnp.maximum(jnp.abs(den), jnp.exp(-m_t))[..., None]
        b_last = bcum[..., -1]
        src = b_last[..., None] - bcum + ic
        m_new = jnp.maximum(b_last + m, jnp.max(src, axis=-1))
        ws = jnp.exp(src - m_new[..., None])
        wc = jnp.exp(b_last + m - m_new)
        C_new = wc[..., None, None] * C + jnp.einsum('bhs,bhsk,bhsv->bhkv', ws, kc, vc)
        n_new = wc[..., None] * n + jnp.einsum('bhs,bhsk->bhk', ws, kc)
        return (C_new, n_new, m_new), h

    state, h = lax.scan(step, state, (to_chunks(q), to_chunks(k), to_chunks(v), to_chunks(i_pre), to_chunks(logf)))
    h = jnp.moveaxis(h, 0, 2).reshape(bsz, nh, L, d)
    return h, state

def mlstm_prep(u_qk, v, g, b_gates, conv_w, conv_b, rows):
    bsz, L, _ = v.shape
    qk = jax.nn.silu(short_conv(u_qk, conv_w, conv_b, rows).astype(jnp.float32))
    q, k = jnp.split(qk, 2, axis=-1)

    def heads(a):
        return a.reshape(bsz, L, MLSTM_HEADS, MLSTM_HEAD_DIM).transpose(0, 2, 1, 3).astype(jnp.float32)

    gates = (g + b_gates).astype(jnp.float32).reshape(bsz, L, 4, MLSTM_HEADS).transpose(2, 0, 3, 1)
    return heads(q), heads(k) * (MLSTM_HEAD_DIM ** -0.5), heads(v), gates

def mlstm_bidirectional(ctx_in, lat_in):
    qc, kc, vc, gc = ctx_in
    ql, kl, vl, gl = lat_in
    bsz = qc.shape[0]
    zero = (jnp.zeros((bsz, MLSTM_HEADS, MLSTM_HEAD_DIM, MLSTM_HEAD_DIM), jnp.float32),
            jnp.zeros((bsz, MLSTM_HEADS, MLSTM_HEAD_DIM), jnp.float32),
            jnp.zeros((bsz, MLSTM_HEADS), jnp.float32))
    flip = lambda a: jnp.flip(a, axis=2)
    hc_f, st_f = mlstm_chunkwise(qc, kc, vc, gc[0], gc[1], zero)
    hl_f, _ = mlstm_chunkwise(ql, kl, vl, gl[0], gl[1], st_f)
    hc_b, st_b = mlstm_chunkwise(flip(qc), flip(kc), flip(vc), flip(gc[2]), flip(gc[3]), zero)
    hl_b, _ = mlstm_chunkwise(flip(ql), flip(kl), flip(vl), flip(gl[2]), flip(gl[3]), st_b)
    return hc_f + flip(hc_b), hl_f + flip(hl_b)

def mlstm_output(h, o, zm, mh_gain):
    bsz, nh, L, d = h.shape
    h = h.transpose(0, 2, 1, 3) * jax.nn.sigmoid(o.astype(jnp.float32)).reshape(bsz, L, nh, d)
    h = h * lax.rsqrt(jnp.mean(h * h, axis=-1, keepdims=True) + RMS_EPS)
    h = h.reshape(bsz, L, nh * d) * mh_gain.astype(jnp.float32)
    return h * jax.nn.silu(zm.astype(jnp.float32))

def implicit_filters(L, w1, b1, freq, w2, b2, w3):
    f32 = lambda a: a.astype(jnp.float32)
    pos = jnp.arange(L, dtype=jnp.float32)
    bands = jnp.arange(1, FILTER_BANDS + 1, dtype=jnp.float32)
    ang = (2.0 * math.pi / L) * pos[:, None] * bands[None, :]
    feats = jnp.concatenate([(pos / L)[:, None], jnp.sin(ang), jnp.cos(ang)], axis=-1)
    hdn = jnp.sin(f32(freq[0]) * (feats @ f32(w1) + f32(b1)))
    hdn = jnp.sin(f32(freq[1]) * (hdn @ f32(w2) + f32(b2)))
    filt = (hdn @ f32(w3)).reshape(L, HYENA_ORDER, D_HYENA)
    offset = jnp.abs(pos - L // 2) / (L / 2)
    rates = jnp.abs(jnp.linspace(MIN_DECAY, MAX_DECAY, D_HYENA, dtype=jnp.float32))
    filt = filt * jnp.exp(-offset[:, None, None] * rates)
    return filt * lax.rsqrt(jnp.sum(filt * filt, axis=0, keepdims=True) + RMS_EPS)

def fft_long_conv(u, h, bias):
    L = u.shape[1]
    n = 2 * L
    uf = jnp.fft.rfft(u, n=n, axis=1)
    hf = jnp.fft.rfft(h, n=n, axis=0)
    y = jnp.fft.irfft(uf * hf[None], n=n, axis=1)[:, L // 2: L // 2 + L]
    return y + u * bias

def hyena_mixer(u_hy, zh, rows, conv_w, conv_b, filt, fbias):
    uv = short_conv(u_hy, conv_w, conv_b, rows).astype(jnp.float32)
    v, x1, x2 = jnp.split(uv, 3, axis=-1)
    fb = fbias.astype(jnp.float32)
    z = x1 * fft_long_conv(v, filt[:, 0], fb[0])
    y = x2 * fft_long_conv(z, filt[:, 1], fb[1])
    return y * jax.nn.silu(zh.astype(jnp.float32))

def split_proj(u):
    idx = [int(s) for s in np.cumsum(SPLIT_SIZES)[:-1]]
    return jnp.split(u, idx, axis=-1)

def setup_inputs(seed: int = 0) -> dict:
    key = jax.random.key(seed)
    ks = jax.random.split(key, 24)
    nrm = lambda k, shape, s: jax.random.normal(k, shape, jnp.float32) * s
    fbias = jnp.linspace(3.0, 6.0, MLSTM_HEADS, dtype=jnp.float32)
    zb = jnp.zeros_like(fbias)
    gate_offset = jnp.stack([zb, fbias, zb, fbias])[None]
    b_gates = (nrm(ks[9], (DEPTH, 4, MLSTM_HEADS), 0.1) + gate_offset).reshape(DEPTH, N_GATES)
    return {
        'x': nrm(ks[0], (BATCH, SEQ, D_MODEL), 1.0),
        'c': nrm(ks[1], (BATCH, D_MODEL), 1.0),
        'ctx': nrm(ks[2], (BATCH, CTX_LEN, D_MODEL), 1.0),
        'c_ctx': nrm(ks[3], (D_MODEL,), 1.0),
        'w_mod': nrm(ks[4], (DEPTH, D_MODEL, 3 * D_MODEL), 0.5 * D_MODEL ** -0.5),
        'b_mod': nrm(ks[5], (DEPTH, 3 * D_MODEL), 0.01),
        'pre_gain': 1.0 + nrm(ks[6], (DEPTH, D_MODEL), 0.05),
        'post_gain': 1.0 + nrm(ks[7], (DEPTH, D_MODEL), 0.05),
        'w_in': nrm(ks[8], (DEPTH, D_MODEL, D_IN), D_MODEL ** -0.5),
        'b_gates': b_gates,
        'conv_qk_w': nrm(ks[10], (DEPTH, SHORT_CONV, 2 * D_MLSTM), SHORT_CONV ** -0.5),
        'conv_qk_b': nrm(ks[11], (DEPTH, 2 * D_MLSTM), 0.01),
        'mh_gain': 1.0 + nrm(ks[12], (DEPTH, D_MLSTM), 0.05),
        'hy_conv_w': nrm(ks[13], (DEPTH, SHORT_CONV, (HYENA_ORDER + 1) * D_HYENA), SHORT_CONV ** -0.5),
        'hy_conv_b': nrm(ks[14], (DEPTH, (HYENA_ORDER + 1) * D_HYENA), 0.01),
        'filt_w1': nrm(ks[15], (DEPTH, FILTER_EMB, FILTER_HIDDEN), FILTER_EMB ** -0.5),
        'filt_b1': nrm(ks[16], (DEPTH, FILTER_HIDDEN), 0.01),
        'filt_freq': 1.0 + nrm(ks[17], (DEPTH, 2, FILTER_HIDDEN), 0.05),
        'filt_w2': nrm(ks[18], (DEPTH, FILTER_HIDDEN, FILTER_HIDDEN), FILTER_HIDDEN ** -0.5),
        'filt_b2': nrm(ks[19], (DEPTH, FILTER_HIDDEN), 0.01),
        'filt_w3': nrm(ks[20], (DEPTH, FILTER_HIDDEN, HYENA_ORDER * D_HYENA), FILTER_HIDDEN ** -0.5),
        'filt_bias': nrm(ks[21], (DEPTH, HYENA_ORDER, D_HYENA), 0.1),
        'w_out': nrm(ks[22], (DEPTH, D_MIX, D_MODEL), D_MIX ** -0.5),
    }

def reference(x, c, ctx, c_ctx, w_mod, b_mod, pre_gain, post_gain, w_in, b_gates,
              conv_qk_w, conv_qk_b, mh_gain, hy_conv_w, hy_conv_b, filt_w1, filt_b1,
              filt_freq, filt_w2, filt_b2, filt_w3, filt_bias, w_out):
    rows = x.shape[1] // GRID_W
    L_lat, L_ctx = x.shape[1], ctx.shape[1]
    xl, xc = x, ctx
    s_lat = jax.nn.silu(c)
    s_ctx = jax.nn.silu(c_ctx)
    for l in range(DEPTH):
        last = l == DEPTH - 1
        shift_l, scale_l, gate_l = jnp.split(s_lat @ w_mod[l] + b_mod[l], 3, axis=-1)
        shift_c, scale_c, gate_c = jnp.split(s_ctx @ w_mod[l] + b_mod[l], 3, axis=-1)
        hl = rms_norm(xl, pre_gain[l]) * (1.0 + scale_l[:, None]) + shift_l[:, None]
        hc = rms_norm(xc, pre_gain[l]) * (1.0 + scale_c) + shift_c
        qk_l, v_l, o_l, zm_l, g_l, hy_l, zh_l = split_proj(hl @ w_in[l])
        qk_c, v_c, o_c, zm_c, g_c, hy_c, zh_c = split_proj(hc @ w_in[l])
        ctx_in = mlstm_prep(qk_c, v_c, g_c, b_gates[l], conv_qk_w[l], conv_qk_b[l], None)
        lat_in = mlstm_prep(qk_l, v_l, g_l, b_gates[l], conv_qk_w[l], conv_qk_b[l], rows)
        hm_c, hm_l = mlstm_bidirectional(ctx_in, lat_in)
        m_l = mlstm_output(hm_l, o_l, zm_l, mh_gain[l])
        filt_l = implicit_filters(L_lat, filt_w1[l], filt_b1[l], filt_freq[l], filt_w2[l], filt_b2[l], filt_w3[l])
        y_hy_l = hyena_mixer(hy_l, zh_l, rows, hy_conv_w[l], hy_conv_b[l], filt_l, filt_bias[l])
        y_l = jnp.concatenate([m_l, y_hy_l], axis=-1).astype(xl.dtype) @ w_out[l]
        new_xl = xl + gate_l[:, None] * rms_norm(y_l, post_gain[l])
        if not last:
            m_c = mlstm_output(hm_c, o_c, zm_c, mh_gain[l])
            filt_c = implicit_filters(L_ctx, filt_w1[l], filt_b1[l], filt_freq[l], filt_w2[l], filt_b2[l], filt_w3[l])
            y_hy_c = hyena_mixer(hy_c, zh_c, None, hy_conv_w[l], hy_conv_b[l], filt_c, filt_bias[l])
            y_c = jnp.concatenate([m_c, y_hy_c], axis=-1).astype(xc.dtype) @ w_out[l]
            xc = xc + gate_c * rms_norm(y_c, post_gain[l])
        xl = new_xl
    return xl


_drawn_inputs = setup_inputs


def setup_inputs(seed=0):
    import zlib

    import numpy as np

    out = dict(_drawn_inputs(seed))
    spreads = {}
    factors = {'ctx': 8.0,
     'c_ctx': 8.0,
     'b_mod': 3.095,
     'post_gain': 4.285,
     'b_gates': 2.886,
     'conv_qk_w': 5.265,
     'conv_qk_b': 8.0,
     'mh_gain': 8.0,
     'hy_conv_b': 3.871,
     'filt_b1': 4.315,
     'filt_freq': 2.72,
     'filt_b2': 3.335,
     'filt_bias': 5.1}
    for name, (base, spread) in spreads.items():
        noise = np.random.default_rng([zlib.crc32(name.encode()), seed]).standard_normal(out[name].shape)
        drawn = base * np.exp(spread * noise) if base else spread * noise
        out[name] = __import__('jax').numpy.asarray(drawn.astype(out[name].dtype))
    for name, factor in factors.items():
        out[name] = (out[name] * factor).astype(out[name].dtype)
    return out
```

```python
from contextlib import ExitStack
import math

import numpy as np
import concourse.bass as bass
from concourse import mybir
from concourse.alu_op_type import AluOpType as ALU

ACT = mybir.ActivationFunctionType
AX = mybir.AxisListType
F32 = mybir.dt.float32
F32R = mybir.dt.float32r

P = 128
D = 1024
KD = D // P
T_LAT, T_CTX = 2048, 256
T_ALL = T_CTX + T_LAT
NT_CTX, NT_LAT = T_CTX // P, T_LAT // P
NT = NT_CTX + NT_LAT
ROW = 64
HEADS = 4
DH = 128
CH = 512
EPS = 1e-6
SLOT = 256
N_SLOTS = 18
TILE = 512

N2 = 16
N1 = 192
N = N1 * N2
K1 = N1 // 2
NQ = K1 // 4


def sem_maker(nc, ctx):
    return lambda name: ctx.enter_context(nc.semaphore(name))


def mem_makers(nc, ctx):
    sb = lambda name, shape, dt=F32: ctx.enter_context(nc.sbuf_tensor(name, shape, dt))
    ps = lambda name, shape, dt=F32: ctx.enter_context(nc.psum_tensor(name, shape, dt))
    return sb, ps


def spread(src):
    return src.partition_broadcast(P)


CTX_T = (0, T_CTX)
LAT_T = [(T_CTX + i * TILE, TILE) for i in range(T_LAT // TILE)]
GATE_TILES = 1 + len(LAT_T)
K_TILES, V_TILES, B_TILES, A_TILES = 20, 36, 16, 32
K0 = GATE_TILES
V0 = K0 + K_TILES
Q0 = V0 + V_TILES
O0 = Q0 + 4 * B_TILES
Z0 = O0 + 2 * A_TILES
N_TILES = Z0 + B_TILES
ROOT_D = float(math.sqrt(D))
N_MOD = 8


def project(nc, d, s, svec):
    with ExitStack() as ctx:
        sb, ps = mem_makers(nc, ctx)
        sem = sem_maker(nc, ctx)

        h_hi = sb("h_hi", [P, KD, T_ALL], F32R)
        h_lo = sb("h_lo", [P, KD, T_ALL], F32R)
        w_hi = sb("w_hi", [P, 2, KD, SLOT], F32R)
        w_lo = sb("w_lo", [P, 2, KD, SLOT], F32R)
        stage = sb("stage", [P, 3, KD, SLOT])
        work = sb("work", [P, 3 * D])
        ident = sb("ident", [P, P])
        cvec = sb("cvec", [P, KD, 2])
        bmod = sb("bmod", [P, 2 * KD])
        pgain = sb("pgain", [P, KD])
        mod = sb("mod", [P, 2 * KD, 2])
        gcol = sb("gcol", [P, KD, 2])
        gbias = sb("gbias", [P, 1])
        coef = sb("coef", [P, 20, 4])
        sumsq = sb("sumsq", [P, 3])
        rstd = sb("rstd", [P, 3])
        power = sb("power", [P, 2])
        raw = [work[:, i * TILE:(i + 1) * TILE] for i in range(2)]
        res = [work[:, (2 + i) * TILE:(3 + i) * TILE] for i in range(4)]
        ht = [work[:, i * D:(i + 1) * D].rearrange("p (k t) -> p k t", k=KD) for i in range(3)]
        xrow = [stage[:, i, :, :].rearrange("p k n -> p (k n)")[:, 0:D] for i in range(3)]

        bank = [ps(f"bank{i}", [P, TILE]) for i in range(6)]
        psM = ps("psM", [P, 2 * KD, 2])

        small_loaded = sem("small_loaded")
        mod_loaded = [sem(f"mod_loaded{i}") for i in range(3)]
        mod_used = sem("mod_used")
        svec_ready = sem("svec_ready")
        mod_step = sem("mod_step")
        x_loaded = [sem(f"x_loaded{i}") for i in range(3)]
        ssq_ready = sem("ssq_ready")
        power_set = sem("power_set")
        eps_added = sem("eps_added")
        rstd_ready = sem("rstd_ready")
        xhat_ready = sem("xhat_ready")
        xt_ready = sem("xt_ready")
        ht_ready = sem("ht_ready")
        hi_ready = sem("hi_ready")
        lo_ready = sem("lo_ready")
        w_loaded = [sem(f"w_loaded{i}") for i in range(2)]
        w_hi_ready = sem("w_hi_ready")
        w_lo_ready = sem("w_lo_ready")
        tile_ready = sem("tile_ready")
        bank_free = sem("bank_free")
        raw_ready = sem("raw_ready")
        tap_first = sem("tap_first")
        tap_both = sem("tap_both")
        silu_done = sem("silu_done")
        stored = [sem(f"stored{i}") for i in range(4)]

        block = ctx.enter_context(nc.Block())

        @block.sync
        def _(sp):
            for dst, src in ((cvec[:, :, :], d["cvec"]), (bmod[:, :], d["bmod"]), (pgain[:, :], d["pgain"]),
                             (gbias[:, :], d["gbias"]), (coef[:, :, :], d["coef"]), (ident[:, :], d["ident"])):
                sp.dma_start(dst, src).then_inc(small_loaded, 16)
            for c in range(N_MOD):
                if c >= 3:
                    sp.wait_ge(mod_used, c - 2)
                sp.dma_start(stage[:, c % 3, :, :], d["w_mod"][c]).then_inc(mod_loaded[c % 3], 16)
            for j, src in enumerate((d["ctx"][0:P, :], d["ctx"][P:2 * P, :], d["x"][0:P, :])):
                sp.wait_ge(mod_used, N_MOD - 2 + j)
                sp.dma_start(xrow[(j + N_MOD) % 3], src).then_inc(x_loaded[j], 16)
            with sp.Fori(1, NT // 3) as i:
                for j in range(3):
                    sp.wait_ge(xt_ready, 3 * i + (j - 2))
                    sp.dma_start(xrow[(j + N_MOD) % 3],
                                 d["x"][bass.ts(3 * i + (j - NT_CTX), P), :]).then_inc(x_loaded[j], 16)

            sp.wait_ge(xt_ready, NT)
            sp.dma_start(stage[:, 0, :, 0:P], d["w_gate"]).then_inc(w_loaded[0], 16)
            sp.dma_start(stage[:, 1, :, :], d["w_in"][0]).then_inc(w_loaded[1], 16)

            def load_after(item, par):
                sp.wait_ge(w_hi_ready, item + 1)
                sp.wait_ge(w_lo_ready, item + 1)
                sp.dma_start(stage[:, par, :, :], d["w_in"][item + 1]).then_inc(w_loaded[par], 16)

            def store(ready, count, dst, slot, width):
                sp.wait_ge(ready, count)
                sp.dma_start(dst, res[slot][:, 0:width]).then_inc(stored[slot], 16)

            load_after(0, 0)
            for n, (t0, width) in enumerate([CTX_T] + LAT_T):
                store(bank_free, n + 1, s["gates"][:, t0:t0 + width], n % 4, width)
            n = 0
            for half in range(2):
                load_after(1 + half, (1 + half) % 2)
                for b in range(2):
                    for t0, width in [CTX_T] + LAT_T:
                        store(silu_done, n + 1, s["k"][2 * half + b, :, t0:t0 + width], (K0 + n) % 4, width)
                        n += 1
            n = V0
            for half in range(2):
                load_after(3 + half, (3 + half) % 2)
                for t in range(NT):
                    store(bank_free, n + 1, s["v"][t, :, half * SLOT:(half + 1) * SLOT], n % 4, SLOT)
                    n += 1
            for half in range(2):
                load_after(5 + half, (5 + half) % 2)
                for m in range(8):
                    b, j = divmod(m, 4)
                    m += 8 * half
                    store(silu_done, K_TILES + m + 1, s["qhy"][2 * half + b, :, j * TILE:(j + 1) * TILE],
                          (Q0 + m) % 4, TILE)
            with sp.Fori(0, 3) as g:
                for half in range(2):
                    load_after(2 * g + (7 + half), (7 + half) % 2)
                    for m in range(8):
                        b, j = divmod(m, 4)
                        m += 8 * half
                        store(tap_both, B_TILES * g + (K_TILES + B_TILES + m + 1),
                              s["qhy"][4 * g + (4 + 2 * half + b), :, j * TILE:(j + 1) * TILE],
                              (Q0 + m) % 4, TILE)
            with sp.Fori(0, 2) as g:
                for half in range(2):
                    load_after(2 * g + (13 + half), (13 + half) % 2)
                    for t in range(NT_LAT):
                        m = half * NT_LAT + t
                        store(bank_free, A_TILES * g + (O0 + m + 1),
                              s["ozh"][g, t, :, half * SLOT:(half + 1) * SLOT], (O0 + m) % 4, SLOT)
            for m in range(B_TILES):
                store(bank_free, Z0 + m + 1, s["zh"][m // 4, :, m % 4 * TILE:(m % 4 + 1) * TILE],
                      (Z0 + m) % 4, TILE)
            for slot in range(4):
                sp.wait_ge(stored[slot], 16 * len(range(slot, N_TILES, 4)))

        @block.tensor
        def _(pe):
            pe.wait_ge(svec_ready, 1)
            for c in range(N_MOD):
                pe.wait_ge(mod_loaded[c % 3], 16 * (c // 3 + 1))
                for b in range(2):
                    for k in range(KD):
                        mm = pe.matmul(psM[:, 2 * c + b, :], stage[:, c % 3, k, b * P:(b + 1) * P],
                                       svec[:, k, :], start=(k == 0), stop=(k == KD - 1))
                mm.then_inc(mod_used, 1)
            pe.wait_ge(small_loaded, 16 * 6)

            def turn(tile, j, first):
                pe.wait_ge(xhat_ready, tile + 1)
                if not first:
                    pe.wait_ge(ht_ready, tile - 2)
                for k in range(KD):
                    mm = pe.transpose(bank[2 * j + k // 4][:, (k % 4) * P:(k % 4 + 1) * P],
                                      xrow[(j + N_MOD) % 3][:, k * P:(k + 1) * P], ident[:, :])
                mm.then_inc(xt_ready, 1)

            for j in range(3):
                turn(j, j, True)
            with pe.Fori(1, NT // 3) as i:
                for j in range(3):
                    turn(3 * i + j, j, False)

            def three_passes(out, lhs, rhs, k):
                pe.matmul(out, lhs[0], rhs[0], start=(k == 0), stop=False)
                pe.matmul(out, lhs[0], rhs[1], start=False, stop=False)
                return pe.matmul(out, lhs[1], rhs[0], start=False, stop=(k == KD - 1))

            def channels_tile(slot, par, c0, t0, width):
                for k in range(KD):
                    mm = three_passes(bank[slot][:, 0:width],
                                      [w[:, par, k, c0:c0 + P] for w in (w_hi, w_lo)],
                                      [h[:, k, t0:t0 + width] for h in (h_hi, h_lo)], k)
                mm.then_inc(tile_ready, 1)

            def tokens_tile(slot, par, tokens):
                for k in range(KD):
                    mm = three_passes(bank[slot][:, 0:SLOT], [h[:, k, tokens] for h in (h_hi, h_lo)],
                                      [w[:, par, k, :] for w in (w_hi, w_lo)], k)
                mm.then_inc(tile_ready, 1)

            def weights(item):
                pe.wait_ge(w_hi_ready, item + 1)
                pe.wait_ge(w_lo_ready, item + 1)

            pe.wait_ge(hi_ready, NT)
            pe.wait_ge(lo_ready, NT)
            weights(0)
            n = 0
            for t0, width in [CTX_T] + LAT_T:
                if n >= 4:
                    pe.wait_ge(bank_free, n - 3)
                channels_tile(n % 4, 0, 0, t0, width)
                n += 1
            for half in range(2):
                weights(1 + half)
                for b in range(2):
                    for t0, width in [CTX_T] + LAT_T:
                        pe.wait_ge(bank_free, n - 3)
                        channels_tile(n % 4, (1 + half) % 2, b * P, t0, width)
                        n += 1
            for half in range(2):
                weights(3 + half)
                for t in range(NT):
                    pe.wait_ge(bank_free, n - 3)
                    tokens_tile(n % 4, (3 + half) % 2, slice(t * P, (t + 1) * P))
                    n += 1
            with pe.Fori(0, 4) as g:
                for half in range(2):
                    weights(2 * g + (5 + half))
                    for m in range(8):
                        b, j = divmod(m, 4)
                        m += 8 * half
                        pe.wait_ge(bank_free, B_TILES * g + (Q0 + m - 3))
                        channels_tile((Q0 + m) % 4, (5 + half) % 2, b * P, *LAT_T[j])
            with pe.Fori(0, 2) as g:
                for half in range(2):
                    weights(2 * g + (13 + half))
                    for t in range(NT_LAT):
                        m = half * NT_LAT + t
                        pe.wait_ge(bank_free, A_TILES * g + (O0 + m - 3))
                        tokens_tile((O0 + m) % 4, (13 + half) % 2,
                                    slice(T_CTX + t * P, T_CTX + (t + 1) * P))
            for half in range(2):
                weights(17 + half)
                for m in range(8):
                    b, j = divmod(m, 4)
                    m += 8 * half
                    pe.wait_ge(bank_free, Z0 + m - 3)
                    channels_tile((Z0 + m) % 4, (17 + half) % 2, b * P, *LAT_T[j])

        @block.scalar
        def _(act):
            act.wait_ge(small_loaded, 16 * 6)
            act.activation(svec[:, :, :], cvec[:, :, :], ACT.Silu).then_inc(svec_ready, 1)

            def square(tile, j, turn):
                act.wait_ge(x_loaded[j], 16 * (turn + 1))
                if not (isinstance(turn, int) and turn == 0):
                    act.wait_ge(lo_ready, tile - 2)
                act.activation(work[:, j * D:(j + 1) * D], xrow[(j + N_MOD) % 3], ACT.Square,
                               accum_out=sumsq[:, j:j + 1]).then_inc(ssq_ready, 1)

            def high(tile, j):
                act.wait_ge(ht_ready, tile + 1)
                act.copy(h_hi[:, :, bass.ts(tile, P)], ht[j]).then_inc(hi_ready, 1)

            for j in range(3):
                square(j, j, 0)
            for j in range(3):
                high(j, j)
            with act.Fori(1, NT // 3) as i:
                for j in range(3):
                    square(3 * i + j, j, i)
                for j in range(3):
                    high(3 * i + j, j)

            def split(item, par, loads, done_tiles, width=SLOT):
                act.wait_ge(w_loaded[par], 16 * loads)
                if done_tiles is not None:
                    act.wait_ge(tile_ready, done_tiles)
                act.copy(w_hi[:, par, :, 0:width], stage[:, par, :, 0:width]).then_inc(w_hi_ready, 1)

            def begin(n, slot, turn):
                act.wait_ge(tile_ready, n + 1)
                if not (isinstance(turn, int) and turn == 0):
                    act.wait_ge(stored[slot], 16 * turn)

            def plain(n, slot, turn, width, func, bias=0.0):
                begin(n, slot, turn)
                act.activation(res[slot][:, 0:width], bank[slot][:, 0:width], func, bias=bias)\
                   .then_inc(bank_free, 1)

            def conv_tile(n, slot, turn, c, r, width, blk, silu):
                begin(n, slot, turn)
                if not (isinstance(c, int) and c < 2):
                    act.wait_ge(tap_both, c - 1)
                act.copy(raw[r][:, 0:width], bank[slot][:, 0:width]).then_inc(raw_ready, 1)
                w_mid, bias = [coef[:, bass.ds(blk, 1), k:k + 1].rearrange("p a b -> p (a b)") for k in (1, 3)]
                act.activation(res[slot][:, 0:width], bank[slot][:, 0:width], ACT.Identity,
                               bias=bias, scale=w_mid).then_inc(bank_free, 1)
                if silu:
                    act.wait_ge(tap_both, c + 1)
                    act.activation(res[slot][:, 0:width], res[slot][:, 0:width], ACT.Silu)\
                       .then_inc(silu_done, 1)

            split(0, 0, 1, None, P)
            act.wait_ge(lo_ready, NT)
            split(1, 1, 1, None)
            for n, (t0, width) in enumerate([CTX_T] + LAT_T):
                plain(n, n % 4, n // 4, width, ACT.Identity, gbias[:, 0:1])
            n, c = K0, 0
            for half in range(2):
                split(2 + half, half, 2, K0 + half * K_TILES // 2)
                for b in range(2):
                    for t0, width in [CTX_T] + LAT_T:
                        conv_tile(n, n % 4, n // 4, c, c % 2, width, 2 * half + b, True)
                        n, c = n + 1, c + 1
            for half in range(2):
                split(4 + half, half, 3, V0 + half * V_TILES // 2)
                for t in range(NT):
                    plain(n, n % 4, n // 4, SLOT, ACT.Copy)
                    n += 1
            for half in range(2):
                split(6 + half, half, 4, Q0 + half * B_TILES // 2)
                for m in range(8 * half, 8 * half + 8):
                    conv_tile(n, n % 4, n // 4, K_TILES + m, m % 2, TILE, 4 + 2 * half + m // 4 % 2, True)
                    n += 1
            with act.Fori(0, 3) as g:
                for half in range(2):
                    split(None, half, g + 5, B_TILES * g + (Q0 + B_TILES + half * B_TILES // 2))
                    for m in range(8 * half, 8 * half + 8):
                        conv_tile(B_TILES * g + (n + m), (n + m) % 4, 4 * g + (n + m) // 4,
                                  B_TILES * g + (K_TILES + B_TILES + m), m % 2, TILE,
                                  4 * g + (8 + m // 4), False)
            n = O0
            for g, func in enumerate((ACT.Sigmoid, ACT.Silu, ACT.Silu)):
                for half in range(2):
                    if (g, half) != (2, 1):
                        split(None, half, g + 8, n)
                    for t in range(8 if g == 2 else NT_LAT):
                        plain(n, n % 4, n // 4, TILE if g == 2 else SLOT, func)
                        n += 1

        @block.gpsimd
        def _(pool):
            def root(tile, j, first):
                pool.wait_ge(ssq_ready, tile + 1)
                if not first:
                    pool.wait_ge(xhat_ready, tile - 2)
                pool.tensor_tensor(rstd[:, j:j + 1], sumsq[:, j:j + 1], power[:, 1:2], ALU.add)\
                    .then_inc(eps_added, 1)
                pool.wait_ge(eps_added, tile + 1)
                pool.tensor_tensor(rstd[:, j:j + 1], rstd[:, j:j + 1], power[:, 0:1], ALU.pow)\
                    .then_inc(rstd_ready, 1)

            pool.memset(power[:, 0:1], -0.5).then_inc(power_set, 1)
            pool.memset(power[:, 1:2], D * EPS).then_inc(power_set, 1)
            pool.wait_ge(power_set, 2)
            for j in range(3):
                root(j, j, True)
            with pool.Fori(1, NT // 3) as i:
                for j in range(3):
                    root(3 * i + j, j, False)

        @block.vector
        def _(dve):
            dve.wait_ge(small_loaded, 16 * 6)
            dve.wait_ge(mod_used, N_MOD)
            for col in range(2):
                ins = dve.tensor_tensor(mod[:, :, col], psM[:, :, col], bmod[:, :], ALU.add)
            ins.then_inc(mod_step, 1)
            dve.wait_ge(mod_step, 1)
            for col in range(2):
                ins = dve.scalar_tensor_tensor(gcol[:, :, col], mod[:, KD:2 * KD, col], 1.0, pgain[:, :],
                                               ALU.add, ALU.mult)
            ins.then_inc(mod_step, 1)
            dve.wait_ge(mod_step, 2)

            def normalise(tile, j):
                dve.wait_ge(ssq_ready, tile + 1)
                dve.wait_ge(rstd_ready, tile + 1)
                dve.tensor_scalar(xrow[(j + N_MOD) % 3], xrow[(j + N_MOD) % 3], rstd[:, j:j + 1], ROOT_D,
                                  ALU.mult, ALU.mult).then_inc(xhat_ready, 1)

            def modulate(tile, j, stream):
                dve.wait_ge(xt_ready, tile + 1)
                for k in range(KD):
                    ins = dve.tensor_scalar(ht[j][:, k, :], bank[2 * j + k // 4][:, (k % 4) * P:(k % 4 + 1) * P],
                                            gcol[:, k, stream:stream + 1], mod[:, k, stream:stream + 1],
                                            ALU.mult, ALU.add)
                ins.then_inc(ht_ready, 1)

            def low(tile, j):
                dve.wait_ge(hi_ready, tile + 1)
                dve.wait_ge(ht_ready, tile + 1)
                dve.tensor_tensor(h_lo[:, :, bass.ts(tile, P)], ht[j],
                                  h_hi[:, :, bass.ts(tile, P)].bitcast(F32), ALU.subtract).then_inc(lo_ready, 1)

            for j in range(3):
                normalise(j, j)
            for j in range(3):
                modulate(j, j, 1 if j < NT_CTX else 0)
            for j in range(3):
                low(j, j)
            with dve.Fori(1, NT // 3) as i:
                for j in range(3):
                    normalise(3 * i + j, j)
                for j in range(3):
                    modulate(3 * i + j, j, 0)
                for j in range(3):
                    low(3 * i + j, j)

            def split(item, par, done_tiles, width=SLOT):
                dve.wait_ge(w_hi_ready, item + 1)
                if done_tiles is not None:
                    dve.wait_ge(tile_ready, done_tiles)
                dve.tensor_tensor(w_lo[:, par, :, 0:width], stage[:, par, :, 0:width],
                                  w_hi[:, par, :, 0:width].bitcast(F32), ALU.subtract).then_inc(w_lo_ready, 1)

            def taps(n, slot, c, r, width, blk, rows):
                dve.wait_ge(raw_ready, c + 1)
                dve.wait_ge(bank_free, n + 1)
                u = raw[r][:, 0:width].rearrange("p (a b) -> p a b", a=rows)
                y = res[slot][:, 0:width].rearrange("p (a b) -> p a b", a=rows)
                e = width // rows
                w_left, w_right = [coef[:, bass.ds(blk, 1), k:k + 1].rearrange("p a b -> p (a b)") for k in (0, 2)]
                dve.scalar_tensor_tensor(y[:, :, 1:e], u[:, :, 0:e - 1], w_left, y[:, :, 1:e],
                                         ALU.mult, ALU.add).then_inc(tap_first, 1)
                dve.wait_ge(tap_first, c + 1)
                dve.scalar_tensor_tensor(y[:, :, 0:e - 1], u[:, :, 1:e], w_right, y[:, :, 0:e - 1],
                                         ALU.mult, ALU.add).then_inc(tap_both, 1)

            split(0, 0, None, P)
            split(1, 1, None)
            n, c = K0, 0
            for half in range(2):
                split(2 + half, half, K0 + half * K_TILES // 2)
                for b in range(2):
                    for t0, width in [CTX_T] + LAT_T:
                        taps(n, n % 4, c, c % 2, width, 2 * half + b, 1 if width == T_CTX else TILE // ROW)
                        n, c = n + 1, c + 1
            for half in range(2):
                split(4 + half, half, V0 + half * V_TILES // 2)
            with dve.Fori(0, 4) as g:
                for half in range(2):
                    split(2 * g + (6 + half), half, B_TILES * g + (Q0 + half * B_TILES // 2))
                    for m in range(8 * half, 8 * half + 8):
                        taps(B_TILES * g + (Q0 + m), (Q0 + m) % 4, B_TILES * g + (K_TILES + m), m % 2, TILE,
                             4 * g + (4 + m // 4), TILE // ROW)
            for i in range(5):
                split(14 + i, i % 2, O0 + i * A_TILES // 2)


HC = HEADS * NT
CTX_STEPS = 2 * NT_CTX
V1 = DH + 1


def mlstm(nc, d, s):
    with ExitStack() as ctx:
        sb, ps = mem_makers(nc, ctx)
        sem = sem_maker(nc, ctx)

        ipre = sb("ipre", [HC, 2, P])
        fpre = sb("fpre", [HC, 2, P])
        logf = sb("logf", [HC, 2, P])
        ones = sb("ones", [HC, P])
        bsum = sb("bsum", [HC, 2, P])
        arow = sb("arow", [HC, 2, P])
        mrow = sb("mrow", [HC, 2, P])
        wsrow = sb("wsrow", [HC, 2, P])
        wirow = sb("wirow", [HC, 2, P])
        emrow = sb("emrow", [HC, 2, P])
        mprev = sb("mprev", [HC, 2])
        mlast = sb("mlast", [HC, 2])
        nmlast = sb("nmlast", [HC, 2])
        wcol = sb("wcol", [HC, 2])
        logroot = sb("logroot", [HC, 1])
        chain = sb("chain", [HEADS, 2, 2, NT])
        carry = sb("carry", [HEADS, 2, NT])
        mp = sb("mp", [HEADS, 2, NT])
        ident = sb("ident_m", [P, P])
        mask = sb("mask", [P, 2, P])
        gain = sb("gain", [P, CH])
        cols = sb("cols", [P, 2, 3, HC])
        wc = sb("wc", [P, 2, HC])

        qT = sb("qT", [P, 4, HEADS, P])
        kT = sb("kT", [P, 4, HEADS, P])
        v1 = sb("v1", [P, 4, HEADS, V1])
        mb = sb("mb", [P, 4, HEADS, P])
        wib = sb("wib", [P, 4, HEADS, P])
        E = sb("E", [P, 2, HEADS, P])
        pm = sb("pm", [P, 2, HEADS, P])
        kw = sb("kw", [P, 2, HEADS, P])
        C = sb("C", [P, 2, HEADS, V1])
        den = sb("den", [P, 2, HEADS])
        h = sb("h", [P, 4, HEADS, P])
        other = sb("other", [P, 2, HEADS, P])
        og = sb("og", [P, 2, HEADS, P])
        zg = sb("zg", [P, 2, HEADS, P])
        sq = sb("sq", [P, 2, HEADS, P])
        ssq = sb("ssq", [P, 2, HEADS])
        rinv = sb("rinv", [P, 2, HEADS])
        power = sb("power_m", [P, 2, HEADS])
        yT = sb("yT", [P, 2, HEADS, P])

        psK = ps("psK", [P, HEADS, P])
        psY = ps("psY", [P, HEADS, P])
        psS = [ps(f"psS{i}", [P, HEADS, P]) for i in range(2)]
        psN = ps("psN", [P, 2, 512])[:, :, 0:2 * V1].rearrange("p a (b v) -> p a b v", b=2)
        psU = ps("psU", [P, 2, 512])[:, :, 0:2 * V1].rearrange("p a (b v) -> p a b v", b=2)

        rows_in = sem("rows_in")
        act_row = sem("act_row")
        dve_row = sem("dve_row")
        ends_out = sem("ends_out")
        ends_in = sem("ends_in")
        mprev_out = sem("mprev_out")
        mprev_in = sem("mprev_in")
        rows_out = sem("rows_out")
        wc_in = sem("wc_in")
        turned = sem("turned")
        cols_ready = sem("cols_ready")
        const_in = sem("const_in")
        const_set = sem("const_set")
        step_in = [sem(f"step_in{i}") for i in range(4)]
        masked = sem("masked")
        q_scaled = sem("q_scaled")
        e_ready = sem("e_ready")
        k_turned = sem("k_turned")
        kw_ready = sem("kw_ready")
        s_ready = sem("s_ready")
        p_ready = sem("p_ready")
        num_ready = sem("num_ready")
        den_neg = sem("den_neg")
        den_max = sem("den_max")
        den_inv = sem("den_inv")
        h_ready = sem("h_ready")
        u_ready = sem("u_ready")
        c_ready = sem("c_ready")
        h_out = [sem(f"h_out{i}") for i in range(4)]
        fin_in = [sem(f"fin_in{i}") for i in range(2)]
        summed = sem("summed")
        gated = sem("gated")
        zgain = sem("zgain")
        gain_ready = sem("gain_ready")
        ssq_ready = sem("ssq_ready_m")
        guard_added = sem("guard_added")
        rinv_ready = sem("rinv_ready")
        y_ready = sem("y_ready")
        y_turned = sem("y_turned")
        yT_ready = sem("yT_ready")
        y_out = [sem(f"y_out{i}") for i in range(2)]

        CTX = [(0, 0), (1, 1), (0, 1), (1, 0)]
        LOOP = 4
        HALF = NT_LAT // 4

        def chunk_of(it, j):
            i = 2 * it + j // 2
            return i if j % 2 == 0 else i * -1 + (NT_LAT - 1)

        block = ctx.enter_context(nc.Block())

        @block.sync
        def _(sp):
            for dr in range(2):
                for dst, kind in ((ipre, 0), (fpre, 1)):
                    r0 = 32 * (2 * dr + kind)
                    sp.dma_start(dst[:, dr, :], s["gates"][r0:r0 + HEADS, :].rearrange("h (c t) -> (h c) t", t=P))\
                      .then_inc(rows_in, 16)
            sp.dma_start(ident[:, :], d["ident"]).then_inc(const_in, 16)
            sp.dma_start(mask[:, :, :], d["mask"]).then_inc(const_in, 16)
            sp.dma_start(gain[:, :], spread(d["mh_gain"][0])).then_inc(const_in, 16)

            def load_kv(slot, dr, c):
                sp.dma_start(kT[:, slot, :, :], s["k"][:, :, bass.ts(c, P)].rearrange("h p t -> p h t"))\
                  .then_inc(step_in[slot], 16)
                sp.dma_start(v1[:, slot, :, 0:DH], s["v"][c].rearrange("p (h v) -> p h v", h=HEADS))\
                  .then_inc(step_in[slot], 16)

            sp.wait_ge(const_set, 1)
            for j, (dr, c) in enumerate(CTX):
                load_kv(j, dr, c)

            sp.wait_ge(dve_row, 6)
            for dr in range(2):
                end = P - 1 if dr == 0 else 0
                sp.dma_start(s["small"][dr, 0], bsum[:, dr, end:end + 1]).then_inc(ends_out, 16)
                sp.dma_start(s["small"][dr, 1], mrow[:, dr, end:end + 1]).then_inc(ends_out, 16)
            sp.wait_ge(ends_out, 64)
            for dr in range(2):
                sp.dma_start(chain[:, dr, :, :], s["small"][dr, 0:2].rearrange("w (h c) -> h w c", h=HEADS))\
                  .then_inc(ends_in, 16)
            sp.wait_ge(dve_row, 10)
            for dr in range(2):
                sp.dma_start(s["small"][dr, 2].rearrange("(h c) -> h c", h=HEADS), mp[:, dr, :])\
                  .then_inc(mprev_out, 16)
            sp.wait_ge(mprev_out, 32)
            for dr in range(2):
                sp.dma_start(mprev[:, dr:dr + 1], s["small"][dr, 2]).then_inc(mprev_in, 16)
            sp.wait_ge(dve_row, 13)
            sp.wait_ge(act_row, 6)
            for dr in range(2):
                sp.dma_start(s["rows"][dr, 0], mrow[:, dr, :]).then_inc(rows_out, 16)
                sp.dma_start(s["rows"][dr, 1], wirow[:, dr, :]).then_inc(rows_out, 16)
                sp.dma_start(s["small"][dr, 3], wcol[:, dr:dr + 1]).then_inc(rows_out, 16)
            sp.wait_ge(rows_out, 96)
            for dr in range(2):
                sp.dma_start(wc[:, dr, :], spread(s["small"][dr, 3])).then_inc(wc_in, 16)

            def load_step(it, j):
                dr, t = j % 2, chunk_of(it, j)
                sp.dma_start(qT[:, j, :, :], s["qhy"][0:HEADS, :, bass.ts(t, P)].rearrange("h p t -> p h t"))\
                  .then_inc(step_in[j], 16)
                load_kv(j, dr, t + NT_CTX)
                for dst, which in ((mb, 0), (wib, 1)):
                    src = s["rows"][dr, which].rearrange("(h c) t -> c h t", h=HEADS)
                    sp.dma_start(dst[:, j, :, :], spread(src[bass.ds(t + NT_CTX, 1)].rearrange("c h t -> (c h) t")))\
                      .then_inc(step_in[j], 16)

            for j in range(LOOP):
                sp.wait_ge(u_ready, j + 1)
                load_step(0, j)

            def ahead(it, j):
                sp.wait_ge(u_ready, LOOP * it + (CTX_STEPS + j + 1))
                load_step(it + 1, j)

            with sp.Fori(0, HALF) as it:
                for j in range(LOOP):
                    sp.wait_ge(h_ready, LOOP * it + (j + 1))
                    sp.dma_start(s["hf"][chunk_of(it, j)], h[:, j, :, :]).then_inc(h_out[j], 16)
                    ahead(it, j)
            for j in range(LOOP):
                sp.wait_ge(h_out[j], 16 * HALF)

            def load_fin(it, j):
                t = chunk_of(it, j)
                for dst, src in ((other, s["hf"][t]), (og, s["ozh"][0, t]), (zg, s["ozh"][1, t])):
                    sp.dma_start(dst[:, j % 2, :, :].rearrange("p h v -> p (h v)"), src)\
                      .then_inc(fin_in[j % 2], 16)

            def finish(it, j, count, last=False):
                if not last:
                    ahead(it, j)
                sp.wait_ge(yT_ready, count + 1)
                sp.dma_start(s["y"][0:HEADS, :, bass.ts(chunk_of(it, j), P)].rearrange("h p t -> p h t"),
                             yT[:, j % 2, :, :]).then_inc(y_out[j % 2], 16)

            load_fin(HALF, 0)
            load_fin(HALF, 1)
            with sp.Fori(HALF, 2 * HALF - 1) as it:
                for j in range(LOOP):
                    finish(it, j, LOOP * it + (j - LOOP * HALF))
                    load_fin(it if j < 2 else it + 1, (j + 2) % LOOP)
            it = 2 * HALF - 1
            for j in range(LOOP):
                finish(it, j, LOOP * (it - HALF) + j, True)
                if j < 2:
                    load_fin(it, j + 2)
            for j in range(2):
                sp.wait_ge(y_out[j], 16 * 2 * HALF)

        @block.gpsimd
        def _(pool):
            pool.memset(v1[:, :, :, DH:V1], 1.0).then_inc(const_set, 1)
            pool.memset(C[:, :, :, :], 0.0).then_inc(const_set, 1)
            pool.memset(power[:, 0, :], -0.5).then_inc(const_set, 1)
            pool.memset(power[:, 1, :], DH * EPS).then_inc(const_set, 1)
            pool.memset(ones[:, :], 1.0).then_inc(const_set, 1)
            pool.memset(logroot[:, :], 0.5 * math.log(DH)).then_inc(const_set, 1)
            pool.wait_ge(const_set, 6)
            pool.wait_ge(const_in, 48)

            def prepare(it, j):
                pool.wait_ge(step_in[j], 80 * it + (32 + 80))
                pool.tensor_tensor(mb[:, j, :, :], mb[:, j, :, :],
                                   mask[:, j % 2:j % 2 + 1, :].to_broadcast([P, HEADS, P]), ALU.add)\
                    .then_inc(masked, 1)
                pool.tensor_tensor(wib[:, j, :, :], wib[:, j, :, :], qT[:, j, :, :], ALU.mult)\
                    .then_inc(q_scaled, 1)

            def gate(it, j):
                b = j % 2
                pool.wait_ge(fin_in[b], 96 * it + 48 * (j // 2 + 1 - 2 * HALF))
                pool.wait_ge(h_ready, LOOP * it + (j + 1))
                pool.tensor_tensor(other[:, b, :, :], other[:, b, :, :], h[:, j, :, :], ALU.add).then_inc(summed, 1)
                pool.wait_ge(summed, LOOP * it + (j + 1 - LOOP * HALF))
                pool.tensor_tensor(og[:, b, :, :], other[:, b, :, :], og[:, b, :, :], ALU.mult).then_inc(gated, 1)
                pool.tensor_tensor(zg[:, b, :, :], zg[:, b, :, :], gain[:, :].rearrange("p (h v) -> p h v", h=HEADS),
                                   ALU.mult).then_inc(zgain, 1)

            def root(it, j):
                b, n = j % 2, LOOP * it + (j + 1 - LOOP * HALF)
                pool.wait_ge(ssq_ready, n)
                pool.tensor_tensor(rinv[:, b, :], ssq[:, b, :], power[:, 1, :], ALU.add).then_inc(guard_added, 1)
                pool.wait_ge(guard_added, n)
                pool.tensor_tensor(rinv[:, b, :], rinv[:, b, :], power[:, 0, :], ALU.pow).then_inc(rinv_ready, 1)

            with pool.Fori(0, HALF) as it:
                for j in range(LOOP):
                    prepare(it, j)
            pool.wait_ge(gain_ready, 1)
            with pool.Fori(HALF, 2 * HALF) as it:
                prepare(it, 0)
                for j in range(LOOP):
                    if j < LOOP - 1:
                        prepare(it, j + 1)
                    gate(it, j)
                    root(it, j)

        @block.tensor
        def _(pe):
            pe.wait_ge(const_in, 48)

            def turn_k(slot, step, loads, first=False):
                pe.wait_ge(step_in[slot], loads)
                if not first:
                    pe.wait_ge(kw_ready, step)
                for hd in range(HEADS):
                    mm = pe.transpose(psK[:, hd, :], kT[:, slot, hd, :], ident[:, :])
                mm.then_inc(k_turned, 1)

            def state(slot, dr, step, first=False):
                pe.wait_ge(kw_ready, step + 1)
                if not first:
                    pe.wait_ge(c_ready, step)
                for hd in range(HEADS):
                    mm = pe.matmul(psU[:, hd // 2, hd % 2, :], kw[:, dr, hd, :], v1[:, slot, hd, :],
                                   start=True, stop=True)
                mm.then_inc(u_ready, 1)

            pe.wait_ge(act_row, 6)
            for dr in range(2):
                for w, row in enumerate((arow, wsrow, emrow)):
                    mm = pe.transpose(psN[:, dr, :, :].rearrange("p a b -> p (a b)")[:, w * HC:(w + 1) * HC],
                                      row[:, dr, :], ident[0:HC, 0:HC])
                mm.then_inc(turned, 1)

            for j, (dr, c) in enumerate(CTX):
                turn_k(j, j, 32, j == 0)
                state(j, dr, j, j == 0)

            def scores(it, j):
                if j >= 2 or not isinstance(it, int):
                    pe.wait_ge(p_ready, LOOP * it + (j - 1))
                for hd in range(HEADS):
                    mm = pe.matmul(psS[j % 2][:, hd, :], kT[:, j, hd, :], qT[:, j, hd, :], start=True, stop=True)
                mm.then_inc(s_ready, 1)

            def numerators(it, j):
                n = LOOP * it + j
                pe.wait_ge(p_ready, n + 1)
                pe.wait_ge(q_scaled, n + 1)
                pe.wait_ge(c_ready, n + (CTX_STEPS - 1))
                if j or not isinstance(it, int):
                    pe.wait_ge(h_ready, n)
                for hd in range(HEADS):
                    pe.matmul(psN[:, hd // 2, hd % 2, :], pm[:, j % 2, hd, :], v1[:, j, hd, :],
                              start=True, stop=False)
                    mm = pe.matmul(psN[:, hd // 2, hd % 2, :], wib[:, j, hd, :], C[:, j % 2, hd, :],
                                   start=False, stop=True)
                mm.then_inc(num_ready, 1)

            def turn_y(it, j):
                n = LOOP * it + (j - LOOP * HALF)
                pe.wait_ge(y_ready, n + 1)
                pe.wait_ge(yT_ready, n)
                for hd in range(HEADS):
                    mm = pe.transpose(psY[:, hd, :], og[:, j % 2, hd, :], ident[:, :])
                mm.then_inc(y_turned, 1)

            def body(it, final):
                def front(j):
                    turn_k(j, LOOP * it + (CTX_STEPS + j), 80 * it + (32 + 80))
                    scores(it, j)
                front(0)
                for j in range(LOOP):
                    if j < LOOP - 1:
                        front(j + 1)
                    numerators(it, j)
                    state(j, j % 2, LOOP * it + (CTX_STEPS + j))
                    if final and j:
                        turn_y(it, j - 1)
                if final:
                    turn_y(it, LOOP - 1)

            pe.wait_ge(cols_ready, 2)
            body(0, False)
            with pe.Fori(1, HALF) as it:
                body(it, False)
            with pe.Fori(HALF, 2 * HALF) as it:
                body(it, True)

        @block.scalar
        def _(act):
            act.wait_ge(rows_in, 64)
            act.activation(logf[:, :, :], fpre[:, :, :], ACT.Abs).then_inc(act_row, 1)
            act.wait_ge(act_row, 1)
            act.activation(logf[:, :, :], logf[:, :, :], ACT.Exp, scale=-1.0).then_inc(act_row, 1)
            act.wait_ge(act_row, 2)
            act.wait_ge(const_set, 6)
            act.activation(logf[:, :, :], logf[:, :, :], ACT.Ln, bias=ones[:, 0:1]).then_inc(act_row, 1)

            act.wait_ge(dve_row, 12)
            act.wait_ge(mprev_in, 32)
            for dr in range(2):
                act.activation(wsrow[:, dr, :], arow[:, dr, :], ACT.Exp, bias=nmlast[:, dr:dr + 1])
                act.activation(wirow[:, dr, :], mrow[:, dr, :], ACT.Exp, scale=-1.0, bias=mprev[:, dr:dr + 1])
                act.activation(wcol[:, dr:dr + 1], mlast[:, dr:dr + 1], ACT.Exp, scale=-1.0,
                               bias=mprev[:, dr:dr + 1]).then_inc(act_row, 1)
            act.wait_ge(dve_row, 13)
            act.activation(emrow[:, :, :], emrow[:, :, :], ACT.Exp, scale=-1.0, bias=logroot[:, 0:1])\
               .then_inc(act_row, 1)
            for dr in range(2):
                act.wait_ge(turned, dr + 1)
                act.copy(cols[:, dr, :, :].rearrange("p w r -> p (w r)"),
                         psN[:, dr, :, :].rearrange("p a b -> p (a b)")[:, 0:3 * HC]).then_inc(cols_ready, 1)
            act.wait_ge(cols_ready, 2)

            def column(dr, which, c, hd):
                return cols[:, dr, which, bass.ds(c + hd * NT, 1)]

            def weigh_k(step, dr, c, first=False):
                act.wait_ge(k_turned, step + 1)
                if not first:
                    act.wait_ge(u_ready, step - 1)
                for hd in range(HEADS):
                    ins = act.activation(kw[:, dr, hd, :], psK[:, hd, :], ACT.Copy, scale=column(dr, 1, c, hd))
                ins.then_inc(kw_ready, 1)

            for j, (dr, c) in enumerate(CTX):
                weigh_k(j, dr, c, j < 2)

            def weights(it, j):
                n = LOOP * it + j
                act.wait_ge(masked, n + 1)
                if j >= 2 or not isinstance(it, int):
                    act.wait_ge(p_ready, n - 1)
                for hd in range(HEADS):
                    ins = act.activation(E[:, j % 2, hd, :], mb[:, j, hd, :], ACT.Exp, scale=-1.0,
                                         bias=column(j % 2, 0, chunk_of(it, j) + NT_CTX, hd))
                ins.then_inc(e_ready, 1)

            def front(it, j):
                weights(it, j)
                weigh_k(LOOP * it + (CTX_STEPS + j), j % 2, chunk_of(it, j) + NT_CTX)

            def squares(it, j):
                b = j % 2
                act.wait_ge(gated, LOOP * it + (j + 1 - LOOP * HALF))
                for hd in range(HEADS):
                    ins = act.activation(sq[:, b, hd, :], og[:, b, hd, :], ACT.Square, accum_out=ssq[:, b, hd:hd + 1])
                ins.then_inc(ssq_ready, 1)

            def copy_y(it, j):
                act.wait_ge(y_turned, LOOP * it + (j + 1 - LOOP * HALF))
                act.wait_ge(y_out[j % 2], 32 * it + 16 * (j // 2 - 2 * HALF))
                act.copy(yT[:, j % 2, :, :], psY[:, :, :]).then_inc(yT_ready, 1)

            def body(it):
                for j in range(LOOP):
                    front(it, j)

            body(0)
            with act.Fori(1, HALF) as it:
                body(it)
            with act.Fori(HALF, 2 * HALF) as it:
                front(it, 0)
                for j in range(LOOP):
                    if j < LOOP - 1:
                        front(it, j + 1)
                    squares(it, j)
                    if j:
                        copy_y(it, j - 1)
                copy_y(it, LOOP - 1)

        @block.vector
        def _(dve):
            row = lambda t, dr, back=False: t[:, dr, ::-1] if back else t[:, dr, :]
            dve.wait_ge(rows_in, 64)
            dve.wait_ge(act_row, 3)
            dve.scalar_tensor_tensor(logf[:, :, :], fpre[:, :, :], 0.0, logf[:, :, :], ALU.min, ALU.subtract)\
               .then_inc(dve_row, 1)
            dve.wait_ge(dve_row, 1)
            dve.wait_ge(const_set, 6)
            for dr in range(2):
                dve.tensor_tensor_scan(row(bsum, dr, dr), ones[:, :], row(logf, dr, dr), 0.0,
                                       ALU.mult, ALU.add).then_inc(dve_row, 1)
            dve.wait_ge(dve_row, 3)
            dve.tensor_tensor(arow[:, :, :], ipre[:, :, :], bsum[:, :, :], ALU.subtract).then_inc(dve_row, 1)
            dve.wait_ge(dve_row, 4)
            for dr in range(2):
                dve.tensor_tensor_scan(row(mrow, dr, dr), row(arow, dr, dr), row(arow, dr, dr), -3.0e38,
                                       ALU.max, ALU.max).then_inc(dve_row, 1)
            dve.wait_ge(ends_in, 32)
            dve.tensor_tensor_scan(carry[:, 0, :], chain[:, 0, 1, :], chain[:, 0, 0, :], 0.0,
                                   ALU.max, ALU.add).then_inc(dve_row, 1)
            dve.tensor_tensor_scan(carry[:, 1, 1::-1], chain[:, 1, 1, 1::-1], chain[:, 1, 0, 1::-1], 0.0,
                                   ALU.max, ALU.add).then_inc(dve_row, 1)
            dve.wait_ge(dve_row, 8)
            dve.tensor_tensor_scan(carry[:, 1, NT - 1:1:-1], chain[:, 1, 1, NT - 1:1:-1],
                                   chain[:, 1, 0, NT - 1:1:-1], carry[:, 1, 0:1],
                                   ALU.max, ALU.add).then_inc(dve_row, 1)
            dve.wait_ge(dve_row, 9)
            dve.memset(mp[:, 0, 0:1], 0.0)
            dve.memset(mp[:, 1, 1:2], 0.0)
            dve.tensor_copy(mp[:, 0, 1:NT], carry[:, 0, 0:NT - 1])
            dve.tensor_copy(mp[:, 1, 0:1], carry[:, 1, 1:2])
            dve.tensor_copy(mp[:, 1, NT - 1:NT], carry[:, 1, 0:1])
            dve.tensor_copy(mp[:, 1, 2:NT - 1], carry[:, 1, 3:NT]).then_inc(dve_row, 1)
            dve.wait_ge(mprev_in, 32)
            dve.wait_ge(dve_row, 6)
            dve.wait_ge(ends_out, 64)
            for dr in range(2):
                end = P - 1 if dr == 0 else 0
                dve.tensor_scalar(mlast[:, dr:dr + 1], mrow[:, dr, end:end + 1], mprev[:, dr:dr + 1], None, ALU.max)
                ins = dve.tensor_scalar(nmlast[:, dr:dr + 1], mrow[:, dr, end:end + 1], mprev[:, dr:dr + 1], -1.0,
                                        ALU.max, ALU.mult)
            ins.then_inc(dve_row, 1)
            dve.wait_ge(dve_row, 11)
            for dr in range(2):
                ins = dve.tensor_scalar(mrow[:, dr, :], mrow[:, dr, :], mprev[:, dr:dr + 1], None, ALU.max)
            ins.then_inc(dve_row, 1)
            dve.wait_ge(dve_row, 12)
            dve.tensor_tensor(emrow[:, :, :], bsum[:, :, :], mrow[:, :, :], ALU.add).then_inc(dve_row, 1)

            def update(step, dr, c, first=False):
                dve.wait_ge(u_ready, step + 1)
                if not first:
                    dve.wait_ge(c_ready, step - 1)
                for hd in range(HEADS):
                    ins = dve.scalar_tensor_tensor(C[:, dr, hd, :], C[:, dr, hd, :], wc[:, dr, bass.ds(c + hd * NT, 1)],
                                                   psU[:, hd // 2, hd % 2, :], ALU.mult, ALU.add)
                ins.then_inc(c_ready, 1)

            dve.wait_ge(wc_in, 32)
            for j, (dr, c) in enumerate(CTX):
                update(j, dr, c, j < 2)

            def products(it, j):
                n = LOOP * it + j
                dve.wait_ge(s_ready, n + 1)
                dve.wait_ge(e_ready, n + 1)
                if j >= 2 or not isinstance(it, int):
                    dve.wait_ge(num_ready, n - 1)
                dve.tensor_tensor(pm[:, j % 2, :, :], psS[j % 2][:, :, :], E[:, j % 2, :, :], ALU.mult)\
                   .then_inc(p_ready, 1)

            def normalise(it, j, final):
                n, b = LOOP * it + j, j % 2
                dve.wait_ge(num_ready, n + 1)
                floor = cols[:, b, 2, :].rearrange("p (h c) -> p h c", h=HEADS)[:, :, bass.ds(chunk_of(it, j) + NT_CTX, 1)]
                floor = floor.rearrange("p (a b) c -> p a b c", a=2)[:, :, :, 0]
                size = psN[:, :, :, DH]
                dn = den[:, b, :].rearrange("p (a b) -> p a b", a=2)
                dve.scalar_tensor_tensor(dn, size, -1.0, floor, ALU.mult, ALU.max).then_inc(den_neg, 1)
                dve.wait_ge(den_neg, n + 1)
                dve.tensor_tensor(dn, size, dn, ALU.max).then_inc(den_max, 1)
                dve.wait_ge(den_max, n + 1)
                dve.reciprocal(den[:, b, :], den[:, b, :]).then_inc(den_inv, 1)
                dve.wait_ge(den_inv, n + 1)
                if final:
                    dve.wait_ge(h_out[j], 16 * HALF)
                elif not isinstance(it, int):
                    dve.wait_ge(h_out[j], 16 * it)
                dve.tensor_tensor(h[:, j, :, :].rearrange("p (a b) v -> p a b v", a=2), psN[:, :, :, 0:DH],
                                  dn.unsqueeze(3).to_broadcast([P, 2, 2, DH]), ALU.mult).then_inc(h_ready, 1)

            def outputs(it, j):
                b, n = j % 2, LOOP * it + (j + 1 - LOOP * HALF)
                dve.wait_ge(rinv_ready, n)
                dve.wait_ge(zgain, n)
                for hd in range(HEADS):
                    ins = dve.scalar_tensor_tensor(og[:, b, hd, :], og[:, b, hd, :], rinv[:, b, hd:hd + 1],
                                                   zg[:, b, hd, :], ALU.mult, ALU.mult)
                ins.then_inc(y_ready, 1)

            def body(it, final):
                products(it, 0)
                for j in range(LOOP):
                    if j < LOOP - 1:
                        products(it, j + 1)
                    normalise(it, j, final)
                    update(LOOP * it + (CTX_STEPS + j), j % 2, chunk_of(it, j) + NT_CTX)
                    if final and j:
                        outputs(it, j - 1)
                if final:
                    outputs(it, LOOP - 1)

            dve.wait_ge(const_in, 48)
            dve.tensor_scalar(gain[:, :], gain[:, :], float(math.sqrt(DH)), None, ALU.mult).then_inc(gain_ready, 1)
            body(0, False)
            with dve.Fori(1, HALF) as it:
                body(it, False)
            with dve.Fori(HALF, 2 * HALF) as it:
                body(it, True)


MAGIC = 12582912.0
TWO_PI_A = 6.28125
TWO_PI_B = 2 * math.pi - TWO_PI_A
PI_DOWN = 3.1415925
GROUPS = CH // P
HID = 64
HALF_T = T_LAT // 2
S_TILES = N2 // 2
Q_TILES = NQ // 4
F_TILES = N2 // 4


def hidden_layers(nc, d, hidden):
    with ExitStack() as ctx:
        sb, ps = mem_makers(nc, ctx)
        sem = sem_maker(nc, ctx)
        feats = sb("feats", [2 * 17, HALF_T])
        w1 = sb("w1", [2 * 17, P])
        w2 = sb("w2", [P, P])
        fcol = sb("fcol", [P, 4])
        arg = sb("arg", [P, HALF_T])
        turns = sb("turns", [P, HALF_T])
        psH = [ps(f"psH{i}", [P, TILE]) for i in range(2)]

        const_in = sem("const_in_f")
        hid_sum = sem("hid_sum")
        hid_step = [sem(f"hid_step{j}") for j in range(2)]
        hid_ready = sem("hid_ready")

        block = ctx.enter_context(nc.Block())

        @block.sync
        def _(sp):
            for dst, src in ((feats[:, :], d["feats"]), (w1[:, :], d["fw1"]), (w2[:, :], d["fw2"]),
                             (fcol[:, :], d["fcol"])):
                sp.dma_start(dst, src).then_inc(const_in, 16)

        @block.tensor
        def _(pe):
            pe.wait_ge(const_in, 64)
            for layer in range(2):
                for j in range(2):
                    cut = slice(j * TILE, (j + 1) * TILE)
                    if layer:
                        pe.wait_ge(hid_ready, j + 1)
                    w, src = (w2[:, :], hidden[:, cut]) if layer else (w1[:, :], feats[:, cut])
                    pe.matmul(psH[j][:, :], w, src, start=True, stop=True).then_inc(hid_sum, 1)

        @block.scalar
        def _(act):
            for layer in range(2):
                for j in range(2):
                    cut = slice(j * TILE, (j + 1) * TILE)
                    act.wait_ge(hid_step[j], 6 * (layer + 1))
                    act.wait_ge(hid_sum, 2 * layer + j + 1)
                    act.activation(hidden[:, cut], arg[:, cut], ACT.Sin).then_inc(hid_ready, 1)

        @block.vector
        def _(dve):
            dve.wait_ge(const_in, 64)
            for layer in range(2):
                for step in range(6):
                    for j in range(2):
                        cut = slice(j * TILE, (j + 1) * TILE)
                        if step == 0:
                            if layer:
                                dve.wait_ge(hid_ready, j + 1)
                            dve.wait_ge(hid_sum, 2 * layer + j + 1)
                            ins = dve.tensor_scalar(arg[:, cut], psH[j][:, :], fcol[:, 2 * layer:2 * layer + 1],
                                                    fcol[:, 2 * layer + 1:2 * layer + 2], ALU.add, ALU.mult)
                        else:
                            dve.wait_ge(hid_step[j], 6 * layer + step)
                        if step == 1:
                            ins = dve.tensor_scalar(turns[:, cut], arg[:, cut], 1.0 / (2 * math.pi), MAGIC,
                                                    ALU.mult, ALU.add)
                        if step == 2:
                            ins = dve.tensor_scalar(turns[:, cut], turns[:, cut], -MAGIC, None, ALU.add)
                        if step == 3:
                            ins = dve.scalar_tensor_tensor(arg[:, cut], turns[:, cut], -TWO_PI_A, arg[:, cut],
                                                           ALU.mult, ALU.add)
                        if step == 4:
                            ins = dve.scalar_tensor_tensor(arg[:, cut], turns[:, cut], -TWO_PI_B, arg[:, cut],
                                                           ALU.mult, ALU.add)
                        if step == 5:
                            ins = dve.tensor_scalar(arg[:, cut], arg[:, cut], PI_DOWN, -PI_DOWN, ALU.min, ALU.max)
                        ins.then_inc(hid_step[j], 1)


PER_UNIT = {"S": 2 * S_TILES + 1, "T": F_TILES + Q_TILES + 2 * F_TILES + Q_TILES,
            "X": F_TILES + Q_TILES + F_TILES + 2 * Q_TILES, "I": Q_TILES}
START = {"S": S_TILES + 1, "T": F_TILES + Q_TILES, "X": F_TILES + 2 * Q_TILES, "I": 0}
NORM_AFTER = 2


def wait_count(engine, sem, g, per, const):
    if not isinstance(g, int):
        engine.wait_ge(sem, g * per + const)
    elif per * g + const > 0:
        engine.wait_ge(sem, per * g + const)


def places(start=None):
    return dict(start or START)


def hyena(nc, d, s):
    with ExitStack() as ctx:
        sb, ps = mem_makers(nc, ctx)
        sem = sem_maker(nc, ctx)
        hidden = sb("hidden", [P, HALF_T])
        hidden_layers(nc, d, hidden)

        tables = sb("tables", [P, 5, NQ, P])
        outer = sb("outer", [P, 2 * K1])
        back = sb("back", [K1, 2, P])
        ident = sb("ident_h", [P, P])
        ones = sb("ones_h", [P, P])
        guard = sb("guard_h", [P, 1])
        w3 = sb("w3", [P, 2, 2, P])
        fb = sb("fb", [P, 2, P])
        window = sb("window", [P, N2, P])
        f = sb("f", [P, N2, P])
        Bf = sb("Bf", [P, NQ, 8, N2])
        A2f = sb("A2f", [P, NQ, P])
        sums = sb("sums", [P, P])
        total = sb("total", [P, P])
        H = sb("H", [P, 2, NQ, P])
        xin = sb("xin", [P, T_LAT])
        x2 = sb("x2", [P, T_LAT])
        zh = sb("zh", [P, T_LAT])
        nat = sb("nat", [P, N2, P])
        x1 = sb("x1", [P, N2, P])
        B = sb("B", [P, NQ, 8, N2])
        Bi = B[:, :, :, :].rearrange("p q a n -> p (q a n)").rearrange("p (m q j) -> p m q j", q=NQ, j=4)
        A2 = sb("A2", [P, NQ, P])
        Ai = sb("Ai", [K1, 2, N2, P])
        prod = sb("prod", [P, 2, 2, 4, P])
        sqr = Bf[:, :, :, :].rearrange("p q a n -> p (q a n)")[:, 0:N2 * P].rearrange("p (n c) -> p n c", n=N2)

        psS = [ps(f"psS_h{i}", [P, 2, 8, NQ]) for i in range(2)]
        psT = [ps(f"psT{i}", [P, 4, P]) for i in range(2)]
        psX = [ps(f"psX{i}", [P, 4, P]) for i in range(2)]
        psI = [ps(f"psI{i}", [P, 4, P]) for i in range(2)]
        banks = {"S": psS, "T": psT, "X": psX, "I": psI}

        const_in = sem("const_in_h")
        const_set = sem("const_set_h")
        group_in = sem("group_in")
        x_in = sem("x_in")
        gates_in = sem("gates_in")
        summed = {r: sem(f"{r}_summed") for r in "STXI"}
        taken = {r: sem(f"{r}_taken") for r in "STXI"}
        squared = sem("squared")
        n2_summed = sem("n2_summed")
        root_ready = sem("root_ready")
        scale_ready = sem("scale_ready")
        f_scaled = sem("f_scaled")
        f_ready = sem("f_ready")
        gated = sem("gated_h")
        y_out = sem("y_out_h")

        block = ctx.enter_context(nc.Block())
        UNIT1 = {r: START[r] + PER_UNIT[r] for r in START}

        @block.sync
        def _(sp):
            def load_group(g):
                sp.dma_start(w3[:, :, :, :], d["fw3"][g]).then_inc(group_in, 16)
                sp.dma_start(window[:, :, :], d["window"][g]).then_inc(group_in, 16)
                sp.dma_start(fb[P // 2:P // 2 + 1, :, :], d["fbias"][g]).then_inc(group_in, 16)

            def load_x(block_row):
                sp.dma_start(xin[:, :], s["qhy"][block_row]).then_inc(x_in, 16)

            def load_gates(g):
                sp.dma_start(x2[:, :], s["qhy"][g + (HEADS + 2 * GROUPS)]).then_inc(gates_in, 16)
                sp.dma_start(zh[:, :], s["zh"][g]).then_inc(gates_in, 16)

            load_group(0)
            sp.dma_start(ident[:, :], d["ident"]).then_inc(const_in, 16)
            load_x(HEADS)
            for dst, src in ((outer[:, :], d["outer"].rearrange("p a k -> p (a k)")), (back[:, :, :], d["back"]),
                             (tables[:, :, :, :], d["tables"])):
                sp.dma_start(dst, src).then_inc(const_in, 16)
            sp.wait_ge(summed["T"], F_TILES)
            load_x(HEADS + GROUPS)
            load_gates(0)

            def body(g, last):
                if not last:
                    wait_count(sp, summed["T"], g, 2 * PER_UNIT["T"], START["T"] + F_TILES)
                    load_x(g + (HEADS + 1))
                    wait_count(sp, f_ready, g, 2, 2)
                    load_group(g + 1)
                    wait_count(sp, summed["T"], g, 2 * PER_UNIT["T"], UNIT1["T"] + F_TILES)
                    load_x(g + (HEADS + GROUPS + 1))
                end = UNIT1["X"] + Q_TILES + F_TILES + (0 if last else F_TILES)
                wait_count(sp, taken["X"], g, 2 * PER_UNIT["X"], end)
                sp.dma_start(s["y"][g + HEADS], x2[:, :]).then_inc(y_out, 16)
                wait_count(sp, y_out, g, 16, 16)
                if not last:
                    load_gates(g + 1)

            body(0, False)
            with sp.Fori(1, GROUPS - 1) as g:
                body(g, False)
            body(GROUPS - 1, True)

        @block.gpsimd
        def _(pool):
            pool.memset(ones[:, :], 1.0).then_inc(const_set, 1)
            pool.memset(guard[:, :], EPS).then_inc(const_set, 1)
            with pool.Fori(0, GROUPS) as g:
                pool.wait_ge(gates_in, 32 * g + 32)
                pool.tensor_tensor(x2[:, :], x2[:, :], zh[:, :], ALU.mult).then_inc(gated, 1)

        @block.tensor
        def _(pe):
            def fill(g, at, ring):
                n = at[ring]
                at[ring] += 1
                wait_count(pe, taken[ring], g, 2 * PER_UNIT[ring], n - 1)
                return banks[ring][n % 2]

            def outer_tile(g, at, src, t):
                bank = fill(g, at, "S")
                for i in range(2):
                    mm = pe.matmul(bank[:, i, :, :].rearrange("p a q -> p (a q)"), src[:, 2 * t + i, :], outer[:, :],
                                   start=True, stop=True)
                mm.then_inc(summed["S"], 1)

            def turn_x(g, at):
                for t in range(F_TILES):
                    bank = fill(g, at, "T")
                    for i in range(4):
                        mm = pe.transpose(bank[:, i, :], xin[:, 4 * t + i:T_LAT:N2], ident[:, :])
                    mm.then_inc(summed["T"], 1)

            def to_rows(g, at, src, t):
                bank = fill(g, at, "T")
                for i in range(4):
                    mm = pe.transpose(bank[:, i, :], src[:, 4 * t + i, :, :].rearrange("p a n -> p (a n)"), ident[:, :])
                mm.then_inc(summed["T"], 1)

            def in_time(g, at, o):
                for t in range(F_TILES):
                    bank = fill(g, at, "X")
                    for i in range(2):
                        mm = pe.matmul(bank[:, 2 * i:2 * i + 2, :], hidden[:, 2 * t + i:HALF_T:N2 // 2],
                                       w3[:, o, :, :].rearrange("k e c -> k (e c)"), start=True, stop=True)
                    mm.then_inc(summed["X"], 1)

            def norm(g, at, unit):
                wait_count(pe, n2_summed, g, 2, unit + 1)
                bank = fill(g, at, "S")
                pe.matmul(bank[:, :, :, :].rearrange("p b a q -> p (b a q)")[:, 0:P], ones[:, :], sums[:, :],
                          start=True, stop=True).then_inc(summed["S"], 1)

            def filter_outer(g, at, unit):
                wait_count(pe, f_ready, g, 2, unit + 1)
                for t in range(S_TILES):
                    outer_tile(g, at, f, t)

            def filter_inner(g, at):
                wait_count(pe, taken["S"], g, 2 * PER_UNIT["S"], at["S"])
                for t in range(Q_TILES + 1):
                    if t < Q_TILES:
                        to_rows(g, at, Bf, t)
                    if t:
                        wait_count(pe, taken["T"], g, 2 * PER_UNIT["T"], at["T"] - (t < Q_TILES))
                        for part in range(2):
                            bank = fill(g, at, "X")
                            for i in range(4):
                                q = 4 * (t - 1) + i
                                mm = pe.matmul(bank[:, i, :], tables[:, 1 + part, q, :], A2f[:, q, :],
                                               start=True, stop=True)
                            mm.then_inc(summed["X"], 1)

            pe.wait_ge(const_set, 2)
            pe.wait_ge(group_in, 48)
            at = {"S": 0, "T": 0, "X": 0, "I": 0}
            in_time(0, at, 0)
            pe.wait_ge(const_in, 64)
            pe.wait_ge(x_in, 16)
            turn_x(0, at)
            norm(0, at, 0)
            filter_outer(0, at, 0)
            filter_inner(0, at)

            def unit(g, at, o, more):
                for t in range(S_TILES):
                    if t % 2 == 0:
                        if o:
                            wait_count(pe, taken["X"], g, 2 * PER_UNIT["X"],
                                       UNIT1["X"] - 2 * Q_TILES - F_TILES + t // 2 + 1)
                        elif isinstance(g, int) and g == 0:
                            pe.wait_ge(taken["T"], t // 2 + 1)
                        else:
                            wait_count(pe, taken["T"], g, 2 * PER_UNIT["T"],
                                       UNIT1["T"] - 2 * PER_UNIT["T"] + t // 2 + 1)
                    outer_tile(g, at, nat, t)
                if more:
                    wait_count(pe, x_in, g, 32, 32 + 16 * o)
                    turn_x(g, at)
                wait_count(pe, taken["S"], g, 2 * PER_UNIT["S"], at["S"])
                rows_at = at["T"]
                for t in range(Q_TILES):
                    to_rows(g, at, B, t)
                if more:
                    wait_count(pe, group_in, g, 48, 48 + 48 * o)
                    in_time(g, at, 1 - o)

                def inverse(t, product_at):
                    wait_count(pe, taken["X"], g, 2 * PER_UNIT["X"], product_at + 1)
                    bank = fill(g, at, "I")
                    for i in range(4):
                        q = 4 * t + i
                        for part in range(2):
                            mm = pe.matmul(bank[:, i, :], prod[:, t % 2, part, i, :], tables[:, 3 + part, q, :],
                                           start=(part == 0), stop=(part == 1))
                    mm.then_inc(summed["I"], 1)

                for t in range(Q_TILES):
                    wait_count(pe, taken["T"], g, 2 * PER_UNIT["T"], rows_at + t + 1)
                    bank = fill(g, at, "X")
                    for i in range(4):
                        mm = pe.matmul(bank[:, i, :], tables[:, 0, 4 * t + i, :], A2[:, 4 * t + i, :],
                                       start=True, stop=True)
                    mm.then_inc(summed["X"], 1)
                    if t:
                        inverse(t - 1, at["X"] - 2)
                    if more and t == NORM_AFTER:
                        norm(g, at, o + 1)
                inverse(Q_TILES - 1, at["X"] - 1)
                if more:
                    filter_outer(g, at, o + 1)
                wait_count(pe, taken["I"], g, 2 * PER_UNIT["I"], at["I"])
                for t in range(F_TILES + 1):
                    if t < F_TILES:
                        for r in range(2):
                            bank = fill(g, at, "T")
                            for i in range(4):
                                mm = pe.transpose(bank[0:K1, i, :], Bi[:, N2 * r + 4 * t + i, :, :].rearrange("c q j -> c (q j)"),
                                                  ident[:, :])
                            mm.then_inc(summed["T"], 1)
                    if t:
                        n2 = 4 * (t - 1)
                        wait_count(pe, taken["T"], g, 2 * PER_UNIT["T"], at["T"] - 2 * (t < F_TILES))
                        bank = fill(g, at, "X")
                        if o == 0:
                            for r in range(2):
                                mm = pe.matmul(bank[:, :, :], back[:, r, :],
                                               Ai[:, r, n2:n2 + 4, :].rearrange("k n c -> k (n c)"),
                                               start=(r == 0), stop=(r == 1))
                        else:
                            for i in range(4):
                                for r in range(2):
                                    mm = pe.matmul(bank[:, i, :], Ai[:, r, n2 + i, :], back[:, r, :],
                                                   start=(r == 0), stop=(r == 1))
                        mm.then_inc(summed["X"], 1)
                if more:
                    filter_inner(g, at)

            def body(g, last):
                at = places()
                unit(g, at, 0, True)
                unit(g, at, 1, not last)

            body(0, False)
            with pe.Fori(1, GROUPS - 1) as g:
                body(g, False)
            body(GROUPS - 1, True)

        @block.scalar
        def _(act):
            def take(g, at, ring, dst, rows=P):
                n = at[ring]
                at[ring] += 1
                wait_count(act, summed[ring], g, 2 * PER_UNIT[ring], n + 1)
                act.copy(dst, banks[ring][n % 2][0:rows]).then_inc(taken[ring], 1)

            def take_outer(g, at, dst):
                for t in range(S_TILES):
                    take(g, at, "S", dst[:, :, :, 2 * t:2 * t + 2].rearrange("p q a n -> p n a q"))

            def take_tiles(g, at, ring, dst, tiles):
                for t in range(tiles):
                    take(g, at, ring, dst[:, 4 * t:4 * t + 4])

            def square(g, x_at, unit):
                wait_count(act, taken["X"], g, 2 * PER_UNIT["X"], x_at)
                act.activation(sqr, f[:, :, :], ACT.Square).then_inc(squared, 1)

            def root(g, at):
                n = at["S"]
                at["S"] += 1
                wait_count(act, summed["S"], g, 2 * PER_UNIT["S"], n + 1)
                act.activation(total[:, :], banks["S"][n % 2][:, :, :, :].rearrange("p b a q -> p (b a q)")[:, 0:P],
                               ACT.Sqrt, bias=guard[:, 0:1]).then_inc(taken["S"], 1)

            act.wait_ge(const_set, 2)
            at = {"S": 0, "T": 0, "X": 0, "I": 0}
            square(0, F_TILES, 0)
            take_tiles(0, at, "T", nat, F_TILES)
            root(0, at)
            take_outer(0, at, Bf)
            take_tiles(0, at, "T", A2f, Q_TILES)

            def unit(g, at, o, more):
                take_outer(g, at, B)
                if more:
                    take_tiles(g, at, "T", nat if o else x1, F_TILES)
                take_tiles(g, at, "T", A2, Q_TILES)
                if more:
                    square(g, (UNIT1 if o else START)["X"] + F_TILES, o + 1)
                for t in range(Q_TILES):
                    n = at["I"]
                    at["I"] += 1
                    wait_count(act, summed["I"], g, 2 * PER_UNIT["I"], n + 1)
                    act.copy(Bi[:, :, 4 * t:4 * t + 4, :],
                             psI[n % 2][:, :, :].rearrange("p q (m j) -> p m q j", j=4)).then_inc(taken["I"], 1)
                    if more and t == NORM_AFTER - 1:
                        root(g, at)
                if more:
                    take_outer(g, at, Bf)
                for t in range(F_TILES):
                    for r in range(2):
                        take(g, at, "T", Ai[:, r, 4 * t:4 * t + 4, :], K1)
                if more:
                    take_tiles(g, at, "T", A2f, Q_TILES)

            def body(g, last):
                at = places()
                unit(g, at, 0, True)
                unit(g, at, 1, not last)

            body(0, False)
            with act.Fori(1, GROUPS - 1) as g:
                body(g, False)
            body(GROUPS - 1, True)

        @block.vector
        def _(dve):
            def tile_of(g, at, ring):
                n = at[ring]
                at[ring] += 1
                wait_count(dve, summed[ring], g, 2 * PER_UNIT[ring], n + 1)
                return banks[ring][n % 2][:, :, :]

            def weigh(g, at, loads):
                wait_count(dve, group_in, g, 48, 48 * loads)
                for t in range(F_TILES):
                    dve.tensor_tensor(f[:, 4 * t:4 * t + 4, :], tile_of(g, at, "X"), window[:, 4 * t:4 * t + 4, :],
                                      ALU.mult).then_inc(taken["X"], 1)

            def sum_squares(g, unit):
                wait_count(dve, squared, g, 2, unit + 1)
                dve.tensor_reduce(sums[:, :], sqr.rearrange("p n c -> p c n"), AX.X, ALU.add).then_inc(n2_summed, 1)

            def scale(g, at, unit, o):
                wait_count(dve, taken["S"], g, 2 * PER_UNIT["S"], at["S"] + 1)
                dve.reciprocal(total[:, :], total[:, :]).then_inc(scale_ready, 1)
                wait_count(dve, scale_ready, g, 2, unit + 1)
                dve.tensor_tensor(f[:, :, :], f[:, :, :], total[:, :].unsqueeze(1).to_broadcast([P, N2, P]),
                                  ALU.mult).then_inc(f_scaled, 1)
                wait_count(dve, f_scaled, g, 2, unit + 1)
                dve.tensor_tensor(f[P // 2:P // 2 + 1, 0, :], f[P // 2:P // 2 + 1, 0, :],
                                  fb[P // 2:P // 2 + 1, o, :], ALU.add).then_inc(f_ready, 1)

            def take_spectrum(g, at):
                for t in range(Q_TILES):
                    for part in range(2):
                        dve.tensor_copy(H[:, part, 4 * t:4 * t + 4, :], tile_of(g, at, "X")).then_inc(taken["X"], 1)

            at = {"S": 0, "T": 0, "X": 0, "I": 0}
            weigh(0, at, 1)
            sum_squares(0, 0)
            scale(0, at, 0, 0)
            take_spectrum(0, at)

            def unit(g, at, o, more):
                spectrum_at = at["X"]
                if more:
                    weigh(g, at, 1 + o)
                wait_count(dve, taken["X"], g, 2 * PER_UNIT["X"], spectrum_at)
                for t in range(Q_TILES):
                    wait_count(dve, summed["I"], g, 2 * PER_UNIT["I"], Q_TILES * o + t - 1)
                    tile = tile_of(g, at, "X")
                    for part in range(2):
                        ins = dve.tensor_tensor(prod[:, t % 2, part], tile, H[:, part, 4 * t:4 * t + 4, :], ALU.mult)
                    ins.then_inc(taken["X"], 1)
                    if more and t == NORM_AFTER - 1:
                        sum_squares(g, o + 1)
                    if more and t == Q_TILES - 2:
                        scale(g, {"S": (UNIT1 if o else START)["S"] + S_TILES}, o + 1, 1 - o)
                if o:
                    wait_count(dve, gated, g, 1, 1)
                else:
                    wait_count(dve, taken["T"], g, 2 * PER_UNIT["T"], START["T"] + F_TILES)
                for t in range(F_TILES):
                    tile = tile_of(g, at, "X")
                    if o:
                        y = x2[:, :].rearrange("p (t n) -> p n t", n=N2)[:, 4 * t:4 * t + 4, :]
                        ins = dve.tensor_tensor(y, tile, y, ALU.mult)
                    else:
                        ins = dve.tensor_tensor(nat[:, 4 * t:4 * t + 4, :], tile, x1[:, 4 * t:4 * t + 4, :], ALU.mult)
                    ins.then_inc(taken["X"], 1)
                if more:
                    take_spectrum(g, at)

            def body(g, last):
                at = places()
                unit(g, at, 0, True)
                unit(g, at, 1, not last)

            body(0, False)
            with dve.Fori(1, GROUPS - 1) as g:
                body(g, False)
            body(GROUPS - 1, True)


def output(nc, d, s, svec, out):
    with ExitStack() as ctx:
        sb, ps = mem_makers(nc, ctx)
        sem = sem_maker(nc, ctx)
        w_hi = sb("wo_hi", [P, KD, D], F32R)
        w_lo = sb("wo_lo", [P, KD, D], F32R)
        y_hi = sb("y_hi", [P, 2, KD, P], F32R)
        y_lo = sb("y_lo", [P, 2, KD, P], F32R)
        stage = sb("stage_o", [P, KD, D])
        y = sb("y", [P, 2, KD, P])
        x = sb("x_o", [P, 2, D])
        z = sb("z_o", [P, 2, D])
        sfull = sb("sfull", [P, KD, P])
        gate = sb("gate", [P, D])
        bgate = sb("bgate", [P, D])
        post = sb("post", [P, D])
        sumsq = sb("sumsq_o", [P, 2, 2])
        rinv = sb("rinv_o", [P, 2])
        power = sb("power_o", [P, 2])

        acc = [[ps(f"acc{i}{c}", [P, TILE]) for c in range(2)] for i in range(2)]
        psG = [ps(f"psG{c}", [P, TILE]) for c in range(2)]

        w_in = sem("wo_in")
        row_in = sem("row_in")
        g_in = sem("g_in")
        w_split = sem("wo_split")
        s_spread = sem("s_spread")
        g_sum = sem("g_sum")
        gate_step = sem("gate_step")
        power_set = sem("power_set_o")
        y_in = [sem(f"y_in{i}") for i in range(2)]
        x_in = [sem(f"xo_in{i}") for i in range(2)]
        hi_ready = sem("yhi_ready")
        lo_ready = sem("ylo_ready")
        acc_ready = sem("acc_ready")
        squared = sem("squared_o")
        rinv_step = sem("rinv_step_o")
        gated = sem("gated_o")
        res_ready = sem("res_ready_o")
        out_done = [sem(f"out_done{i}") for i in range(2)]

        block = ctx.enter_context(nc.Block())

        @block.sync
        def _(sp):
            gate_cols = d["w_mod"][2 * D // SLOT:3 * D // SLOT].rearrange("j p k n -> p k j n")
            for k in range(KD):
                sp.dma_start(stage[:, k, :].rearrange("p (j n) -> p j n", n=SLOT), gate_cols[:, k])\
                  .then_inc(g_in, 16)
            sp.dma_start(bgate[:, :], spread(d["bgate"][0])).then_inc(row_in, 16)
            sp.dma_start(post[:, :], spread(d["post"][0])).then_inc(row_in, 16)

            def load_tile(t, b):
                sp.dma_start(y[:, b, :, :], s["y"][:, :, bass.ts(t, P)].rearrange("k p t -> p k t"))\
                  .then_inc(y_in[b], 16)
                sp.dma_start(x[:, b, :], d["x"][bass.ts(t, P), :]).then_inc(x_in[b], 16)

            load_tile(0, 0)
            load_tile(1, 1)
            sp.wait_ge(g_sum, 1)
            sp.dma_start(stage[:, :, :], d["w_out"]).then_inc(w_in, 16)

            def store(i, b, more):
                sp.wait_ge(res_ready, 2 * i + (b + 1))
                sp.dma_start(out[bass.ts(2 * i + b, P), :], z[:, b, :]).then_inc(out_done[b], 16)
                if more:
                    load_tile(2 * i + (b + 2), b)

            with sp.Fori(0, NT_LAT // 2 - 1) as i:
                for b in range(2):
                    store(i, b, True)
            for b in range(2):
                store(NT_LAT // 2 - 1, b, False)
            for b in range(2):
                sp.wait_ge(out_done[b], 16 * (NT_LAT // 2))

        @block.gpsimd
        def _(pool):
            pool.memset(power[:, 0:1], -0.5).then_inc(power_set, 1)
            pool.memset(power[:, 1:2], D * EPS).then_inc(power_set, 1)
            pool.wait_ge(power_set, 2)
            with pool.Fori(0, NT_LAT // 2) as i:
                for b in range(2):
                    n = 2 * i + (b + 1)
                    pool.wait_ge(squared, n)
                    pool.tensor_tensor(rinv[:, b:b + 1], sumsq[:, b, 0:1], sumsq[:, b, 1:2], ALU.add)\
                        .then_inc(rinv_step, 1)
                    pool.wait_ge(rinv_step, 6 * i + (3 * b + 1))
                    pool.tensor_tensor(rinv[:, b:b + 1], rinv[:, b:b + 1], power[:, 1:2], ALU.add)\
                        .then_inc(rinv_step, 1)
                    pool.wait_ge(rinv_step, 6 * i + (3 * b + 2))
                    pool.tensor_tensor(rinv[:, b:b + 1], rinv[:, b:b + 1], power[:, 0:1], ALU.pow)\
                        .then_inc(rinv_step, 1)

        @block.tensor
        def _(pe):
            pe.wait_ge(s_spread, 1)
            pe.wait_ge(g_in, 16 * KD)
            for c in range(2):
                for k in range(KD):
                    mm = pe.matmul(psG[c][:, :], sfull[:, k, :], stage[:, k, c * TILE:(c + 1) * TILE],
                                   start=(k == 0), stop=(k == KD - 1))
            mm.then_inc(g_sum, 1)
            pe.wait_ge(w_split, 2)

            def tile(i, b, first):
                pe.wait_ge(hi_ready, 2 * i + (b + 1))
                pe.wait_ge(lo_ready, 2 * i + (b + 1))
                if not first:
                    pe.wait_ge(gated, 2 * i + (b - 1))
                for c in range(2):
                    o, cut = acc[b][c][:, :], slice(c * TILE, (c + 1) * TILE)
                    for k in range(KD):
                        pe.matmul(o, y_hi[:, b, k, :], w_hi[:, k, cut], start=(k == 0), stop=False)
                        pe.matmul(o, y_hi[:, b, k, :], w_lo[:, k, cut], start=False, stop=False)
                        mm = pe.matmul(o, y_lo[:, b, k, :], w_hi[:, k, cut], start=False, stop=(k == KD - 1))
                mm.then_inc(acc_ready, 1)

            for b in range(2):
                tile(0, b, True)
            with pe.Fori(1, NT_LAT // 2) as i:
                for b in range(2):
                    tile(i, b, False)

        @block.scalar
        def _(act):
            def high(i, b, first):
                act.wait_ge(y_in[b], 16 * i + 16)
                if not first:
                    act.wait_ge(acc_ready, 2 * i + (b - 1))
                act.copy(y_hi[:, b], y[:, b]).then_inc(hi_ready, 1)

            for b in range(2):
                high(0, b, True)
            act.wait_ge(w_in, 16)
            act.copy(w_hi[:, :, :], stage[:, :, :]).then_inc(w_split, 1)

            def squares(i, b, first):
                act.wait_ge(acc_ready, 2 * i + (b + 1))
                if not first:
                    act.wait_ge(out_done[b], 16 * i)
                for c in range(2):
                    ins = act.activation(z[:, b, c * TILE:(c + 1) * TILE], acc[b][c][:, :], ACT.Square,
                                         accum_out=sumsq[:, b, c:c + 1])
                ins.then_inc(squared, 1)

            def body(i, first, last):
                for b in range(2):
                    squares(i, b, first)
                    if not last:
                        high(i + 1, b, False)

            body(0, True, False)
            with act.Fori(1, NT_LAT // 2 - 1) as i:
                body(i, False, False)
            body(NT_LAT // 2 - 1, False, True)

        @block.vector
        def _(dve):
            dve.tensor_copy(sfull[:, :, :], svec[:, :, 0:1].to_broadcast([P, KD, P])).then_inc(s_spread, 1)

            def low(i, b):
                dve.wait_ge(hi_ready, 2 * i + (b + 1))
                dve.tensor_tensor(y_lo[:, b], y[:, b], y_hi[:, b].bitcast(F32), ALU.subtract).then_inc(lo_ready, 1)

            for b in range(2):
                low(0, b)
            dve.wait_ge(row_in, 32)
            dve.wait_ge(g_sum, 1)
            for c in range(2):
                cut = slice(c * TILE, (c + 1) * TILE)
                ins = dve.tensor_tensor(gate[:, cut], psG[c][:, :], bgate[:, cut], ALU.add)
            ins.then_inc(gate_step, 1)
            dve.wait_ge(gate_step, 1)
            dve.scalar_tensor_tensor(gate[:, :], gate[:, :], ROOT_D, post[:, :], ALU.mult, ALU.mult)\
               .then_inc(gate_step, 1)
            dve.wait_ge(w_split, 1)
            dve.tensor_tensor(w_lo[:, :, :], stage[:, :, :], w_hi[:, :, :].bitcast(F32), ALU.subtract).then_inc(w_split, 1)
            dve.wait_ge(gate_step, 2)

            def finish(i, b):
                n = 2 * i + (b + 1)
                dve.wait_ge(rinv_step, 6 * i + (3 * b + 3))
                for c in range(2):
                    cut = slice(c * TILE, (c + 1) * TILE)
                    ins = dve.scalar_tensor_tensor(z[:, b, cut], acc[b][c][:, :], rinv[:, b:b + 1], gate[:, cut],
                                                   ALU.mult, ALU.mult)
                ins.then_inc(gated, 1)
                dve.wait_ge(gated, n)
                dve.wait_ge(x_in[b], 16 * i + 16)
                dve.tensor_tensor(z[:, b, :], z[:, b, :], x[:, b, :], ALU.add).then_inc(res_ready, 1)

            def body(i, last):
                for b in range(2):
                    finish(i, b)
                    if not last:
                        low(i + 1, b)

            with dve.Fori(0, NT_LAT // 2 - 1) as i:
                body(i, False)
            body(NT_LAT // 2 - 1, True)


def build(nc, d, out, stages=("project", "mlstm", "hyena", "output")):
    scratch = {
        "gates": (P, T_ALL), "k": (HEADS, P, T_ALL), "v": (NT, P, CH), "qhy": (16, P, T_LAT),
        "ozh": (2, NT_LAT, P, CH), "zh": (GROUPS, P, T_LAT), "rows": (2, 2, HEADS * NT, P), "small": (2, 4, HEADS * NT),
        "hf": (NT_LAT, P, CH), "y": (KD, P, T_LAT),
    }
    s = {k: nc.dram_tensor(f"s_{k}", v, F32).ap() for k, v in scratch.items()}
    with ExitStack() as ctx:
        svec = ctx.enter_context(nc.sbuf_tensor("svec", [P, KD, 2], F32))
        project(nc, d, s, svec)
        if "mlstm" in stages:
            mlstm(nc, d, s)
        if "hyena" in stages:
            hyena(nc, d, s)
        if "output" in stages:
            output(nc, d, s, svec, out)


def columns(v):
    return np.ascontiguousarray(v.reshape(-1, P).T)


def dft_tables():
    n1, k1 = np.arange(P), np.arange(K1)
    n2, k2 = np.arange(N2), np.arange(N2)
    ang = -2 * np.pi * np.outer(n1, k1 + 0.5) / N1
    outer = np.stack([np.cos(ang), np.sin(ang)], 1)
    fwd = np.zeros((NQ, 4, 2, N2, 4, 2, N2))
    inv = np.zeros((NQ, 4, 2, N2, 4, 2, N2))
    for q in range(NQ):
        for j in range(4):
            a = -2 * np.pi * (n2[:, None] * (NQ * j + q + 0.5) / N + n2[:, None] * k2 / N2)
            c, z = np.cos(a), np.sin(a)
            fwd[q, j, 0, :, j, 0, :], fwd[q, j, 1, :, j, 0, :] = c, -z
            fwd[q, j, 0, :, j, 1, :], fwd[q, j, 1, :, j, 1, :] = z, c
            c, z = c.T, -z.T
            inv[q, j, 0, :, j, 0, :], inv[q, j, 1, :, j, 0, :] = c, -z
            inv[q, j, 0, :, j, 1, :], inv[q, j, 1, :, j, 1, :] = z, c
    turned = np.empty_like(inv)
    turned[:, :, 0], turned[:, :, 1] = inv[:, :, 1], -inv[:, :, 0]
    fwd_re, fwd_im = np.empty_like(fwd), np.empty_like(fwd)
    fwd_re[:, :, :, :, :, 0], fwd_re[:, :, :, :, :, 1] = fwd[:, :, :, :, :, 0], fwd[:, :, :, :, :, 0]
    fwd_im[:, :, :, :, :, 0], fwd_im[:, :, :, :, :, 1] = fwd[:, :, :, :, :, 1], fwd[:, :, :, :, :, 1]
    fwd, fwd_re, fwd_im = [a.transpose(0, 2, 1, 3, 4, 5, 6).reshape(NQ, P, P) for a in (fwd, fwd_re, fwd_im)]
    inv, turned = [a.transpose(0, 1, 2, 3, 5, 6, 4).reshape(NQ, P, P) for a in (inv, turned)]
    ang = 2 * np.pi * np.outer(k1 + 0.5, n1 + N1 // 3) / N1
    back = np.stack([np.cos(ang), -np.sin(ang)], 1) * (2.0 / N)
    back = back.reshape(4, NQ, 2, P).transpose(1, 0, 2, 3).reshape(K1, 2, P)
    tables = np.stack([fwd, fwd_re, fwd_im, inv, turned], 0).transpose(2, 0, 1, 3)
    f = lambda a: np.ascontiguousarray(a.astype(np.float32))
    return f(outer), f(tables), f(back)


def filter_tables():
    f = np.float32
    pos = np.arange(T_LAT, dtype=f)
    bands = np.arange(1, 9, dtype=f)
    ang = f(2.0 * math.pi / T_LAT) * pos[:, None] * bands[None, :]
    feats = np.concatenate([(pos / f(T_LAT))[:, None], np.sin(ang), np.cos(ang)], -1).astype(f)
    lo, hi = math.log(1e-2) / 1.5, math.log(1e-2) / 0.3
    rates = np.abs(np.linspace(lo, hi, CH, dtype=f))
    offset = np.abs(pos - T_LAT // 2) / f(T_LAT / 2)
    window = np.exp(-offset[:, None] * rates).astype(f)
    window = window.reshape(P, N2, 4, P).transpose(2, 0, 1, 3)
    feats = feats.T.reshape(17, P, N2 // 2, 2).transpose(3, 0, 1, 2).reshape(2 * 17, T_LAT // 2)
    return np.ascontiguousarray(feats), np.ascontiguousarray(window)


def two_blocks(w):
    out = np.zeros((2 * w.shape[0], 2 * w.shape[1]), np.float32)
    out[:w.shape[0], :w.shape[1]] = w
    out[w.shape[0]:, w.shape[1]:] = w
    return out


def lay_out(a):
    a = {k: np.asarray(v) for k, v in a.items()}
    w = a["w_in"][0]
    cuts = np.cumsum([2 * CH, CH, CH, CH, 4 * HEADS, 3 * CH, CH])
    qk, v, o, zm, g, hy, zh = np.split(w, cuts[:-1], axis=1)
    wide = np.concatenate([qk[:, CH:], v, qk[:, :CH], hy, o, zm, zh], 1)
    w_in = wide.reshape(KD, P, N_SLOTS, SLOT).transpose(2, 1, 0, 3)
    w_gate = np.zeros((P, KD, P), np.float32)
    gbias = np.zeros((P, 1), np.float32)
    for kind in range(4):
        at = slice(32 * kind, 32 * kind + HEADS)
        w_gate[:, :, at] = g[:, kind * HEADS:(kind + 1) * HEADS].reshape(KD, P, HEADS).transpose(1, 0, 2)
        gbias[at, 0] = a["b_gates"][0, kind * HEADS:(kind + 1) * HEADS]
    wm = a["w_mod"][0].reshape(KD, P, 3 * D // SLOT, SLOT).transpose(2, 1, 0, 3)
    taps = np.concatenate([a["conv_qk_w"][0][:, CH:], a["conv_qk_w"][0][:, :CH], a["hy_conv_w"][0]], 1)
    bias = np.concatenate([a["conv_qk_b"][0][CH:], a["conv_qk_b"][0][:CH], a["hy_conv_b"][0]])
    coef = np.concatenate([taps, bias[None]], 0).reshape(4, 20, P).transpose(2, 1, 0)
    w3 = np.zeros((GROUPS, 2, HID, 2, 2, P), np.float32)
    for e in range(2):
        w3[:, e, :, :, e] = a["filt_w3"][0].reshape(HID, 2, GROUPS, P).transpose(2, 0, 1, 3)
    w3 = w3.reshape(GROUPS, P, 2, 2, P)
    outer, tables, back = dft_tables()
    feats, window = filter_tables()
    row = np.arange(P)
    before = row[:, None] <= row[None, :]
    far = np.float32(1e30)
    out = {
        "x": a["x"][0], "ctx": a["ctx"][0],
        "cvec": np.stack([columns(a["c"][0]), columns(a["c_ctx"])], 2),
        "w_mod": wm, "bmod": columns(a["b_mod"][0, :2 * D]), "bgate": a["b_mod"][0, 2 * D:][None],
        "pgain": columns(a["pre_gain"][0]), "post": a["post_gain"][0][None],
        "gbias": gbias, "w_gate": w_gate, "w_in": w_in, "coef": coef,
        "ident": np.eye(P, dtype=np.float32),
        "mask": np.stack([np.where(before, 0, far), np.where(before.T, 0, far)], 1).astype(np.float32),
        "mh_gain": a["mh_gain"][0][None],
        "outer": outer, "tables": tables, "back": back, "feats": feats, "window": window,
        "fw1": two_blocks(a["filt_w1"][0]), "fw2": two_blocks(a["filt_w2"][0]),
        "fw3": w3,
        "fcol": np.tile(np.stack([a["filt_b1"][0], a["filt_freq"][0, 0],
                                  a["filt_b2"][0], a["filt_freq"][0, 1]], 1), (2, 1)),
        "fbias": a["filt_bias"][0].reshape(2, 4, P).transpose(1, 0, 2)[:, None],
        "w_out": a["w_out"][0].reshape(KD, P, D).transpose(1, 0, 2),
    }
    return {k: np.ascontiguousarray(v) for k, v in out.items()}


def kernel(**inputs):
    from concourse import bacc
    from concourse.bass_utils import run_bass_kernel_spmd

    nc = bacc.Bacc("TRN2", target_bir_lowering=False, num_devices=1, dynamic_dma_scratch_size=1024)
    arrays = {f"in_{k}": v for k, v in lay_out(inputs).items()}
    d = {k[3:]: nc.dram_tensor(k, v.shape, mybir.dt.from_np(v.dtype), kind="ExternalInput").ap()
         for k, v in arrays.items()}
    out = nc.dram_tensor("out", (T_LAT, D), F32, kind="ExternalOutput").ap()
    build(nc, d, out)
    r = run_bass_kernel_spmd(nc, [arrays], core_ids=[0])
    return r.results[0]["out"].reshape(1, T_LAT, D)
```

```python
from contextlib import ExitStack
import math

import numpy as np
import concourse.bass as bass
from concourse import mybir
from concourse.alu_op_type import AluOpType as ALU

ACT = mybir.ActivationFunctionType
AX = mybir.AxisListType
F32 = mybir.dt.float32
F32R = mybir.dt.float32r

P = 128
D = 1024
KD = D // P
T_LAT, T_CTX = 2048, 256
T_ALL = T_CTX + T_LAT
NT_CTX, NT_LAT = T_CTX // P, T_LAT // P
NT = NT_CTX + NT_LAT
ROW = 64
HEADS = 4
DH = 128
CH = 512
EPS = 1e-6
SLOT = 256
N_SLOTS = 18
TILE = 512

N2 = 16
N1 = 192
N = N1 * N2
K1 = N1 // 2
NQ = K1 // 4


def sem_maker(nc, ctx):
    return lambda name: ctx.enter_context(nc.semaphore(name))


def mem_makers(nc, ctx):
    sb = lambda name, shape, dt=F32: ctx.enter_context(nc.sbuf_tensor(name, shape, dt))
    ps = lambda name, shape, dt=F32: ctx.enter_context(nc.psum_tensor(name, shape, dt))
    return sb, ps


def spread(src):
    return src.partition_broadcast(P)


def wait_count(engine, sem, g, per, const):
    if not isinstance(g, int):
        engine.wait_ge(sem, g * per + const)
    elif per * g + const > 0:
        engine.wait_ge(sem, per * g + const)


CTX_T = (0, T_CTX)
LAT_T = [(T_CTX + i * TILE, TILE) for i in range(T_LAT // TILE)]
GATE_TILES = 1 + len(LAT_T)
K_TILES, V_TILES, B_TILES, A_TILES = 20, 36, 16, 32
K0 = GATE_TILES
V0 = K0 + K_TILES
Q0 = V0 + V_TILES
O0 = Q0 + 4 * B_TILES
Z0 = O0 + 2 * A_TILES
N_TILES = Z0 + B_TILES
ROOT_D = float(math.sqrt(D))
N_MOD = 8


def project(nc, d, s, svec):
    with ExitStack() as ctx:
        sb, ps = mem_makers(nc, ctx)
        sem = sem_maker(nc, ctx)

        h_hi = sb("h_hi", [P, KD, T_ALL], F32R)
        h_lo = sb("h_lo", [P, KD, T_ALL], F32R)
        w_hi = sb("w_hi", [P, 2, KD, SLOT], F32R)
        w_lo = sb("w_lo", [P, 2, KD, SLOT], F32R)
        stage = sb("stage", [P, 3, KD, SLOT])
        work = sb("work", [P, 3 * D])
        ident = sb("ident", [P, P])
        cvec = sb("cvec", [P, KD, 2])
        bmod = sb("bmod", [P, 2 * KD])
        pgain = sb("pgain", [P, KD])
        mod = sb("mod", [P, 2 * KD, 2])
        gcol = sb("gcol", [P, KD, 2])
        modrow = sb("modrow", [2, 2 * D])
        gbias = sb("gbias", [P, 1])
        coef = sb("coef", [P, 20, 4])
        sumsq = sb("sumsq", [P, 3])
        rstd = sb("rstd", [P, 3])
        power = sb("power", [P, 2])
        raw = [work[:, i * TILE:(i + 1) * TILE] for i in range(2)]
        res = [work[:, (2 + i) * TILE:(3 + i) * TILE] for i in range(4)]
        ht = [work[:, i * D:(i + 1) * D].rearrange("p (k t) -> p k t", k=KD) for i in range(3)]
        xrow = [stage[:, i, :, :].rearrange("p k n -> p (k n)")[:, 0:D] for i in range(3)]

        bank = [ps(f"bank{i}", [P, TILE]) for i in range(6)]
        psM = ps("psM", [P, 2 * KD, 2])

        small_loaded = sem("small_loaded")
        mod_loaded = [sem(f"mod_loaded{i}") for i in range(3)]
        mod_used = sem("mod_used")
        svec_ready = sem("svec_ready")
        mod_rows = sem("mod_rows")
        mod_turned = sem("mod_turned")
        mod_step = sem("mod_step")
        x_loaded = [sem(f"x_loaded{i}") for i in range(3)]
        ssq_ready = sem("ssq_ready")
        power_set = sem("power_set")
        eps_added = sem("eps_added")
        rstd_ready = sem("rstd_ready")
        xhat_ready = sem("xhat_ready")
        xt_ready = sem("xt_ready")
        ht_ready = sem("ht_ready")
        hi_ready = sem("hi_ready")
        lo_ready = sem("lo_ready")
        w_loaded = [sem(f"w_loaded{i}") for i in range(2)]
        w_hi_ready = sem("w_hi_ready")
        w_lo_ready = sem("w_lo_ready")
        tile_ready = sem("tile_ready")
        bank_free = sem("bank_free")
        raw_ready = sem("raw_ready")
        tap_first = sem("tap_first")
        tap_both = sem("tap_both")
        silu_done = sem("silu_done")
        stored = [sem(f"stored{i}") for i in range(4)]

        block = ctx.enter_context(nc.Block())

        @block.sync
        def _(sp):
            for dst, src in ((cvec[:, :, :], d["cvec"]), (bmod[:, :], d["bmod"]), (pgain[:, :], d["pgain"]),
                             (gbias[:, :], d["gbias"]), (coef[:, :, :], d["coef"]), (ident[:, :], d["ident"])):
                sp.dma_start(dst, src).then_inc(small_loaded, 16)
            for c in range(N_MOD):
                if c >= 3:
                    sp.wait_ge(mod_used, c - 2)
                sp.dma_start(stage[:, c % 3, :, :], d["w_mod"][c]).then_inc(mod_loaded[c % 3], 16)
            for j, src in enumerate((d["ctx"][0:P, :], d["ctx"][P:2 * P, :], d["x"][0:P, :])):
                sp.wait_ge(mod_used, N_MOD - 2 + j)
                sp.dma_start(xrow[(j + N_MOD) % 3], src).then_inc(x_loaded[j], 16)
            with sp.Fori(1, NT // 3) as i:
                for j in range(3):
                    sp.wait_ge(xt_ready, 3 * i + (j - 2))
                    sp.dma_start(xrow[(j + N_MOD) % 3],
                                 d["x"][bass.ts(3 * i + (j - NT_CTX), P), :]).then_inc(x_loaded[j], 16)

            sp.wait_ge(xt_ready, NT)
            sp.dma_start(stage[:, 0, :, 0:P], d["w_gate"]).then_inc(w_loaded[0], 16)
            sp.dma_start(stage[:, 1, :, :], d["w_in"][0]).then_inc(w_loaded[1], 16)

            def load_after(item, par):
                sp.wait_ge(w_hi_ready, item + 1)
                sp.wait_ge(w_lo_ready, item + 1)
                sp.dma_start(stage[:, par, :, :], d["w_in"][item + 1]).then_inc(w_loaded[par], 16)

            def store(ready, count, dst, slot, width):
                sp.wait_ge(ready, count)
                sp.dma_start(dst, res[slot][:, 0:width]).then_inc(stored[slot], 16)

            load_after(0, 0)
            for n, (t0, width) in enumerate([CTX_T] + LAT_T):
                store(bank_free, n + 1, s["gates"][:, t0:t0 + width], n % 4, width)
            n = 0
            for half in range(2):
                load_after(1 + half, (1 + half) % 2)
                for b in range(2):
                    for t0, width in [CTX_T] + LAT_T:
                        store(silu_done, n + 1, s["k"][2 * half + b, :, t0:t0 + width], (K0 + n) % 4, width)
                        n += 1
            n = V0
            for half in range(2):
                load_after(3 + half, (3 + half) % 2)
                for t in range(NT):
                    store(bank_free, n + 1, s["v"][t, :, half * SLOT:(half + 1) * SLOT], n % 4, SLOT)
                    n += 1
            for half in range(2):
                load_after(5 + half, (5 + half) % 2)
                for m in range(8):
                    b, j = divmod(m, 4)
                    m += 8 * half
                    store(silu_done, K_TILES + m + 1, s["qhy"][2 * half + b, :, j * TILE:(j + 1) * TILE],
                          (Q0 + m) % 4, TILE)
            with sp.Fori(0, 3) as g:
                for half in range(2):
                    load_after(2 * g + (7 + half), (7 + half) % 2)
                    for m in range(8):
                        b, j = divmod(m, 4)
                        m += 8 * half
                        store(tap_both, B_TILES * g + (K_TILES + B_TILES + m + 1),
                              s["qhy"][4 * g + (4 + 2 * half + b), :, j * TILE:(j + 1) * TILE],
                              (Q0 + m) % 4, TILE)
            with sp.Fori(0, 2) as g:
                for half in range(2):
                    load_after(2 * g + (13 + half), (13 + half) % 2)
                    for t in range(NT_LAT):
                        m = half * NT_LAT + t
                        store(bank_free, A_TILES * g + (O0 + m + 1),
                              s["ozh"][g, t, :, half * SLOT:(half + 1) * SLOT], (O0 + m) % 4, SLOT)
            for m in range(B_TILES):
                store(bank_free, Z0 + m + 1, s["zh"][m // 4, :, m % 4 * TILE:(m % 4 + 1) * TILE],
                      (Z0 + m) % 4, TILE)
            for slot in range(4):
                sp.wait_ge(stored[slot], 16 * len(range(slot, N_TILES, 4)))

        @block.tensor
        def _(pe):
            pe.wait_ge(svec_ready, 1)
            for c in range(N_MOD):
                pe.wait_ge(mod_loaded[c % 3], 16 * (c // 3 + 1))
                for k in range(KD):
                    mm = pe.matmul(bank[c // 2][0:2, c % 2 * SLOT:(c % 2 + 1) * SLOT], svec[:, k, :],
                                   stage[:, c % 3, k, :], start=(k == 0), stop=(k == KD - 1))
                mm.then_inc(mod_used, 1)
            pe.wait_ge(small_loaded, 16 * 6)
            for m in range(2 * KD):
                if m % 4 == 0:
                    pe.wait_ge(mod_rows, m // 4 + 1)
                mm = pe.transpose(psM[:, m, :], modrow[:, m * P:(m + 1) * P], ident[0:2, 0:2])
            mm.then_inc(mod_turned, 1)

            def turn(tile, j, first):
                pe.wait_ge(xhat_ready, tile + 1)
                if not first:
                    pe.wait_ge(ht_ready, tile - 2)
                for k in range(KD):
                    mm = pe.transpose(bank[2 * j + k // 4][:, (k % 4) * P:(k % 4 + 1) * P],
                                      xrow[(j + N_MOD) % 3][:, k * P:(k + 1) * P], ident[:, :])
                mm.then_inc(xt_ready, 1)

            for j in range(3):
                turn(j, j, True)
            with pe.Fori(1, NT // 3) as i:
                for j in range(3):
                    turn(3 * i + j, j, False)

            def three_passes(out, lhs, rhs, k):
                pe.matmul(out, lhs[0], rhs[0], start=(k == 0), stop=False)
                pe.matmul(out, lhs[0], rhs[1], start=False, stop=False)
                return pe.matmul(out, lhs[1], rhs[0], start=False, stop=(k == KD - 1))

            def channels_tile(slot, par, c0, t0, width):
                for k in range(KD):
                    mm = three_passes(bank[slot][:, 0:width],
                                      [w[:, par, k, c0:c0 + P] for w in (w_hi, w_lo)],
                                      [h[:, k, t0:t0 + width] for h in (h_hi, h_lo)], k)
                mm.then_inc(tile_ready, 1)

            def tokens_tile(slot, par, tokens):
                for k in range(KD):
                    mm = three_passes(bank[slot][:, 0:SLOT], [h[:, k, tokens] for h in (h_hi, h_lo)],
                                      [w[:, par, k, :] for w in (w_hi, w_lo)], k)
                mm.then_inc(tile_ready, 1)

            def weights(item):
                pe.wait_ge(w_hi_ready, item + 1)
                pe.wait_ge(w_lo_ready, item + 1)

            pe.wait_ge(hi_ready, NT)
            pe.wait_ge(lo_ready, NT)
            weights(0)
            n = 0
            for t0, width in [CTX_T] + LAT_T:
                if n >= 4:
                    pe.wait_ge(bank_free, n - 3)
                channels_tile(n % 4, 0, 0, t0, width)
                n += 1
            for half in range(2):
                weights(1 + half)
                for b in range(2):
                    for t0, width in [CTX_T] + LAT_T:
                        pe.wait_ge(bank_free, n - 3)
                        channels_tile(n % 4, (1 + half) % 2, b * P, t0, width)
                        n += 1
            for half in range(2):
                weights(3 + half)
                for t in range(NT):
                    pe.wait_ge(bank_free, n - 3)
                    tokens_tile(n % 4, (3 + half) % 2, slice(t * P, (t + 1) * P))
                    n += 1
            with pe.Fori(0, 4) as g:
                for half in range(2):
                    weights(2 * g + (5 + half))
                    for m in range(8):
                        b, j = divmod(m, 4)
                        m += 8 * half
                        pe.wait_ge(bank_free, B_TILES * g + (Q0 + m - 3))
                        channels_tile((Q0 + m) % 4, (5 + half) % 2, b * P, *LAT_T[j])
            with pe.Fori(0, 2) as g:
                for half in range(2):
                    weights(2 * g + (13 + half))
                    for t in range(NT_LAT):
                        m = half * NT_LAT + t
                        pe.wait_ge(bank_free, A_TILES * g + (O0 + m - 3))
                        tokens_tile((O0 + m) % 4, (13 + half) % 2,
                                    slice(T_CTX + t * P, T_CTX + (t + 1) * P))
            for half in range(2):
                weights(17 + half)
                for m in range(8):
                    b, j = divmod(m, 4)
                    m += 8 * half
                    pe.wait_ge(bank_free, Z0 + m - 3)
                    channels_tile((Z0 + m) % 4, (17 + half) % 2, b * P, *LAT_T[j])

        @block.scalar
        def _(act):
            act.wait_ge(small_loaded, 16 * 6)
            act.activation(svec[:, :, :], cvec[:, :, :], ACT.Silu).then_inc(svec_ready, 1)

            def square(tile, j, turn):
                act.wait_ge(x_loaded[j], 16 * (turn + 1))
                wait_count(act, lo_ready, turn, 3, j - 2)
                act.activation(work[:, j * D:(j + 1) * D], xrow[(j + N_MOD) % 3], ACT.Square,
                               accum_out=sumsq[:, j:j + 1]).then_inc(ssq_ready, 1)

            def normalise(tile, j):
                act.wait_ge(rstd_ready, tile + 1)
                act.activation(xrow[(j + N_MOD) % 3], xrow[(j + N_MOD) % 3], ACT.Copy, scale=rstd[:, j:j + 1])\
                   .then_inc(xhat_ready, 1)

            def high(tile, j):
                act.wait_ge(ht_ready, tile + 1)
                act.copy(h_hi[:, :, bass.ts(tile, P)], ht[j]).then_inc(hi_ready, 1)

            def turns(i, last=False):
                for j in range(3):
                    if j < 2 or not last:
                        normalise(3 * i + (j + 1), (j + 1) % 3)
                    high(3 * i + j, j)
                    if j < 1 or not last:
                        square(3 * i + (j + 2), (j + 2) % 3, i + ((j + 2) // 3))

            square(0, 0, 0)
            square(1, 1, 0)
            for c in range(4):
                act.wait_ge(mod_used, 2 * c + 2)
                act.copy(modrow[:, c * TILE:(c + 1) * TILE], bank[c][0:2, :]).then_inc(mod_rows, 1)
            normalise(0, 0)
            turns(0)
            with act.Fori(1, NT // 3 - 1) as i:
                turns(i)
            turns(NT // 3 - 1, True)

            def split(item, par, loads, done_tiles, width=SLOT):
                act.wait_ge(w_loaded[par], 16 * loads)
                if done_tiles is not None:
                    act.wait_ge(tile_ready, done_tiles)
                act.copy(w_hi[:, par, :, 0:width], stage[:, par, :, 0:width]).then_inc(w_hi_ready, 1)

            def begin(n, slot, turn):
                act.wait_ge(tile_ready, n + 1)
                if not (isinstance(turn, int) and turn == 0):
                    act.wait_ge(stored[slot], 16 * turn)

            def plain(n, slot, turn, width, func, bias=0.0):
                begin(n, slot, turn)
                act.activation(res[slot][:, 0:width], bank[slot][:, 0:width], func, bias=bias)\
                   .then_inc(bank_free, 1)

            def conv_tile(n, slot, turn, c, r, width, blk, silu):
                begin(n, slot, turn)
                if not (isinstance(c, int) and c < 2):
                    act.wait_ge(tap_both, c - 1)
                act.copy(raw[r][:, 0:width], bank[slot][:, 0:width]).then_inc(raw_ready, 1)
                w_mid, bias = [coef[:, bass.ds(blk, 1), k:k + 1].rearrange("p a b -> p (a b)") for k in (1, 3)]
                act.activation(res[slot][:, 0:width], bank[slot][:, 0:width], ACT.Identity,
                               bias=bias, scale=w_mid).then_inc(bank_free, 1)
                if silu:
                    act.wait_ge(tap_both, c + 1)
                    act.activation(res[slot][:, 0:width], res[slot][:, 0:width], ACT.Silu)\
                       .then_inc(silu_done, 1)

            split(0, 0, 1, None, P)
            act.wait_ge(lo_ready, NT)
            split(1, 1, 1, None)
            for n, (t0, width) in enumerate([CTX_T] + LAT_T):
                plain(n, n % 4, n // 4, width, ACT.Identity, gbias[:, 0:1])
            n, c = K0, 0
            for half in range(2):
                split(2 + half, half, 2, K0 + half * K_TILES // 2)
                for b in range(2):
                    for t0, width in [CTX_T] + LAT_T:
                        conv_tile(n, n % 4, n // 4, c, c % 2, width, 2 * half + b, True)
                        n, c = n + 1, c + 1
            for half in range(2):
                split(4 + half, half, 3, V0 + half * V_TILES // 2)
                for t in range(NT):
                    plain(n, n % 4, n // 4, SLOT, ACT.Copy)
                    n += 1
            for half in range(2):
                split(6 + half, half, 4, Q0 + half * B_TILES // 2)
                for m in range(8 * half, 8 * half + 8):
                    conv_tile(n, n % 4, n // 4, K_TILES + m, m % 2, TILE, 4 + 2 * half + m // 4 % 2, True)
                    n += 1
            with act.Fori(0, 3) as g:
                for half in range(2):
                    split(None, half, g + 5, B_TILES * g + (Q0 + B_TILES + half * B_TILES // 2))
                    for m in range(8 * half, 8 * half + 8):
                        conv_tile(B_TILES * g + (n + m), (n + m) % 4, 4 * g + (n + m) // 4,
                                  B_TILES * g + (K_TILES + B_TILES + m), m % 2, TILE,
                                  4 * g + (8 + m // 4), False)
            n = O0
            for g, func in enumerate((ACT.Sigmoid, ACT.Silu, ACT.Silu)):
                for half in range(2):
                    if (g, half) != (2, 1):
                        split(None, half, g + 8, n)
                    for t in range(8 if g == 2 else NT_LAT):
                        plain(n, n % 4, n // 4, TILE if g == 2 else SLOT, func)
                        n += 1

        @block.gpsimd
        def _(pool):
            def root(tile, j, turn):
                pool.wait_ge(ssq_ready, tile + 1)
                wait_count(pool, xhat_ready, turn, 3, j - 2)
                pool.tensor_tensor(rstd[:, j:j + 1], sumsq[:, j:j + 1], power[:, 1:2], ALU.add)\
                    .then_inc(eps_added, 1)
                pool.wait_ge(eps_added, tile + 1)
                pool.tensor_tensor(rstd[:, j:j + 1], rstd[:, j:j + 1], power[:, 0:1], ALU.pow)\
                    .then_inc(rstd_ready, 1)

            def low(tile, j):
                pool.wait_ge(hi_ready, tile + 1)
                pool.tensor_tensor(h_lo[:, :, bass.ts(tile, P)], ht[j],
                                   h_hi[:, :, bass.ts(tile, P)].bitcast(F32), ALU.subtract).then_inc(lo_ready, 1)

            def turns(i, last=False):
                for j in range(3):
                    if j < 1 or not last:
                        root(3 * i + (j + 2), (j + 2) % 3, i + ((j + 2) // 3))
                    low(3 * i + j, j)

            pool.memset(power[:, 0:1], -0.5).then_inc(power_set, 1)
            pool.memset(power[:, 1:2], D * EPS).then_inc(power_set, 1)
            pool.wait_ge(power_set, 2)
            root(0, 0, 0)
            root(1, 1, 0)
            turns(0)
            with pool.Fori(1, NT // 3 - 1) as i:
                turns(i)
            turns(NT // 3 - 1, True)

        @block.vector
        def _(dve):
            dve.wait_ge(small_loaded, 16 * 6)
            dve.wait_ge(mod_turned, 1)
            for col in range(2):
                ins = dve.tensor_tensor(mod[:, :, col], psM[:, :, col], bmod[:, :], ALU.add)
            ins.then_inc(mod_step, 1)
            dve.wait_ge(mod_step, 1)
            for col in range(2):
                ins = dve.scalar_tensor_tensor(gcol[:, :, col], mod[:, KD:2 * KD, col], 1.0, pgain[:, :],
                                               ALU.add, ALU.mult)
            ins.then_inc(mod_step, 1)
            dve.wait_ge(mod_step, 2)
            dve.tensor_scalar(gcol[:, :, :], gcol[:, :, :], ROOT_D, None, ALU.mult).then_inc(mod_step, 1)
            dve.wait_ge(mod_step, 3)

            def modulate(tile, j, stream):
                dve.wait_ge(xt_ready, tile + 1)
                dve.wait_ge(ssq_ready, tile + 1)
                for k in range(KD):
                    ins = dve.tensor_scalar(ht[j][:, k, :], bank[2 * j + k // 4][:, (k % 4) * P:(k % 4 + 1) * P],
                                            gcol[:, k, stream:stream + 1], mod[:, k, stream:stream + 1],
                                            ALU.mult, ALU.add)
                ins.then_inc(ht_ready, 1)

            for j in range(3):
                modulate(j, j, 1 if j < NT_CTX else 0)
            with dve.Fori(1, NT // 3) as i:
                for j in range(3):
                    modulate(3 * i + j, j, 0)

            def split(item, par, done_tiles, width=SLOT):
                dve.wait_ge(w_hi_ready, item + 1)
                if done_tiles is not None:
                    dve.wait_ge(tile_ready, done_tiles)
                dve.tensor_tensor(w_lo[:, par, :, 0:width], stage[:, par, :, 0:width],
                                  w_hi[:, par, :, 0:width].bitcast(F32), ALU.subtract).then_inc(w_lo_ready, 1)

            def taps(n, slot, c, r, width, blk, rows):
                dve.wait_ge(raw_ready, c + 1)
                dve.wait_ge(bank_free, n + 1)
                u = raw[r][:, 0:width].rearrange("p (a b) -> p a b", a=rows)
                y = res[slot][:, 0:width].rearrange("p (a b) -> p a b", a=rows)
                e = width // rows
                w_left, w_right = [coef[:, bass.ds(blk, 1), k:k + 1].rearrange("p a b -> p (a b)") for k in (0, 2)]
                dve.scalar_tensor_tensor(y[:, :, 1:e], u[:, :, 0:e - 1], w_left, y[:, :, 1:e],
                                         ALU.mult, ALU.add).then_inc(tap_first, 1)
                dve.wait_ge(tap_first, c + 1)
                dve.scalar_tensor_tensor(y[:, :, 0:e - 1], u[:, :, 1:e], w_right, y[:, :, 0:e - 1],
                                         ALU.mult, ALU.add).then_inc(tap_both, 1)

            split(0, 0, None, P)
            split(1, 1, None)
            n, c = K0, 0
            for half in range(2):
                split(2 + half, half, K0 + half * K_TILES // 2)
                for b in range(2):
                    for t0, width in [CTX_T] + LAT_T:
                        taps(n, n % 4, c, c % 2, width, 2 * half + b, 1 if width == T_CTX else TILE // ROW)
                        n, c = n + 1, c + 1
            for half in range(2):
                split(4 + half, half, V0 + half * V_TILES // 2)
            with dve.Fori(0, 4) as g:
                for half in range(2):
                    split(2 * g + (6 + half), half, B_TILES * g + (Q0 + half * B_TILES // 2))
                    for m in range(8 * half, 8 * half + 8):
                        taps(B_TILES * g + (Q0 + m), (Q0 + m) % 4, B_TILES * g + (K_TILES + m), m % 2, TILE,
                             4 * g + (4 + m // 4), TILE // ROW)
            for i in range(5):
                split(14 + i, i % 2, O0 + i * A_TILES // 2)


HC = HEADS * NT
CTX_STEPS = 2 * NT_CTX
V1 = DH + 1


def mlstm(nc, d, s, svec, wo_hi, wo_lo, gate):
    with ExitStack() as ctx:
        sb, ps = mem_makers(nc, ctx)
        sem = sem_maker(nc, ctx)

        ipre = sb("ipre", [HC, 2, P])
        fpre = sb("fpre", [HC, 2, P])
        logf = sb("logf", [HC, 2, P])
        ones = sb("ones", [HC, P])
        bsum = sb("bsum", [HC, 2, P])
        arow = sb("arow", [HC, 2, P])
        mrow = sb("mrow", [HC, 2, P])
        wsrow = sb("wsrow", [HC, 2, P])
        wirow = sb("wirow", [HC, 2, P])
        emrow = sb("emrow", [HC, 2, P])
        mprev = sb("mprev", [HC, 2])
        mlast = sb("mlast", [HC, 2])
        nmlast = sb("nmlast", [HC, 2])
        wcol = sb("wcol", [HC, 2])
        logroot = sb("logroot", [HC, 1])
        chain = sb("chain", [HEADS, 2, 2, NT])
        carry = sb("carry", [HEADS, 2, NT])
        mp = sb("mp", [HEADS, 2, NT])
        ident = sb("ident_m", [P, P])
        mask = sb("mask", [P, 2, P])
        gain = sb("gain", [P, CH])
        cols = sb("cols", [P, 2, 3, HC])
        wc = sb("wc", [P, 2, HC])

        qT = sb("qT", [P, 4, HEADS, P])
        kT = sb("kT", [P, 4, HEADS, P])
        v1 = sb("v1", [P, 4, HEADS, V1])
        mb = sb("mb", [P, 4, HEADS, P])
        wib = sb("wib", [P, 4, HEADS, P])
        E = sb("E", [P, 2, HEADS, P])
        pm = sb("pm", [P, 2, HEADS, P])
        kw = sb("kw", [P, 2, HEADS, P])
        C = sb("C", [P, 2, HEADS, V1])
        den = sb("den", [P, 2, HEADS])
        h = sb("h", [P, 4, HEADS, P])
        other = sb("other", [P, 4, HEADS, P])
        og = sb("og", [P, 4, HEADS, P])
        zg = sb("zg", [P, 4, HEADS, P])
        sq = sb("sq", [P, 2, HEADS, P])
        ssq = sb("ssq", [P, 4, HEADS])
        rinv = sb("rinv", [P, 4, HEADS])
        power = sb("power_m", [P, 2, HEADS])
        yT = sb("yT", [P, 2, HEADS, P])

        stage = sb("stage_o", [P, KD, D])
        sfull = sb("sfull", [P, KD, P])
        bgate, post = [other[:, i:i + 2].rearrange("p j h v -> p (j h v)") for i in (0, 2)]

        psK = ps("psK", [P, HEADS, P])
        psY = ps("psY", [P, HEADS, P])
        psS = [ps(f"psS{i}", [P, HEADS, P]) for i in range(2)]
        psN = ps("psN", [P, 2, 512])[:, :, 0:2 * V1].rearrange("p a (b v) -> p a b v", b=2)
        psU = ps("psU", [P, 2, 512])[:, :, 0:2 * V1].rearrange("p a (b v) -> p a b v", b=2)

        gate_cols_in = sem("gate_cols_in")
        gate_rows_in = sem("gate_rows_in")
        wo_in = sem("wo_in")
        s_spread = sem("s_spread")
        gate_sum = sem("gate_sum")
        gate_step = sem("gate_step")
        wo_high = sem("wo_high")
        wo_low = sem("wo_low")
        rows_in = sem("rows_in")
        act_row = sem("act_row")
        dve_row = sem("dve_row")
        ends_out = sem("ends_out")
        ends_in = sem("ends_in")
        mprev_out = sem("mprev_out")
        mprev_in = sem("mprev_in")
        rows_out = sem("rows_out")
        wc_in = sem("wc_in")
        turned = sem("turned")
        cols_ready = sem("cols_ready")
        const_in = sem("const_in")
        const_set = sem("const_set")
        step_in = [sem(f"step_in{i}") for i in range(4)]
        masked = sem("masked")
        q_scaled = sem("q_scaled")
        e_ready = sem("e_ready")
        k_turned = sem("k_turned")
        kw_ready = sem("kw_ready")
        s_ready = sem("s_ready")
        p_ready = sem("p_ready")
        num_ready = sem("num_ready")
        den_neg = sem("den_neg")
        den_max = sem("den_max")
        den_inv = sem("den_inv")
        h_ready = sem("h_ready")
        u_ready = sem("u_ready")
        c_ready = sem("c_ready")
        h_out = [sem(f"h_out{i}") for i in range(4)]
        fin_in = [sem(f"fin_in{i}") for i in range(4)]
        gated = sem("gated")
        y_scaled = sem("y_scaled")
        gain_ready = sem("gain_ready")
        ssq_ready = sem("ssq_ready_m")
        guard_added = sem("guard_added")
        rinv_ready = sem("rinv_ready")
        y_ready = sem("y_ready")
        y_turned = sem("y_turned")
        yT_ready = sem("yT_ready")
        y_out = [sem(f"y_out{i}") for i in range(2)]

        CTX = [(0, 0), (1, 1), (0, 1), (1, 0)]
        LOOP = 4
        HALF = NT_LAT // 4

        def chunk_of(it, j):
            i = 2 * it + j // 2
            return i if j % 2 == 0 else i * -1 + (NT_LAT - 1)

        DONE = LOOP * HALF

        def first_body(it):
            return isinstance(it, int) and it == 0

        def earlier(it, j, lag):
            if isinstance(it, int):
                n = LOOP * it + j - lag
                return None if n < DONE or n >= 2 * DONE else divmod(n, LOOP)
            return (it, j - lag) if j >= lag else (it + -1, j - lag + LOOP)

        block = ctx.enter_context(nc.Block())

        @block.sync
        def _(sp):
            for dr in range(2):
                for dst, kind in ((ipre, 0), (fpre, 1)):
                    r0 = 32 * (2 * dr + kind)
                    sp.dma_start(dst[:, dr, :], s["gates"][r0:r0 + HEADS, :].rearrange("h (c t) -> (h c) t", t=P))\
                      .then_inc(rows_in, 16)
            sp.dma_start(ident[:, :], d["ident"]).then_inc(const_in, 16)
            sp.dma_start(mask[:, :, :], d["mask"]).then_inc(const_in, 16)
            sp.dma_start(gain[:, :], spread(d["mh_gain"][0])).then_inc(const_in, 16)

            def load_kv(slot, dr, c):
                sp.dma_start(kT[:, slot, :, :], s["k"][:, :, bass.ts(c, P)].rearrange("h p t -> p h t"))\
                  .then_inc(step_in[slot], 16)
                sp.dma_start(v1[:, slot, :, 0:DH], s["v"][c].rearrange("p (h v) -> p h v", h=HEADS))\
                  .then_inc(step_in[slot], 16)

            gate_cols = d["w_mod"][2 * D // SLOT:3 * D // SLOT].rearrange("j p k n -> p k j n")
            for k in range(KD):
                sp.dma_start(stage[:, k, :].rearrange("p (j n) -> p j n", n=SLOT), gate_cols[:, k])\
                  .then_inc(gate_cols_in, 16)
            sp.dma_start(bgate, spread(d["bgate"][0])).then_inc(gate_rows_in, 16)
            sp.dma_start(post, spread(d["post"][0])).then_inc(gate_rows_in, 16)
            sp.wait_ge(const_set, 1)
            for j, (dr, c) in enumerate(CTX):
                load_kv(j, dr, c)

            sp.wait_ge(dve_row, 6)
            for dr in range(2):
                end = P - 1 if dr == 0 else 0
                sp.dma_start(s["small"][dr, 0], bsum[:, dr, end:end + 1]).then_inc(ends_out, 16)
                sp.dma_start(s["small"][dr, 1], mrow[:, dr, end:end + 1]).then_inc(ends_out, 16)
            sp.wait_ge(ends_out, 64)
            for dr in range(2):
                sp.dma_start(chain[:, dr, :, :], s["small"][dr, 0:2].rearrange("w (h c) -> h w c", h=HEADS))\
                  .then_inc(ends_in, 16)
            sp.wait_ge(dve_row, 10)
            for dr in range(2):
                sp.dma_start(s["small"][dr, 2].rearrange("(h c) -> h c", h=HEADS), mp[:, dr, :])\
                  .then_inc(mprev_out, 16)
            sp.wait_ge(mprev_out, 32)
            for dr in range(2):
                sp.dma_start(mprev[:, dr:dr + 1], s["small"][dr, 2]).then_inc(mprev_in, 16)
            sp.wait_ge(dve_row, 13)
            sp.wait_ge(act_row, 6)
            for dr in range(2):
                sp.dma_start(s["rows"][dr, 0], mrow[:, dr, :]).then_inc(rows_out, 16)
                sp.dma_start(s["rows"][dr, 1], wirow[:, dr, :]).then_inc(rows_out, 16)
                sp.dma_start(s["small"][dr, 3], wcol[:, dr:dr + 1]).then_inc(rows_out, 16)
            sp.wait_ge(rows_out, 96)
            for dr in range(2):
                sp.dma_start(wc[:, dr, :], spread(s["small"][dr, 3])).then_inc(wc_in, 16)

            def load_step(it, j):
                dr, t = j % 2, chunk_of(it, j)
                sp.dma_start(qT[:, j, :, :], s["qhy"][0:HEADS, :, bass.ts(t, P)].rearrange("h p t -> p h t"))\
                  .then_inc(step_in[j], 16)
                load_kv(j, dr, t + NT_CTX)
                for dst, which in ((mb, 0), (wib, 1)):
                    src = s["rows"][dr, which].rearrange("(h c) t -> c h t", h=HEADS)
                    sp.dma_start(dst[:, j, :, :], spread(src[bass.ds(t + NT_CTX, 1)].rearrange("c h t -> (c h) t")))\
                      .then_inc(step_in[j], 16)

            for j in range(LOOP):
                sp.wait_ge(u_ready, j + 1)
                load_step(0, j)

            def ahead(it, j):
                sp.wait_ge(u_ready, LOOP * it + (CTX_STEPS + j + 1))
                load_step(it + 1, j)

            sp.wait_ge(gate_sum, 1)
            sp.dma_start(stage[:, :, :], d["w_out"]).then_inc(wo_in, 16)

            with sp.Fori(0, HALF) as it:
                for j in range(LOOP):
                    sp.wait_ge(h_ready, LOOP * it + (j + 1))
                    sp.dma_start(s["hf"][chunk_of(it, j)], h[:, j, :, :]).then_inc(h_out[j], 16)
                    ahead(it, j)
            for j in range(LOOP):
                sp.wait_ge(h_out[j], 16 * HALF)

            def load_fin(it, j):
                tile = chunk_of(it, j)
                for dst, src in ((other, s["hf"][tile]), (og, s["ozh"][0, tile]), (zg, s["ozh"][1, tile])):
                    sp.dma_start(dst[:, j, :, :].rearrange("p h v -> p (h v)"), src).then_inc(fin_in[j], 16)

            def store_y(it, j):
                wait_count(sp, yT_ready, it, LOOP, j + 1 - DONE)
                sp.dma_start(s["y"][0:HEADS, :, bass.ts(chunk_of(it, j), P)].rearrange("h p t -> p h t"),
                             yT[:, j % 2, :, :]).then_inc(y_out[j % 2], 16)

            def turn(it, j, last=False):
                if not last:
                    ahead(it, j)
                back = earlier(it, j, 2)
                if back and not (last and j >= 2):
                    wait_count(sp, y_ready, back[0], LOOP, back[1] + 1 - DONE)
                    load_fin(*((it, j + 2) if j < 2 else (it + 1, j - 2)))
                back = earlier(it, j, LOOP)
                if back:
                    store_y(*back)

            for j in range(LOOP):
                load_fin(HALF, j)
            for j in range(LOOP):
                turn(HALF, j)
            with sp.Fori(HALF + 1, 2 * HALF - 1) as it:
                for j in range(LOOP):
                    turn(it, j)
            for j in range(LOOP):
                turn(2 * HALF - 1, j, True)
            for j in range(LOOP):
                store_y(2 * HALF - 1, j)
            for j in range(2):
                sp.wait_ge(y_out[j], 16 * 2 * HALF)

        @block.gpsimd
        def _(pool):
            pool.memset(v1[:, :, :, DH:V1], 1.0).then_inc(const_set, 1)
            pool.memset(C[:, :, :, :], 0.0).then_inc(const_set, 1)
            pool.memset(power[:, 0, :], -0.5).then_inc(const_set, 1)
            pool.memset(power[:, 1, :], DH * EPS).then_inc(const_set, 1)
            pool.memset(ones[:, :], 1.0).then_inc(const_set, 1)
            pool.memset(logroot[:, :], 0.5 * math.log(DH)).then_inc(const_set, 1)
            pool.wait_ge(const_set, 6)
            pool.wait_ge(const_in, 48)

            def prepare(it, j):
                pool.wait_ge(step_in[j], 80 * it + (32 + 80))
                pool.tensor_tensor(mb[:, j, :, :], mb[:, j, :, :],
                                   mask[:, j % 2:j % 2 + 1, :].to_broadcast([P, HEADS, P]), ALU.add)\
                    .then_inc(masked, 1)
                pool.tensor_tensor(wib[:, j, :, :], wib[:, j, :, :], qT[:, j, :, :], ALU.mult)\
                    .then_inc(q_scaled, 1)

            def gate(it, j):
                wait_count(pool, fin_in[j], it, 48, 48 * (1 - HALF))
                wait_count(pool, h_ready, it, LOOP, j + 1)
                pool.tensor_tensor(og[:, j, :, :], h[:, j, :, :], og[:, j, :, :], ALU.mult).then_inc(gated, 1)

            def root(it, j):
                wait_count(pool, ssq_ready, it, LOOP, j + 1 - DONE)
                pool.tensor_tensor(rinv[:, j, :], ssq[:, j, :], power[:, 1, :], ALU.add).then_inc(guard_added, 1)
                wait_count(pool, guard_added, it, LOOP, j + 1 - DONE)
                pool.tensor_tensor(rinv[:, j, :], rinv[:, j, :], power[:, 0, :], ALU.pow).then_inc(rinv_ready, 1)

            def turn(it, j, last=False):
                if j < 2:
                    prepare(it, j + 2)
                elif not last:
                    prepare(it + 1, j - 2)
                gate(it, j)
                back = earlier(it, j, 1)
                if back:
                    root(*back)

            with pool.Fori(0, HALF) as it:
                for j in range(LOOP):
                    prepare(it, j)
            for j in range(2):
                prepare(HALF, j)
            for j in range(LOOP):
                turn(HALF, j)
            with pool.Fori(HALF + 1, 2 * HALF - 1) as it:
                for j in range(LOOP):
                    turn(it, j)
            for j in range(LOOP):
                turn(2 * HALF - 1, j, True)
            root(2 * HALF - 1, LOOP - 1)

        @block.tensor
        def _(pe):
            pe.wait_ge(const_in, 48)

            def turn_k(slot, step, loads, first=False):
                pe.wait_ge(step_in[slot], loads)
                if not first:
                    pe.wait_ge(kw_ready, step)
                for hd in range(HEADS):
                    mm = pe.transpose(psK[:, hd, :], kT[:, slot, hd, :], ident[:, :])
                mm.then_inc(k_turned, 1)

            def state(slot, dr, step, first=False):
                pe.wait_ge(kw_ready, step + 1)
                if not first:
                    pe.wait_ge(c_ready, step)
                for hd in range(HEADS):
                    mm = pe.matmul(psU[:, hd // 2, hd % 2, :], kw[:, dr, hd, :], v1[:, slot, hd, :],
                                   start=True, stop=True)
                mm.then_inc(u_ready, 1)

            pe.wait_ge(s_spread, 1)
            pe.wait_ge(gate_cols_in, 16 * KD)
            for c in range(2):
                for k in range(KD):
                    mm = pe.matmul(psS[c][:, :, :], sfull[:, k, :], stage[:, k, c * TILE:(c + 1) * TILE],
                                   start=(k == 0), stop=(k == KD - 1))
            mm.then_inc(gate_sum, 1)

            pe.wait_ge(act_row, 6)
            for dr in range(2):
                for w, row in enumerate((arow, wsrow, emrow)):
                    mm = pe.transpose(psN[:, dr, :, :].rearrange("p a b -> p (a b)")[:, w * HC:(w + 1) * HC],
                                      row[:, dr, :], ident[0:HC, 0:HC])
                mm.then_inc(turned, 1)

            for j, (dr, c) in enumerate(CTX):
                turn_k(j, j, 32, j == 0)
                state(j, dr, j, j == 0)

            def scores(it, j):
                if j >= 2 or not first_body(it):
                    pe.wait_ge(p_ready, LOOP * it + (j - 1))
                for hd in range(HEADS):
                    mm = pe.matmul(psS[j % 2][:, hd, :], kT[:, j, hd, :], qT[:, j, hd, :], start=True, stop=True)
                mm.then_inc(s_ready, 1)

            def numerators(it, j):
                n = LOOP * it + j
                pe.wait_ge(p_ready, n + 1)
                pe.wait_ge(q_scaled, n + 1)
                pe.wait_ge(c_ready, n + (CTX_STEPS - 1))
                if j or not first_body(it):
                    pe.wait_ge(h_ready, n)
                for hd in range(HEADS):
                    pe.matmul(psN[:, hd // 2, hd % 2, :], pm[:, j % 2, hd, :], v1[:, j, hd, :],
                              start=True, stop=False)
                    mm = pe.matmul(psN[:, hd // 2, hd % 2, :], wib[:, j, hd, :], C[:, j % 2, hd, :],
                                   start=False, stop=True)
                mm.then_inc(num_ready, 1)

            def turn_y(it, j):
                wait_count(pe, y_ready, it, LOOP, j + 1 - DONE)
                wait_count(pe, yT_ready, it, LOOP, j - DONE)
                for hd in range(HEADS):
                    mm = pe.transpose(psY[:, hd, :], h[:, j, hd, :], ident[:, :])
                mm.then_inc(y_turned, 1)

            def front(it, j):
                turn_k(j, LOOP * it + (CTX_STEPS + j), 80 * it + (32 + 80))
                scores(it, j)

            def body(it, final):
                front(it, 0)
                for j in range(LOOP):
                    if j < LOOP - 1:
                        front(it, j + 1)
                    numerators(it, j)
                    state(j, j % 2, LOOP * it + (CTX_STEPS + j))
                    back = final and earlier(it, j, 3)
                    if back:
                        turn_y(*back)

            pe.wait_ge(cols_ready, 2)
            pe.wait_ge(gate_step, 1)
            body(0, False)
            with pe.Fori(1, HALF) as it:
                body(it, False)
            body(HALF, True)
            with pe.Fori(HALF + 1, 2 * HALF) as it:
                body(it, True)
            for j in range(1, LOOP):
                turn_y(2 * HALF - 1, j)

        @block.scalar
        def _(act):
            act.wait_ge(rows_in, 64)
            act.activation(logf[:, :, :], fpre[:, :, :], ACT.Abs).then_inc(act_row, 1)
            act.wait_ge(act_row, 1)
            act.activation(logf[:, :, :], logf[:, :, :], ACT.Exp, scale=-1.0).then_inc(act_row, 1)
            act.wait_ge(act_row, 2)
            act.wait_ge(const_set, 6)
            act.activation(logf[:, :, :], logf[:, :, :], ACT.Ln, bias=ones[:, 0:1]).then_inc(act_row, 1)

            act.wait_ge(dve_row, 12)
            act.wait_ge(mprev_in, 32)
            for dr in range(2):
                act.activation(wsrow[:, dr, :], arow[:, dr, :], ACT.Exp, bias=nmlast[:, dr:dr + 1])
                act.activation(wirow[:, dr, :], mrow[:, dr, :], ACT.Exp, scale=-1.0, bias=mprev[:, dr:dr + 1])
                act.activation(wcol[:, dr:dr + 1], mlast[:, dr:dr + 1], ACT.Exp, scale=-1.0,
                               bias=mprev[:, dr:dr + 1]).then_inc(act_row, 1)
            act.wait_ge(dve_row, 13)
            act.activation(emrow[:, :, :], emrow[:, :, :], ACT.Exp, scale=-1.0, bias=logroot[:, 0:1])\
               .then_inc(act_row, 1)
            for dr in range(2):
                act.wait_ge(turned, dr + 1)
                act.copy(cols[:, dr, :, :].rearrange("p w r -> p (w r)"),
                         psN[:, dr, :, :].rearrange("p a b -> p (a b)")[:, 0:3 * HC]).then_inc(cols_ready, 1)
            act.wait_ge(cols_ready, 2)

            def column(dr, which, c, hd):
                return cols[:, dr, which, bass.ds(c + hd * NT, 1)]

            def weigh_k(step, dr, c, first=False):
                act.wait_ge(k_turned, step + 1)
                if not first:
                    act.wait_ge(u_ready, step - 1)
                for hd in range(HEADS):
                    ins = act.activation(kw[:, dr, hd, :], psK[:, hd, :], ACT.Copy, scale=column(dr, 1, c, hd))
                ins.then_inc(kw_ready, 1)

            for j, (dr, c) in enumerate(CTX):
                weigh_k(j, dr, c, j < 2)

            def weights(it, j):
                n = LOOP * it + j
                act.wait_ge(masked, n + 1)
                if j >= 2 or not first_body(it):
                    act.wait_ge(p_ready, n - 1)
                for hd in range(HEADS):
                    ins = act.activation(E[:, j % 2, hd, :], mb[:, j, hd, :], ACT.Exp, scale=-1.0,
                                         bias=column(j % 2, 0, chunk_of(it, j) + NT_CTX, hd))
                ins.then_inc(e_ready, 1)

            def front(it, j):
                weights(it, j)
                weigh_k(LOOP * it + (CTX_STEPS + j), j % 2, chunk_of(it, j) + NT_CTX)

            def squares(it, j):
                wait_count(act, gated, it, LOOP, j + 1 - DONE)
                for hd in range(HEADS):
                    ins = act.activation(sq[:, j % 2, hd, :], og[:, j, hd, :], ACT.Square,
                                         accum_out=ssq[:, j, hd:hd + 1])
                ins.then_inc(ssq_ready, 1)

            def copy_y(it, j):
                wait_count(act, y_turned, it, LOOP, j + 1 - DONE)
                wait_count(act, y_out[j % 2], it, 32, 16 * (j // 2 - 2 * HALF))
                act.copy(yT[:, j % 2, :, :], psY[:, :, :]).then_inc(yT_ready, 1)

            def body(it, final):
                front(it, 0)
                for j in range(LOOP):
                    if j < LOOP - 1:
                        front(it, j + 1)
                    for lag, stage in ((1, squares), (LOOP, copy_y)):
                        back = final and earlier(it, j, lag)
                        if back:
                            stage(*back)

            def split_wo(it):
                if first_body(it):
                    act.wait_ge(wo_in, 16)
                for k in range(2):
                    act.copy(wo_hi[:, bass.ds(2 * it + k, 1), :], stage[:, bass.ds(2 * it + k, 1), :])\
                       .then_inc(wo_high, 1)

            body(0, False)
            split_wo(0)
            with act.Fori(1, HALF) as it:
                body(it, False)
                split_wo(it)
            body(HALF, True)
            with act.Fori(HALF + 1, 2 * HALF) as it:
                body(it, True)
            squares(2 * HALF - 1, LOOP - 1)
            for j in range(LOOP):
                copy_y(2 * HALF - 1, j)

        @block.vector
        def _(dve):
            dve.tensor_copy(sfull[:, :, :], svec[:, :, 0:1].to_broadcast([P, KD, P])).then_inc(s_spread, 1)
            row = lambda t, dr, back=False: t[:, dr, ::-1] if back else t[:, dr, :]
            dve.wait_ge(rows_in, 64)
            dve.wait_ge(act_row, 3)
            dve.scalar_tensor_tensor(logf[:, :, :], fpre[:, :, :], 0.0, logf[:, :, :], ALU.min, ALU.subtract)\
               .then_inc(dve_row, 1)
            dve.wait_ge(dve_row, 1)
            dve.wait_ge(const_set, 6)
            for dr in range(2):
                dve.tensor_tensor_scan(row(bsum, dr, dr), ones[:, :], row(logf, dr, dr), 0.0,
                                       ALU.mult, ALU.add).then_inc(dve_row, 1)
            dve.wait_ge(dve_row, 3)
            dve.tensor_tensor(arow[:, :, :], ipre[:, :, :], bsum[:, :, :], ALU.subtract).then_inc(dve_row, 1)
            dve.wait_ge(dve_row, 4)
            for dr in range(2):
                dve.tensor_tensor_scan(row(mrow, dr, dr), row(arow, dr, dr), row(arow, dr, dr), -3.0e38,
                                       ALU.max, ALU.max).then_inc(dve_row, 1)
            dve.wait_ge(ends_in, 32)
            dve.tensor_tensor_scan(carry[:, 0, :], chain[:, 0, 1, :], chain[:, 0, 0, :], 0.0,
                                   ALU.max, ALU.add).then_inc(dve_row, 1)
            dve.tensor_tensor_scan(carry[:, 1, 1::-1], chain[:, 1, 1, 1::-1], chain[:, 1, 0, 1::-1], 0.0,
                                   ALU.max, ALU.add).then_inc(dve_row, 1)
            dve.wait_ge(dve_row, 8)
            dve.tensor_tensor_scan(carry[:, 1, NT - 1:1:-1], chain[:, 1, 1, NT - 1:1:-1],
                                   chain[:, 1, 0, NT - 1:1:-1], carry[:, 1, 0:1],
                                   ALU.max, ALU.add).then_inc(dve_row, 1)
            dve.wait_ge(dve_row, 9)
            dve.memset(mp[:, 0, 0:1], 0.0)
            dve.memset(mp[:, 1, 1:2], 0.0)
            dve.tensor_copy(mp[:, 0, 1:NT], carry[:, 0, 0:NT - 1])
            dve.tensor_copy(mp[:, 1, 0:1], carry[:, 1, 1:2])
            dve.tensor_copy(mp[:, 1, NT - 1:NT], carry[:, 1, 0:1])
            dve.tensor_copy(mp[:, 1, 2:NT - 1], carry[:, 1, 3:NT]).then_inc(dve_row, 1)
            dve.wait_ge(mprev_in, 32)
            dve.wait_ge(dve_row, 6)
            dve.wait_ge(ends_out, 64)
            for dr in range(2):
                end = P - 1 if dr == 0 else 0
                dve.tensor_scalar(mlast[:, dr:dr + 1], mrow[:, dr, end:end + 1], mprev[:, dr:dr + 1], None, ALU.max)
                ins = dve.tensor_scalar(nmlast[:, dr:dr + 1], mrow[:, dr, end:end + 1], mprev[:, dr:dr + 1], -1.0,
                                        ALU.max, ALU.mult)
            ins.then_inc(dve_row, 1)
            dve.wait_ge(dve_row, 11)
            for dr in range(2):
                ins = dve.tensor_scalar(mrow[:, dr, :], mrow[:, dr, :], mprev[:, dr:dr + 1], None, ALU.max)
            ins.then_inc(dve_row, 1)
            dve.wait_ge(dve_row, 12)
            dve.tensor_tensor(emrow[:, :, :], bsum[:, :, :], mrow[:, :, :], ALU.add).then_inc(dve_row, 1)

            def update(step, dr, c, first=False):
                dve.wait_ge(u_ready, step + 1)
                if not first:
                    dve.wait_ge(c_ready, step - 1)
                for hd in range(HEADS):
                    ins = dve.scalar_tensor_tensor(C[:, dr, hd, :], C[:, dr, hd, :], wc[:, dr, bass.ds(c + hd * NT, 1)],
                                                   psU[:, hd // 2, hd % 2, :], ALU.mult, ALU.add)
                ins.then_inc(c_ready, 1)

            dve.wait_ge(wc_in, 32)
            for j, (dr, c) in enumerate(CTX):
                update(j, dr, c, j < 2)

            def products(it, j):
                n = LOOP * it + j
                dve.wait_ge(s_ready, n + 1)
                dve.wait_ge(e_ready, n + 1)
                if j >= 2 or not first_body(it):
                    dve.wait_ge(num_ready, n - 1)
                dve.tensor_tensor(pm[:, j % 2, :, :], psS[j % 2][:, :, :], E[:, j % 2, :, :], ALU.mult)\
                   .then_inc(p_ready, 1)

            def normalise(it, j, final):
                n, b = LOOP * it + j, j % 2
                dve.wait_ge(num_ready, n + 1)
                floor = cols[:, b, 2, :].rearrange("p (h c) -> p h c", h=HEADS)[:, :, bass.ds(chunk_of(it, j) + NT_CTX, 1)]
                floor = floor.rearrange("p (a b) c -> p a b c", a=2)[:, :, :, 0]
                size = psN[:, :, :, DH]
                dn = den[:, b, :].rearrange("p (a b) -> p a b", a=2)
                dve.scalar_tensor_tensor(dn, size, -1.0, floor, ALU.mult, ALU.max).then_inc(den_neg, 1)
                dve.wait_ge(den_neg, n + 1)
                dve.tensor_tensor(dn, size, dn, ALU.max).then_inc(den_max, 1)
                dve.wait_ge(den_max, n + 1)
                dve.reciprocal(den[:, b, :], den[:, b, :]).then_inc(den_inv, 1)
                dve.wait_ge(den_inv, n + 1)
                if final:
                    dve.wait_ge(h_out[j], 16 * HALF)
                    if earlier(it, j, LOOP):
                        wait_count(dve, y_turned, it, LOOP, j + 1 - LOOP - DONE)
                elif not first_body(it):
                    dve.wait_ge(h_out[j], 16 * it)
                if final:
                    wait_count(dve, fin_in[j], it, 48, 48 * (1 - HALF))
                    for hd in range(HEADS):
                        ins = dve.scalar_tensor_tensor(h[:, j, hd, :], psN[:, hd // 2, hd % 2, 0:DH],
                                                       den[:, b, hd:hd + 1], other[:, j, hd, :], ALU.mult, ALU.add)
                else:
                    ins = dve.tensor_tensor(h[:, j, :, :].rearrange("p (a b) v -> p a b v", a=2), psN[:, :, :, 0:DH],
                                            dn.unsqueeze(3).to_broadcast([P, 2, 2, DH]), ALU.mult)
                ins.then_inc(h_ready, 1)

            def outputs(it, j):
                wait_count(dve, rinv_ready, it, LOOP, j + 1 - DONE)
                for hd in range(HEADS):
                    ins = dve.scalar_tensor_tensor(h[:, j, hd, :], og[:, j, hd, :], rinv[:, j, hd:hd + 1],
                                                   zg[:, j, hd, :], ALU.mult, ALU.mult)
                ins.then_inc(y_scaled, 1)
                wait_count(dve, y_scaled, it, LOOP, j + 1 - DONE)
                dve.tensor_tensor(h[:, j, :, :], h[:, j, :, :], gain[:, :].rearrange("p (h v) -> p h v", h=HEADS),
                                  ALU.mult).then_inc(y_ready, 1)

            def body(it, final):
                products(it, 0)
                for j in range(LOOP):
                    if j < LOOP - 1:
                        products(it, j + 1)
                    normalise(it, j, final)
                    update(LOOP * it + (CTX_STEPS + j), j % 2, chunk_of(it, j) + NT_CTX)
                    back = final and earlier(it, j, 2)
                    if back:
                        outputs(*back)

            dve.wait_ge(const_in, 48)
            dve.tensor_scalar(gain[:, :], gain[:, :], float(math.sqrt(DH)), None, ALU.mult).then_inc(gain_ready, 1)
            dve.wait_ge(gate_rows_in, 32)
            dve.wait_ge(gate_sum, 1)
            for c in range(2):
                cut = slice(c * TILE, (c + 1) * TILE)
                ins = dve.tensor_tensor(gate[:, cut], psS[c][:, :, :].rearrange("p h t -> p (h t)"), bgate[:, cut],
                                        ALU.add)
            ins.then_inc(gate_step, 1)
            dve.wait_ge(gate_step, 1)
            dve.scalar_tensor_tensor(gate[:, :], gate[:, :], ROOT_D, post, ALU.mult, ALU.mult)\
               .then_inc(gate_step, 1)

            def split_wo(it):
                for k in range(2):
                    block_k = bass.ds(2 * it + k, 1)
                    dve.wait_ge(wo_high, 2 * it + (k + 1))
                    dve.tensor_tensor(wo_lo[:, block_k, :], stage[:, block_k, :], wo_hi[:, block_k, :].bitcast(F32),
                                      ALU.subtract).then_inc(wo_low, 1)

            body(0, False)
            split_wo(0)
            with dve.Fori(1, HALF) as it:
                body(it, False)
                split_wo(it)
            dve.wait_ge(gain_ready, 1)
            body(HALF, True)
            with dve.Fori(HALF + 1, 2 * HALF) as it:
                body(it, True)
            for j in range(LOOP - 2, LOOP):
                outputs(2 * HALF - 1, j)


MAGIC = 12582912.0
TWO_PI_A = 6.28125
TWO_PI_B = 2 * math.pi - TWO_PI_A
PI_DOWN = 3.1415925
GROUPS = CH // P
HID = 64
HALF_T = T_LAT // 2
S_TILES = N2 // 2
Q_TILES = NQ // 4
F_TILES = N2 // 4


PER_UNIT = {"S": 2 * S_TILES + 1, "T": F_TILES + Q_TILES + 2 * F_TILES + Q_TILES,
            "X": F_TILES + Q_TILES + F_TILES + 2 * Q_TILES, "I": Q_TILES}
START = {"S": S_TILES + 1, "T": F_TILES + Q_TILES, "X": F_TILES + 2 * Q_TILES, "I": 0}
NORM_AFTER = 2


def places(start=None):
    return dict(start or START)


def hyena(nc, d, s):
    with ExitStack() as ctx:
        sb, ps = mem_makers(nc, ctx)
        sem = sem_maker(nc, ctx)
        hidden = sb("hidden", [P, HALF_T])
        tables = sb("tables", [P, 5, NQ, P])
        outer = sb("outer", [P, 2 * K1])
        back = sb("back", [K1, 2, P])
        ident = sb("ident_h", [P, P])
        ones = sb("ones_h", [P, P])
        guard = sb("guard_h", [P, 1])
        w3 = sb("w3", [P, 2, 2, P])
        fb = sb("fb", [P, 2, P])
        window = sb("window", [P, N2, P])
        f = sb("f", [P, N2, P])
        Bf = sb("Bf", [P, NQ, 8, N2])
        A2f = sb("A2f", [P, NQ, P])
        sums = sb("sums", [P, P])
        total = sb("total", [P, P])
        H = sb("H", [P, 2, NQ, P])
        xin = sb("xin", [P, T_LAT])
        x2 = sb("x2", [P, T_LAT])
        zh = sb("zh", [P, T_LAT])
        nat = sb("nat", [P, N2, P])
        x1 = sb("x1", [P, N2, P])
        B = sb("B", [P, NQ, 8, N2])
        Bi = B[:, :, :, :].rearrange("p q a n -> p (q a n)").rearrange("p (m q j) -> p m q j", q=NQ, j=4)
        A2 = sb("A2", [P, NQ, P])
        Ai = sb("Ai", [K1, 2, N2, P])
        prod = sb("prod", [P, 2, 2, 4, P])
        sqr = Bf[:, :, :, :].rearrange("p q a n -> p (q a n)")[:, 0:N2 * P].rearrange("p (n c) -> p n c", n=N2)

        arg, turns = [A2[:, :, :].rearrange("p q c -> p (q c)")[:, i * HALF_T:(i + 1) * HALF_T] for i in range(2)]
        early = Ai[:, :, :, :].rearrange("p r n c -> p (r n c)")
        feats, w1 = early[0:2 * 17, 0:HALF_T], early[0:2 * 17, HALF_T:HALF_T + P]
        early = prod[:, :, :, :, :].rearrange("p a b i c -> p (a b i c)")
        w2, fcol = early[:, 0:P], early[:, P:P + 4]

        psS = [ps(f"psS_h{i}", [P, 2, 8, NQ]) for i in range(2)]
        psT = [ps(f"psT{i}", [P, 4, P]) for i in range(2)]
        psX = [ps(f"psX{i}", [P, 4, P]) for i in range(2)]
        psI = [ps(f"psI{i}", [P, 4, P]) for i in range(2)]
        banks = {"S": psS, "T": psT, "X": psX, "I": psI}

        hid_in = sem("hid_in")
        hid_sum = sem("hid_sum")
        hid_step = [sem(f"hid_step{j}") for j in range(2)]
        hid_ready = sem("hid_ready")
        start_in = sem("start_in")
        filter_in = sem("filter_in")
        const_in = sem("const_in_h")
        const_set = sem("const_set_h")
        group_in = sem("group_in")
        x_in = sem("x_in")
        gates_in = sem("gates_in")
        summed = {r: sem(f"{r}_summed") for r in "STXI"}
        taken = {r: sem(f"{r}_taken") for r in "STXI"}
        squared = sem("squared")
        n2_summed = sem("n2_summed")
        root_ready = sem("root_ready")
        scale_ready = sem("scale_ready")
        f_scaled = sem("f_scaled")
        f_ready = sem("f_ready")
        gated = sem("gated_h")
        y_out = sem("y_out_h")

        block = ctx.enter_context(nc.Block())
        UNIT1 = {r: START[r] + PER_UNIT[r] for r in START}

        @block.sync
        def _(sp):
            def load_group(g):
                sp.dma_start(w3[:, :, :, :], d["fw3"][g]).then_inc(group_in, 16)
                sp.dma_start(window[:, :, :], d["window"][g]).then_inc(group_in, 16)
                sp.dma_start(fb[P // 2:P // 2 + 1, :, :], d["fbias"][g]).then_inc(group_in, 16)

            def load_x(block_row):
                sp.dma_start(xin[:, :], s["qhy"][block_row]).then_inc(x_in, 16)

            def load_gates(g):
                sp.dma_start(x2[:, :], s["qhy"][g + (HEADS + 2 * GROUPS)]).then_inc(gates_in, 16)
                sp.dma_start(zh[:, :], s["zh"][g]).then_inc(gates_in, 16)

            for dst, src in ((feats, d["feats"]), (w1, d["fw1"]), (w2, d["fw2"]), (fcol, d["fcol"])):
                sp.dma_start(dst, src).then_inc(hid_in, 16)
            load_group(0)
            sp.dma_start(ident[:, :], d["ident"]).then_inc(start_in, 16)
            load_x(HEADS)
            sp.dma_start(outer[:, :], d["outer"].rearrange("p a k -> p (a k)")).then_inc(start_in, 16)
            sp.dma_start(tables[:, 1:3, :, :], d["tables"][:, 1:3]).then_inc(filter_in, 16)
            for dst, src in ((tables[:, 0, :, :], d["tables"][:, 0]), (tables[:, 3:5, :, :], d["tables"][:, 3:5]),
                             (back[:, :, :], d["back"])):
                sp.dma_start(dst, src).then_inc(const_in, 16)
            sp.wait_ge(summed["T"], F_TILES)
            load_x(HEADS + GROUPS)
            load_gates(0)

            def body(g, last):
                if not last:
                    wait_count(sp, summed["T"], g, 2 * PER_UNIT["T"], START["T"] + F_TILES)
                    load_x(g + (HEADS + 1))
                    wait_count(sp, f_ready, g, 2, 2)
                    load_group(g + 1)
                    wait_count(sp, summed["T"], g, 2 * PER_UNIT["T"], UNIT1["T"] + F_TILES)
                    load_x(g + (HEADS + GROUPS + 1))
                end = UNIT1["X"] + Q_TILES + F_TILES + (0 if last else F_TILES)
                wait_count(sp, taken["X"], g, 2 * PER_UNIT["X"], end)
                sp.dma_start(s["y"][g + HEADS], x2[:, :]).then_inc(y_out, 16)
                wait_count(sp, y_out, g, 16, 16)
                if not last:
                    load_gates(g + 1)

            body(0, False)
            with sp.Fori(1, GROUPS - 1) as g:
                body(g, False)
            body(GROUPS - 1, True)

        @block.gpsimd
        def _(pool):
            pool.memset(ones[:, :], 1.0).then_inc(const_set, 1)
            pool.memset(guard[:, :], EPS).then_inc(const_set, 1)
            with pool.Fori(0, GROUPS) as g:
                pool.wait_ge(gates_in, 32 * g + 32)
                pool.tensor_tensor(x2[:, :], x2[:, :], zh[:, :], ALU.mult).then_inc(gated, 1)

        @block.tensor
        def _(pe):
            def fill(g, at, ring):
                n = at[ring]
                at[ring] += 1
                wait_count(pe, taken[ring], g, 2 * PER_UNIT[ring], n - 1)
                return banks[ring][n % 2]

            def outer_tile(g, at, src, t):
                bank = fill(g, at, "S")
                for i in range(2):
                    mm = pe.matmul(bank[:, i, :, :].rearrange("p a q -> p (a q)"), src[:, 2 * t + i, :], outer[:, :],
                                   start=True, stop=True)
                mm.then_inc(summed["S"], 1)

            def turn_x(g, at):
                for t in range(F_TILES):
                    bank = fill(g, at, "T")
                    for i in range(4):
                        mm = pe.transpose(bank[:, i, :], xin[:, 4 * t + i:T_LAT:N2], ident[:, :])
                    mm.then_inc(summed["T"], 1)

            def to_rows(g, at, src, t):
                bank = fill(g, at, "T")
                for i in range(4):
                    mm = pe.transpose(bank[:, i, :], src[:, 4 * t + i, :, :].rearrange("p a n -> p (a n)"), ident[:, :])
                mm.then_inc(summed["T"], 1)

            def in_time(g, at, o):
                for t in range(F_TILES):
                    bank = fill(g, at, "X")
                    for i in range(2):
                        mm = pe.matmul(bank[:, 2 * i:2 * i + 2, :], hidden[:, 2 * t + i:HALF_T:N2 // 2],
                                       w3[:, o, :, :].rearrange("k e c -> k (e c)"), start=True, stop=True)
                    mm.then_inc(summed["X"], 1)

            def norm(g, at, unit):
                wait_count(pe, n2_summed, g, 2, unit + 1)
                bank = fill(g, at, "S")
                pe.matmul(bank[:, :, :, :].rearrange("p b a q -> p (b a q)")[:, 0:P], ones[:, :], sums[:, :],
                          start=True, stop=True).then_inc(summed["S"], 1)

            def filter_outer(g, at, unit):
                wait_count(pe, f_ready, g, 2, unit + 1)
                for t in range(S_TILES):
                    outer_tile(g, at, f, t)

            def filter_inner(g, at):
                wait_count(pe, taken["S"], g, 2 * PER_UNIT["S"], at["S"])
                for t in range(Q_TILES + 1):
                    if t < Q_TILES:
                        to_rows(g, at, Bf, t)
                    if t:
                        wait_count(pe, taken["T"], g, 2 * PER_UNIT["T"], at["T"] - (t < Q_TILES))
                        for part in range(2):
                            bank = fill(g, at, "X")
                            for i in range(4):
                                q = 4 * (t - 1) + i
                                mm = pe.matmul(bank[:, i, :], tables[:, 1 + part, q, :], A2f[:, q, :],
                                               start=True, stop=True)
                            mm.then_inc(summed["X"], 1)

            pe.wait_ge(hid_in, 64)
            for layer in range(2):
                for j in range(2):
                    cut = slice(j * TILE, (j + 1) * TILE)
                    if layer:
                        pe.wait_ge(hid_ready, j + 1)
                    w, src = (w2, hidden[:, cut]) if layer else (w1, feats[:, cut])
                    pe.matmul(psX[j][:, :, :], w, src, start=True, stop=True).then_inc(hid_sum, 1)

            pe.wait_ge(const_set, 2)
            pe.wait_ge(group_in, 48)
            pe.wait_ge(start_in, 32)
            pe.wait_ge(x_in, 16)
            pe.wait_ge(hid_ready, 4)
            at = {"S": 0, "T": 0, "X": 0, "I": 0}
            in_time(0, at, 0)
            turn_x(0, at)
            norm(0, at, 0)
            filter_outer(0, at, 0)
            pe.wait_ge(filter_in, 16)
            filter_inner(0, at)
            pe.wait_ge(const_in, 48)

            def unit(g, at, o, more):
                for t in range(S_TILES):
                    if t % 2 == 0:
                        if o:
                            wait_count(pe, taken["X"], g, 2 * PER_UNIT["X"],
                                       UNIT1["X"] - 2 * Q_TILES - F_TILES + t // 2 + 1)
                        elif isinstance(g, int) and g == 0:
                            pe.wait_ge(taken["T"], t // 2 + 1)
                        else:
                            wait_count(pe, taken["T"], g, 2 * PER_UNIT["T"],
                                       UNIT1["T"] - 2 * PER_UNIT["T"] + t // 2 + 1)
                    outer_tile(g, at, nat, t)
                if more:
                    wait_count(pe, x_in, g, 32, 32 + 16 * o)
                    turn_x(g, at)
                wait_count(pe, taken["S"], g, 2 * PER_UNIT["S"], at["S"])
                rows_at = at["T"]
                for t in range(Q_TILES):
                    to_rows(g, at, B, t)
                if more:
                    wait_count(pe, group_in, g, 48, 48 + 48 * o)
                    in_time(g, at, 1 - o)

                def inverse(t, product_at):
                    wait_count(pe, taken["X"], g, 2 * PER_UNIT["X"], product_at + 1)
                    bank = fill(g, at, "I")
                    for i in range(4):
                        q = 4 * t + i
                        for part in range(2):
                            mm = pe.matmul(bank[:, i, :], prod[:, t % 2, part, i, :], tables[:, 3 + part, q, :],
                                           start=(part == 0), stop=(part == 1))
                    mm.then_inc(summed["I"], 1)

                for t in range(Q_TILES):
                    wait_count(pe, taken["T"], g, 2 * PER_UNIT["T"], rows_at + t + 1)
                    bank = fill(g, at, "X")
                    for i in range(4):
                        mm = pe.matmul(bank[:, i, :], tables[:, 0, 4 * t + i, :], A2[:, 4 * t + i, :],
                                       start=True, stop=True)
                    mm.then_inc(summed["X"], 1)
                    if t:
                        inverse(t - 1, at["X"] - 2)
                    if more and t == NORM_AFTER:
                        norm(g, at, o + 1)
                inverse(Q_TILES - 1, at["X"] - 1)
                if more:
                    filter_outer(g, at, o + 1)
                wait_count(pe, taken["I"], g, 2 * PER_UNIT["I"], at["I"])
                for t in range(F_TILES + 1):
                    if t < F_TILES:
                        for r in range(2):
                            bank = fill(g, at, "T")
                            for i in range(4):
                                mm = pe.transpose(bank[0:K1, i, :], Bi[:, N2 * r + 4 * t + i, :, :].rearrange("c q j -> c (q j)"),
                                                  ident[:, :])
                            mm.then_inc(summed["T"], 1)
                    if t:
                        n2 = 4 * (t - 1)
                        wait_count(pe, taken["T"], g, 2 * PER_UNIT["T"], at["T"] - 2 * (t < F_TILES))
                        bank = fill(g, at, "X")
                        if o == 0:
                            for r in range(2):
                                mm = pe.matmul(bank[:, :, :], back[:, r, :],
                                               Ai[:, r, n2:n2 + 4, :].rearrange("k n c -> k (n c)"),
                                               start=(r == 0), stop=(r == 1))
                        else:
                            for i in range(4):
                                for r in range(2):
                                    mm = pe.matmul(bank[:, i, :], Ai[:, r, n2 + i, :], back[:, r, :],
                                                   start=(r == 0), stop=(r == 1))
                        mm.then_inc(summed["X"], 1)
                if more:
                    filter_inner(g, at)

            def body(g, last):
                at = places()
                unit(g, at, 0, True)
                unit(g, at, 1, not last)

            body(0, False)
            with pe.Fori(1, GROUPS - 1) as g:
                body(g, False)
            body(GROUPS - 1, True)

        @block.scalar
        def _(act):
            def take(g, at, ring, dst, rows=P):
                n = at[ring]
                at[ring] += 1
                wait_count(act, summed[ring], g, 2 * PER_UNIT[ring], n + 1)
                act.copy(dst, banks[ring][n % 2][0:rows]).then_inc(taken[ring], 1)

            def take_outer(g, at, dst):
                for t in range(S_TILES):
                    take(g, at, "S", dst[:, :, :, 2 * t:2 * t + 2].rearrange("p q a n -> p n a q"))

            def take_tiles(g, at, ring, dst, tiles):
                for t in range(tiles):
                    take(g, at, ring, dst[:, 4 * t:4 * t + 4])

            def square(g, x_at, unit):
                wait_count(act, taken["X"], g, 2 * PER_UNIT["X"], x_at)
                act.activation(sqr, f[:, :, :], ACT.Square).then_inc(squared, 1)

            def root(g, at):
                n = at["S"]
                at["S"] += 1
                wait_count(act, summed["S"], g, 2 * PER_UNIT["S"], n + 1)
                act.activation(total[:, :], banks["S"][n % 2][:, :, :, :].rearrange("p b a q -> p (b a q)")[:, 0:P],
                               ACT.Sqrt, bias=guard[:, 0:1]).then_inc(taken["S"], 1)

            for layer in range(2):
                for j in range(2):
                    cut = slice(j * TILE, (j + 1) * TILE)
                    act.wait_ge(hid_step[j], 6 * (layer + 1))
                    act.wait_ge(hid_sum, 2 * layer + j + 1)
                    act.activation(hidden[:, cut], arg[:, cut], ACT.Sin).then_inc(hid_ready, 1)

            act.wait_ge(const_set, 2)
            at = {"S": 0, "T": 0, "X": 0, "I": 0}
            square(0, F_TILES, 0)
            take_tiles(0, at, "T", nat, F_TILES)
            root(0, at)
            take_outer(0, at, Bf)
            take_tiles(0, at, "T", A2f, Q_TILES)

            def unit(g, at, o, more):
                take_outer(g, at, B)
                if more:
                    take_tiles(g, at, "T", nat if o else x1, F_TILES)
                take_tiles(g, at, "T", A2, Q_TILES)
                if more:
                    square(g, (UNIT1 if o else START)["X"] + F_TILES, o + 1)
                for t in range(Q_TILES):
                    n = at["I"]
                    at["I"] += 1
                    wait_count(act, summed["I"], g, 2 * PER_UNIT["I"], n + 1)
                    act.copy(Bi[:, :, 4 * t:4 * t + 4, :],
                             psI[n % 2][:, :, :].rearrange("p q (m j) -> p m q j", j=4)).then_inc(taken["I"], 1)
                    if more and t == NORM_AFTER - 1:
                        root(g, at)
                if more:
                    take_outer(g, at, Bf)
                for t in range(F_TILES):
                    for r in range(2):
                        take(g, at, "T", Ai[:, r, 4 * t:4 * t + 4, :], K1)
                if more:
                    take_tiles(g, at, "T", A2f, Q_TILES)

            def body(g, last):
                at = places()
                unit(g, at, 0, True)
                unit(g, at, 1, not last)

            body(0, False)
            with act.Fori(1, GROUPS - 1) as g:
                body(g, False)
            body(GROUPS - 1, True)

        @block.vector
        def _(dve):
            def tile_of(g, at, ring):
                n = at[ring]
                at[ring] += 1
                wait_count(dve, summed[ring], g, 2 * PER_UNIT[ring], n + 1)
                return banks[ring][n % 2][:, :, :]

            def weigh(g, at, loads):
                wait_count(dve, group_in, g, 48, 48 * loads)
                for t in range(F_TILES):
                    dve.tensor_tensor(f[:, 4 * t:4 * t + 4, :], tile_of(g, at, "X"), window[:, 4 * t:4 * t + 4, :],
                                      ALU.mult).then_inc(taken["X"], 1)

            def sum_squares(g, unit):
                wait_count(dve, squared, g, 2, unit + 1)
                dve.tensor_reduce(sums[:, :], sqr.rearrange("p n c -> p c n"), AX.X, ALU.add).then_inc(n2_summed, 1)

            def scale(g, at, unit, o):
                wait_count(dve, taken["S"], g, 2 * PER_UNIT["S"], at["S"] + 1)
                dve.reciprocal(total[:, :], total[:, :]).then_inc(scale_ready, 1)
                wait_count(dve, scale_ready, g, 2, unit + 1)
                dve.tensor_tensor(f[:, :, :], f[:, :, :], total[:, :].unsqueeze(1).to_broadcast([P, N2, P]),
                                  ALU.mult).then_inc(f_scaled, 1)
                wait_count(dve, f_scaled, g, 2, unit + 1)
                dve.tensor_tensor(f[P // 2:P // 2 + 1, 0, :], f[P // 2:P // 2 + 1, 0, :],
                                  fb[P // 2:P // 2 + 1, o, :], ALU.add).then_inc(f_ready, 1)

            def take_spectrum(g, at):
                for t in range(Q_TILES):
                    for part in range(2):
                        dve.tensor_copy(H[:, part, 4 * t:4 * t + 4, :], tile_of(g, at, "X")).then_inc(taken["X"], 1)

            dve.wait_ge(hid_in, 64)
            for layer in range(2):
                for step in range(6):
                    for j in range(2):
                        cut = slice(j * TILE, (j + 1) * TILE)
                        a, k = arg[:, cut], turns[:, cut]
                        if step:
                            dve.wait_ge(hid_step[j], 6 * layer + step)
                        elif layer:
                            dve.wait_ge(hid_ready, j + 1)
                        if step == 0:
                            dve.wait_ge(hid_sum, 2 * layer + j + 1)
                            ins = dve.tensor_scalar(a, psX[j][:, :, :].rearrange("p i c -> p (i c)"),
                                                    fcol[:, 2 * layer:2 * layer + 1],
                                                    fcol[:, 2 * layer + 1:2 * layer + 2], ALU.add, ALU.mult)
                        elif step == 1:
                            ins = dve.tensor_scalar(k, a, 1.0 / (2 * math.pi), MAGIC, ALU.mult, ALU.add)
                        elif step == 2:
                            ins = dve.tensor_scalar(k, k, -MAGIC, None, ALU.add)
                        elif step < 5:
                            ins = dve.scalar_tensor_tensor(a, k, -(TWO_PI_A, TWO_PI_B)[step - 3], a, ALU.mult, ALU.add)
                        else:
                            ins = dve.tensor_scalar(a, a, PI_DOWN, -PI_DOWN, ALU.min, ALU.max)
                        ins.then_inc(hid_step[j], 1)

            at = {"S": 0, "T": 0, "X": 0, "I": 0}
            weigh(0, at, 1)
            sum_squares(0, 0)
            scale(0, at, 0, 0)
            take_spectrum(0, at)

            def unit(g, at, o, more):
                spectrum_at = at["X"]
                if more:
                    weigh(g, at, 1 + o)
                wait_count(dve, taken["X"], g, 2 * PER_UNIT["X"], spectrum_at)
                for t in range(Q_TILES):
                    wait_count(dve, summed["I"], g, 2 * PER_UNIT["I"], Q_TILES * o + t - 1)
                    tile = tile_of(g, at, "X")
                    for part in range(2):
                        ins = dve.tensor_tensor(prod[:, t % 2, part], tile, H[:, part, 4 * t:4 * t + 4, :], ALU.mult)
                    ins.then_inc(taken["X"], 1)
                    if more and t == NORM_AFTER - 1:
                        sum_squares(g, o + 1)
                    if more and t == Q_TILES - 2:
                        scale(g, {"S": (UNIT1 if o else START)["S"] + S_TILES}, o + 1, 1 - o)
                if o:
                    wait_count(dve, gated, g, 1, 1)
                else:
                    wait_count(dve, taken["T"], g, 2 * PER_UNIT["T"], START["T"] + F_TILES)
                for t in range(F_TILES):
                    tile = tile_of(g, at, "X")
                    if o:
                        y = x2[:, :].rearrange("p (t n) -> p n t", n=N2)[:, 4 * t:4 * t + 4, :]
                        ins = dve.tensor_tensor(y, tile, y, ALU.mult)
                    else:
                        ins = dve.tensor_tensor(nat[:, 4 * t:4 * t + 4, :], tile, x1[:, 4 * t:4 * t + 4, :], ALU.mult)
                    ins.then_inc(taken["X"], 1)
                if more:
                    take_spectrum(g, at)

            def body(g, last):
                at = places()
                unit(g, at, 0, True)
                unit(g, at, 1, not last)

            body(0, False)
            with dve.Fori(1, GROUPS - 1) as g:
                body(g, False)
            body(GROUPS - 1, True)


def output(nc, d, s, w_hi, w_lo, gate, out):
    with ExitStack() as ctx:
        sb, ps = mem_makers(nc, ctx)
        sem = sem_maker(nc, ctx)
        y_hi = sb("y_hi", [P, 2, KD, P], F32R)
        y_lo = sb("y_lo", [P, 2, KD, P], F32R)
        y = sb("y", [P, 2, KD, P])
        x = sb("x_o", [P, 2, D])
        z = sb("z_o", [P, 2, D])
        sumsq = sb("sumsq_o", [P, 2, 2])
        rinv = sb("rinv_o", [P, 2])
        power = sb("power_o", [P, 2])

        acc = [[ps(f"acc{i}{c}", [P, TILE]) for c in range(2)] for i in range(2)]

        power_set = sem("power_set_o")
        y_in = [sem(f"y_in{i}") for i in range(2)]
        x_in = [sem(f"xo_in{i}") for i in range(2)]
        hi_ready = sem("yhi_ready")
        lo_ready = sem("ylo_ready")
        acc_ready = sem("acc_ready")
        squared = sem("squared_o")
        rinv_step = sem("rinv_step_o")
        gated = sem("gated_o")
        res_ready = sem("res_ready_o")
        out_done = [sem(f"out_done{i}") for i in range(2)]

        block = ctx.enter_context(nc.Block())

        @block.sync
        def _(sp):
            def load_y(t, b):
                sp.dma_start(y[:, b, :, :], s["y"][:, :, bass.ts(t, P)].rearrange("k p t -> p k t"))\
                  .then_inc(y_in[b], 16)

            def load_x(t, b):
                sp.dma_start(x[:, b, :], d["x"][bass.ts(t, P), :]).then_inc(x_in[b], 16)

            for b in range(2):
                load_y(b, b)
            for b in range(2):
                load_x(b, b)

            def store(i, b, more):
                if more:
                    sp.wait_ge(lo_ready, 2 * i + (b + 1))
                    load_y(2 * i + (b + 2), b)
                sp.wait_ge(res_ready, 2 * i + (b + 1))
                sp.dma_start(out[bass.ts(2 * i + b, P), :], z[:, b, :]).then_inc(out_done[b], 16)
                if more:
                    load_x(2 * i + (b + 2), b)

            with sp.Fori(0, NT_LAT // 2 - 1) as i:
                for b in range(2):
                    store(i, b, True)
            for b in range(2):
                store(NT_LAT // 2 - 1, b, False)
            for b in range(2):
                sp.wait_ge(out_done[b], 16 * (NT_LAT // 2))

        @block.gpsimd
        def _(pool):
            pool.memset(power[:, 0:1], -0.5).then_inc(power_set, 1)
            pool.memset(power[:, 1:2], D * EPS).then_inc(power_set, 1)
            pool.wait_ge(power_set, 2)
            with pool.Fori(0, NT_LAT // 2) as i:
                for b in range(2):
                    n = 2 * i + (b + 1)
                    pool.wait_ge(squared, n)
                    pool.tensor_tensor(rinv[:, b:b + 1], sumsq[:, b, 0:1], sumsq[:, b, 1:2], ALU.add)\
                        .then_inc(rinv_step, 1)
                    pool.wait_ge(rinv_step, 6 * i + (3 * b + 1))
                    pool.tensor_tensor(rinv[:, b:b + 1], rinv[:, b:b + 1], power[:, 1:2], ALU.add)\
                        .then_inc(rinv_step, 1)
                    pool.wait_ge(rinv_step, 6 * i + (3 * b + 2))
                    pool.tensor_tensor(rinv[:, b:b + 1], rinv[:, b:b + 1], power[:, 0:1], ALU.pow)\
                        .then_inc(rinv_step, 1)

        @block.tensor
        def _(pe):
            def tile(i, b, first):
                pe.wait_ge(hi_ready, 2 * i + (b + 1))
                pe.wait_ge(lo_ready, 2 * i + (b + 1))
                if not first:
                    pe.wait_ge(gated, 2 * i + (b - 1))
                for c in range(2):
                    o, cut = acc[b][c][:, :], slice(c * TILE, (c + 1) * TILE)
                    for k in range(KD):
                        pe.matmul(o, y_hi[:, b, k, :], w_hi[:, k, cut], start=(k == 0), stop=False)
                        pe.matmul(o, y_hi[:, b, k, :], w_lo[:, k, cut], start=False, stop=False)
                        mm = pe.matmul(o, y_lo[:, b, k, :], w_hi[:, k, cut], start=False, stop=(k == KD - 1))
                mm.then_inc(acc_ready, 1)

            for b in range(2):
                tile(0, b, True)
            with pe.Fori(1, NT_LAT // 2) as i:
                for b in range(2):
                    tile(i, b, False)

        @block.scalar
        def _(act):
            def high(i, b, first):
                act.wait_ge(y_in[b], 16 * i + 16)
                if not first:
                    act.wait_ge(acc_ready, 2 * i + (b - 1))
                act.copy(y_hi[:, b], y[:, b]).then_inc(hi_ready, 1)

            for b in range(2):
                high(0, b, True)

            def squares(i, b, first):
                act.wait_ge(acc_ready, 2 * i + (b + 1))
                if not first:
                    act.wait_ge(out_done[b], 16 * i)
                for c in range(2):
                    ins = act.activation(z[:, b, c * TILE:(c + 1) * TILE], acc[b][c][:, :], ACT.Square,
                                         accum_out=sumsq[:, b, c:c + 1])
                ins.then_inc(squared, 1)

            def body(i, first, last):
                for b in range(2):
                    squares(i, b, first)
                    if not last:
                        high(i + 1, b, False)

            body(0, True, False)
            with act.Fori(1, NT_LAT // 2 - 1) as i:
                body(i, False, False)
            body(NT_LAT // 2 - 1, False, True)

        @block.vector
        def _(dve):
            def low(i, b):
                dve.wait_ge(hi_ready, 2 * i + (b + 1))
                dve.tensor_tensor(y_lo[:, b], y[:, b], y_hi[:, b].bitcast(F32), ALU.subtract).then_inc(lo_ready, 1)

            for b in range(2):
                low(0, b)
            def finish(i, b):
                n = 2 * i + (b + 1)
                dve.wait_ge(rinv_step, 6 * i + (3 * b + 3))
                for c in range(2):
                    cut = slice(c * TILE, (c + 1) * TILE)
                    ins = dve.scalar_tensor_tensor(z[:, b, cut], acc[b][c][:, :], rinv[:, b:b + 1], gate[:, cut],
                                                   ALU.mult, ALU.mult)
                ins.then_inc(gated, 1)
                dve.wait_ge(gated, n)
                dve.wait_ge(x_in[b], 16 * i + 16)
                dve.tensor_tensor(z[:, b, :], z[:, b, :], x[:, b, :], ALU.add).then_inc(res_ready, 1)

            def body(i, last):
                for b in range(2):
                    if not last:
                        low(i + 1, b)
                    finish(i, b)

            with dve.Fori(0, NT_LAT // 2 - 1) as i:
                body(i, False)
            body(NT_LAT // 2 - 1, True)


def build(nc, d, out, stages=("project", "mlstm", "hyena", "output")):
    scratch = {
        "gates": (P, T_ALL), "k": (HEADS, P, T_ALL), "v": (NT, P, CH), "qhy": (16, P, T_LAT),
        "ozh": (2, NT_LAT, P, CH), "zh": (GROUPS, P, T_LAT), "rows": (2, 2, HEADS * NT, P), "small": (2, 4, HEADS * NT),
        "hf": (NT_LAT, P, CH), "y": (KD, P, T_LAT),
    }
    s = {k: nc.dram_tensor(f"s_{k}", v, F32).ap() for k, v in scratch.items()}
    with ExitStack() as ctx:
        svec = ctx.enter_context(nc.sbuf_tensor("svec", [P, KD, 2], F32))
        project(nc, d, s, svec)
        if "hyena" in stages:
            hyena(nc, d, s)
        w_hi = ctx.enter_context(nc.sbuf_tensor("wo_hi", [P, KD, D], F32R))
        w_lo = ctx.enter_context(nc.sbuf_tensor("wo_lo", [P, KD, D], F32R))
        gate = ctx.enter_context(nc.sbuf_tensor("gate", [P, D], F32))
        if "mlstm" in stages:
            mlstm(nc, d, s, svec, w_hi, w_lo, gate)
        if "output" in stages:
            output(nc, d, s, w_hi, w_lo, gate, out)


def columns(v):
    return np.ascontiguousarray(v.reshape(-1, P).T)


def dft_tables():
    n1, k1 = np.arange(P), np.arange(K1)
    n2, k2 = np.arange(N2), np.arange(N2)
    ang = -2 * np.pi * np.outer(n1, k1 + 0.5) / N1
    outer = np.stack([np.cos(ang), np.sin(ang)], 1)
    fwd = np.zeros((NQ, 4, 2, N2, 4, 2, N2))
    inv = np.zeros((NQ, 4, 2, N2, 4, 2, N2))
    for q in range(NQ):
        for j in range(4):
            a = -2 * np.pi * (n2[:, None] * (NQ * j + q + 0.5) / N + n2[:, None] * k2 / N2)
            c, z = np.cos(a), np.sin(a)
            fwd[q, j, 0, :, j, 0, :], fwd[q, j, 1, :, j, 0, :] = c, -z
            fwd[q, j, 0, :, j, 1, :], fwd[q, j, 1, :, j, 1, :] = z, c
            c, z = c.T, -z.T
            inv[q, j, 0, :, j, 0, :], inv[q, j, 1, :, j, 0, :] = c, -z
            inv[q, j, 0, :, j, 1, :], inv[q, j, 1, :, j, 1, :] = z, c
    turned = np.empty_like(inv)
    turned[:, :, 0], turned[:, :, 1] = inv[:, :, 1], -inv[:, :, 0]
    fwd_re, fwd_im = np.empty_like(fwd), np.empty_like(fwd)
    fwd_re[:, :, :, :, :, 0], fwd_re[:, :, :, :, :, 1] = fwd[:, :, :, :, :, 0], fwd[:, :, :, :, :, 0]
    fwd_im[:, :, :, :, :, 0], fwd_im[:, :, :, :, :, 1] = fwd[:, :, :, :, :, 1], fwd[:, :, :, :, :, 1]
    fwd, fwd_re, fwd_im = [a.transpose(0, 2, 1, 3, 4, 5, 6).reshape(NQ, P, P) for a in (fwd, fwd_re, fwd_im)]
    inv, turned = [a.transpose(0, 1, 2, 3, 5, 6, 4).reshape(NQ, P, P) for a in (inv, turned)]
    ang = 2 * np.pi * np.outer(k1 + 0.5, n1 + N1 // 3) / N1
    back = np.stack([np.cos(ang), -np.sin(ang)], 1) * (2.0 / N)
    back = back.reshape(4, NQ, 2, P).transpose(1, 0, 2, 3).reshape(K1, 2, P)
    tables = np.stack([fwd, fwd_re, fwd_im, inv, turned], 0).transpose(2, 0, 1, 3)
    f = lambda a: np.ascontiguousarray(a.astype(np.float32))
    return f(outer), f(tables), f(back)


def filter_tables():
    f = np.float32
    pos = np.arange(T_LAT, dtype=f)
    bands = np.arange(1, 9, dtype=f)
    ang = f(2.0 * math.pi / T_LAT) * pos[:, None] * bands[None, :]
    feats = np.concatenate([(pos / f(T_LAT))[:, None], np.sin(ang), np.cos(ang)], -1).astype(f)
    lo, hi = math.log(1e-2) / 1.5, math.log(1e-2) / 0.3
    rates = np.abs(np.linspace(lo, hi, CH, dtype=f))
    offset = np.abs(pos - T_LAT // 2) / f(T_LAT / 2)
    window = np.exp(-offset[:, None] * rates).astype(f)
    window = window.reshape(P, N2, 4, P).transpose(2, 0, 1, 3)
    feats = feats.T.reshape(17, P, N2 // 2, 2).transpose(3, 0, 1, 2).reshape(2 * 17, T_LAT // 2)
    return np.ascontiguousarray(feats), np.ascontiguousarray(window)


def two_blocks(w):
    out = np.zeros((2 * w.shape[0], 2 * w.shape[1]), np.float32)
    out[:w.shape[0], :w.shape[1]] = w
    out[w.shape[0]:, w.shape[1]:] = w
    return out


def lay_out(a):
    a = {k: np.asarray(v) for k, v in a.items()}
    w = a["w_in"][0]
    cuts = np.cumsum([2 * CH, CH, CH, CH, 4 * HEADS, 3 * CH, CH])
    qk, v, o, zm, g, hy, zh = np.split(w, cuts[:-1], axis=1)
    wide = np.concatenate([qk[:, CH:], v, qk[:, :CH], hy, o, zm, zh], 1)
    w_in = wide.reshape(KD, P, N_SLOTS, SLOT).transpose(2, 1, 0, 3)
    w_gate = np.zeros((P, KD, P), np.float32)
    gbias = np.zeros((P, 1), np.float32)
    for kind in range(4):
        at = slice(32 * kind, 32 * kind + HEADS)
        w_gate[:, :, at] = g[:, kind * HEADS:(kind + 1) * HEADS].reshape(KD, P, HEADS).transpose(1, 0, 2)
        gbias[at, 0] = a["b_gates"][0, kind * HEADS:(kind + 1) * HEADS]
    wm = a["w_mod"][0].reshape(KD, P, 3 * D // SLOT, SLOT).transpose(2, 1, 0, 3)
    taps = np.concatenate([a["conv_qk_w"][0][:, CH:], a["conv_qk_w"][0][:, :CH], a["hy_conv_w"][0]], 1)
    bias = np.concatenate([a["conv_qk_b"][0][CH:], a["conv_qk_b"][0][:CH], a["hy_conv_b"][0]])
    coef = np.concatenate([taps, bias[None]], 0).reshape(4, 20, P).transpose(2, 1, 0)
    w3 = np.zeros((GROUPS, 2, HID, 2, 2, P), np.float32)
    for e in range(2):
        w3[:, e, :, :, e] = a["filt_w3"][0].reshape(HID, 2, GROUPS, P).transpose(2, 0, 1, 3)
    w3 = w3.reshape(GROUPS, P, 2, 2, P)
    outer, tables, back = dft_tables()
    feats, window = filter_tables()
    row = np.arange(P)
    before = row[:, None] <= row[None, :]
    far = np.float32(1e30)
    out = {
        "x": a["x"][0], "ctx": a["ctx"][0],
        "cvec": np.stack([columns(a["c"][0]), columns(a["c_ctx"])], 2),
        "w_mod": wm, "bmod": columns(a["b_mod"][0, :2 * D]), "bgate": a["b_mod"][0, 2 * D:][None],
        "pgain": columns(a["pre_gain"][0]), "post": a["post_gain"][0][None],
        "gbias": gbias, "w_gate": w_gate, "w_in": w_in, "coef": coef,
        "ident": np.eye(P, dtype=np.float32),
        "mask": np.stack([np.where(before, 0, far), np.where(before.T, 0, far)], 1).astype(np.float32),
        "mh_gain": a["mh_gain"][0][None],
        "outer": outer, "tables": tables, "back": back, "feats": feats, "window": window,
        "fw1": two_blocks(a["filt_w1"][0]), "fw2": two_blocks(a["filt_w2"][0]),
        "fw3": w3,
        "fcol": np.tile(np.stack([a["filt_b1"][0], a["filt_freq"][0, 0],
                                  a["filt_b2"][0], a["filt_freq"][0, 1]], 1), (2, 1)),
        "fbias": a["filt_bias"][0].reshape(2, 4, P).transpose(1, 0, 2)[:, None],
        "w_out": a["w_out"][0].reshape(KD, P, D).transpose(1, 0, 2),
    }
    return {k: np.ascontiguousarray(v) for k, v in out.items()}


def kernel(**inputs):
    from concourse import bacc
    from concourse.bass_utils import run_bass_kernel_spmd

    nc = bacc.Bacc("TRN2", target_bir_lowering=False, num_devices=1, dynamic_dma_scratch_size=1024)
    arrays = {f"in_{k}": v for k, v in lay_out(inputs).items()}
    d = {k[3:]: nc.dram_tensor(k, v.shape, mybir.dt.from_np(v.dtype), kind="ExternalInput").ap()
         for k, v in arrays.items()}
    out = nc.dram_tensor("out", (T_LAT, D), F32, kind="ExternalOutput").ap()
    build(nc, d, out)
    r = run_bass_kernel_spmd(nc, [arrays], core_ids=[0])
    return r.results[0]["out"].reshape(1, T_LAT, D)
```

```python
from contextlib import ExitStack
import math

import numpy as np
import concourse.bass as bass
from concourse import mybir
from concourse.alu_op_type import AluOpType as ALU

ACT = mybir.ActivationFunctionType
AX = mybir.AxisListType
F32 = mybir.dt.float32
F32R = mybir.dt.float32r

P = 128
D = 1024
KD = D // P
T_LAT, T_CTX = 2048, 256
T_ALL = T_CTX + T_LAT
NT_CTX, NT_LAT = T_CTX // P, T_LAT // P
NT = NT_CTX + NT_LAT
ROW = 64
HEADS = 4
DH = 128
CH = 512
EPS = 1e-6
SLOT = 256
N_SLOTS = 18
TILE = 512

HID = 64
HALF_T = T_LAT // 2
MAGIC = 12582912.0
TWO_PI_A = 6.28125
TWO_PI_B = 2 * math.pi - TWO_PI_A
PI_DOWN = 3.1415925

N2 = 16
N1 = 192
N = N1 * N2
K1 = N1 // 2
NQ = K1 // 4


def sem_maker(nc, ctx):
    return lambda name: ctx.enter_context(nc.semaphore(name))


def mem_makers(nc, ctx):
    sb = lambda name, shape, dt=F32: ctx.enter_context(nc.sbuf_tensor(name, shape, dt))
    ps = lambda name, shape, dt=F32: ctx.enter_context(nc.psum_tensor(name, shape, dt))
    return sb, ps


def spread(src):
    return src.partition_broadcast(P)


def wait_count(engine, sem, g, per, const):
    if not isinstance(g, int):
        engine.wait_ge(sem, g * per + const)
    elif per * g + const > 0:
        engine.wait_ge(sem, per * g + const)


CTX_T = (0, T_CTX)
LAT_T = [(T_CTX + i * TILE, TILE) for i in range(T_LAT // TILE)]
GATE_TILES = 1 + len(LAT_T)
K_TILES, V_TILES, B_TILES, A_TILES = 20, 36, 16, 32
K0 = GATE_TILES
V0 = K0 + K_TILES
Q0 = V0 + V_TILES
O0 = Q0 + 4 * B_TILES
Z0 = O0 + 2 * A_TILES
N_TILES = Z0 + B_TILES
ROOT_D = float(math.sqrt(D))
X_ROWS = 6
N_MOD = 8


def project(nc, d, s, svec, hidden):
    with ExitStack() as ctx:
        sb, ps = mem_makers(nc, ctx)
        sem = sem_maker(nc, ctx)

        h_hi = sb("h_hi", [P, KD, T_ALL], F32R)
        h_lo = sb("h_lo", [P, KD, T_ALL], F32R)
        w_hi = sb("w_hi", [P, 2, KD, SLOT], F32R)
        w_lo = sb("w_lo", [P, 2, KD, SLOT], F32R)
        stage = sb("stage", [P, 3, KD, SLOT])
        work = sb("work", [P, 3 * D])
        ident = sb("ident", [P, P])
        cvec = sb("cvec", [P, KD, 2])
        bmod = sb("bmod", [P, 2 * KD])
        pgain = sb("pgain", [P, KD])
        mod = sb("mod", [P, 2 * KD, 2])
        gcol = sb("gcol", [P, KD, 2])
        modrow = [work[0:2, 2 * D + i * TILE:2 * D + (i + 1) * TILE] for i in range(2)]
        feats = sb("feats", [2 * 17, HALF_T])
        fw1 = sb("fw1", [2 * 17, P])
        fw2 = sb("fw2", [P, P])
        fcol = sb("fcol", [P, 4])
        gbias = sb("gbias", [P, 1])
        coef = sb("coef", [P, 20, 4])
        sumsq = sb("sumsq", [P, X_ROWS])
        rstd = sb("rstd", [P, X_ROWS])
        power = sb("power", [P, 2])
        raw = [work[:, i * TILE:(i + 1) * TILE] for i in range(2)]
        res = [work[:, (2 + i) * TILE:(3 + i) * TILE] for i in range(4)]
        whole = work[:, 0:2 * TILE]
        ht = [work[:, i * D:(i + 1) * D].rearrange("p (k t) -> p k t", k=KD) for i in range(3)]
        xrow = [stage[:, (i // 2 + 2) % 3, :, :].rearrange("p k n -> p (k n)")[:, i % 2 * D:(i % 2 + 1) * D]
                for i in range(X_ROWS)]

        bank = [ps(f"bank{i}", [P, TILE]) for i in range(6)]
        psM = ps("psM", [P, 2 * KD, 2])

        small_loaded = sem("small_loaded")
        mod_loaded = [sem(f"mod_loaded{i}") for i in range(3)]
        mod_used = sem("mod_used")
        svec_ready = sem("svec_ready")
        mod_rows = sem("mod_rows")
        mod_turned = sem("mod_turned")
        mod_step = sem("mod_step")
        x_loaded = [sem(f"x_loaded{i}") for i in range(X_ROWS)]
        ssq_ready = sem("ssq_ready")
        power_set = sem("power_set")
        eps_added = sem("eps_added")
        rstd_ready = sem("rstd_ready")
        xhat_ready = sem("xhat_ready")
        xt_ready = sem("xt_ready")
        ht_ready = sem("ht_ready")
        hi_ready = sem("hi_ready")
        lo_ready = sem("lo_ready")
        w_loaded = [sem(f"w_loaded{i}") for i in range(2)]
        w_hi_ready = sem("w_hi_ready")
        w_lo_ready = sem("w_lo_ready")
        tile_ready = sem("tile_ready")
        bank_free = sem("bank_free")
        raw_ready = sem("raw_ready")
        tap_first = sem("tap_first")
        tap_both = sem("tap_both")
        silu_done = sem("silu_done")
        stored = [sem(f"stored{i}") for i in range(4)]
        hid_in = sem("hid_in")
        hid_sum = sem("hid_sum")
        hid_step = [sem(f"hid_step{j}") for j in range(2)]
        hid_ready = sem("hid_ready")

        def ahead(i, j, by, last):
            return None if last and j + by >= X_ROWS else (i + (j + by) // X_ROWS, (j + by) % X_ROWS)

        block = ctx.enter_context(nc.Block())

        @block.sync
        def _(sp):
            for dst, src in ((cvec[:, :, :], d["cvec"]), (bmod[:, :], d["bmod"]), (pgain[:, :], d["pgain"]),
                             (gbias[:, :], d["gbias"]), (coef[:, :, :], d["coef"]), (ident[:, :], d["ident"])):
                sp.dma_start(dst, src).then_inc(small_loaded, 16)
            for c in range(N_MOD):
                if c >= 3:
                    sp.wait_ge(mod_used, c - 2)
                sp.dma_start(stage[:, c % 3, :, :], d["w_mod"][c]).then_inc(mod_loaded[c % 3], 16)
            def load_x(tile, j):
                src = d["x"][bass.ts(tile - NT_CTX, P), :] if j >= NT_CTX or not isinstance(tile, int) else \
                    d["ctx"][j * P:(j + 1) * P, :]
                sp.dma_start(xrow[j], src).then_inc(x_loaded[j], 16)

            for j in range(X_ROWS):
                sp.wait_ge(mod_used, N_MOD - 2 + j // 2)
                load_x(j, j)
            with sp.Fori(1, NT // X_ROWS) as i:
                for j in range(X_ROWS):
                    sp.wait_ge(xt_ready, i * X_ROWS + (j - X_ROWS + 1))
                    load_x(i * X_ROWS + j, j)

            sp.wait_ge(xt_ready, NT - 2)
            sp.dma_start(stage[:, 0, :, 0:P], d["w_gate"]).then_inc(w_loaded[0], 16)
            sp.wait_ge(xt_ready, NT)
            sp.dma_start(stage[:, 1, :, :], d["w_in"][0]).then_inc(w_loaded[1], 16)

            def load_after(item, par):
                sp.wait_ge(w_hi_ready, item + 1)
                sp.wait_ge(w_lo_ready, item + 1)
                sp.dma_start(stage[:, par, :, :], d["w_in"][item + 1]).then_inc(w_loaded[par], 16)

            def store(ready, count, dst, slot, width):
                sp.wait_ge(ready, count)
                sp.dma_start(dst, res[slot][:, 0:width]).then_inc(stored[slot], 16)

            load_after(0, 0)
            for n, (t0, width) in enumerate([CTX_T] + LAT_T):
                store(bank_free, n + 1, s["gates"][:, t0:t0 + width], n % 4, width)
            n = 0
            for half in range(2):
                load_after(1 + half, (1 + half) % 2)
                for b in range(2):
                    for t0, width in [CTX_T] + LAT_T:
                        store(silu_done, n + 1, s["k"][2 * half + b, :, t0:t0 + width], (K0 + n) % 4, width)
                        n += 1
            n = V0
            for half in range(2):
                load_after(3 + half, (3 + half) % 2)
                for t in range(NT):
                    store(bank_free, n + 1, s["v"][t, :, half * SLOT:(half + 1) * SLOT], n % 4, SLOT)
                    n += 1
            for dst, src in ((feats[:, :], d["feats"]), (fw1[:, :], d["fw1"]), (fw2[:, :], d["fw2"]),
                             (fcol[:, :], d["fcol"])):
                sp.dma_start(dst, src).then_inc(hid_in, 16)
            for half in range(2):
                load_after(5 + half, (5 + half) % 2)
                for m in range(8):
                    b, j = divmod(m, 4)
                    m += 8 * half
                    store(silu_done, K_TILES + m + 1, s["qhy"][2 * half + b, :, j * TILE:(j + 1) * TILE],
                          (Q0 + m) % 4, TILE)
            with sp.Fori(0, 3) as g:
                for half in range(2):
                    load_after(2 * g + (7 + half), (7 + half) % 2)
                    for m in range(8):
                        b, j = divmod(m, 4)
                        m += 8 * half
                        store(tap_both, B_TILES * g + (K_TILES + B_TILES + m + 1),
                              s["qhy"][4 * g + (4 + 2 * half + b), :, j * TILE:(j + 1) * TILE],
                              (Q0 + m) % 4, TILE)
            with sp.Fori(0, 2) as g:
                for half in range(2):
                    load_after(2 * g + (13 + half), (13 + half) % 2)
                    for t in range(NT_LAT):
                        m = half * NT_LAT + t
                        store(bank_free, A_TILES * g + (O0 + m + 1),
                              s["ozh"][g, t, :, half * SLOT:(half + 1) * SLOT], (O0 + m) % 4, SLOT)
            for m in range(B_TILES):
                store(bank_free, Z0 + m + 1, s["zh"][m // 4, :, m % 4 * TILE:(m % 4 + 1) * TILE],
                      (Z0 + m) % 4, TILE)
            for slot in range(4):
                sp.wait_ge(stored[slot], 16 * len(range(slot, N_TILES, 4)))

        @block.tensor
        def _(pe):
            pe.wait_ge(svec_ready, 1)
            for c in range(N_MOD):
                pe.wait_ge(mod_loaded[c % 3], 16 * (c // 3 + 1))
                for k in range(KD):
                    mm = pe.matmul(bank[c // 2][0:2, c % 2 * SLOT:(c % 2 + 1) * SLOT], svec[:, k, :],
                                   stage[:, c % 3, k, :], start=(k == 0), stop=(k == KD - 1))
                mm.then_inc(mod_used, 1)
            pe.wait_ge(small_loaded, 16 * 6)
            for m in range(2 * KD):
                if m % 4 == 0:
                    pe.wait_ge(mod_rows, m // 4 + 1)
                mm = pe.transpose(psM[:, m, :], modrow[m // 4 % 2][:, m % 4 * P:(m % 4 + 1) * P], ident[0:2, 0:2])
                if m % 4 == 3:
                    mm.then_inc(mod_turned, 1)

            def turn(i, j):
                pe.wait_ge(xhat_ready, i * X_ROWS + (j + 1))
                wait_count(pe, ht_ready, i, X_ROWS, j - 2)
                for k in range(KD):
                    mm = pe.transpose(bank[2 * (j % 3) + k // 4][:, (k % 4) * P:(k % 4 + 1) * P],
                                      xrow[j][:, k * P:(k + 1) * P], ident[:, :])
                mm.then_inc(xt_ready, 1)

            for j in range(X_ROWS):
                turn(0, j)
            with pe.Fori(1, NT // X_ROWS) as i:
                for j in range(X_ROWS):
                    turn(i, j)

            def three_passes(out, lhs, rhs, k):
                pe.matmul(out, lhs[0], rhs[0], start=(k == 0), stop=False)
                pe.matmul(out, lhs[0], rhs[1], start=False, stop=False)
                return pe.matmul(out, lhs[1], rhs[0], start=False, stop=(k == KD - 1))

            def channels_tile(slot, par, c0, t0, width):
                for k in range(KD):
                    mm = three_passes(bank[slot][:, 0:width],
                                      [w[:, par, k, c0:c0 + P] for w in (w_hi, w_lo)],
                                      [h[:, k, t0:t0 + width] for h in (h_hi, h_lo)], k)
                mm.then_inc(tile_ready, 1)

            def tokens_tile(slot, par, tokens):
                for k in range(KD):
                    mm = three_passes(bank[slot][:, 0:SLOT], [h[:, k, tokens] for h in (h_hi, h_lo)],
                                      [w[:, par, k, :] for w in (w_hi, w_lo)], k)
                mm.then_inc(tile_ready, 1)

            def weights(item):
                pe.wait_ge(w_hi_ready, item + 1)
                pe.wait_ge(w_lo_ready, item + 1)

            pe.wait_ge(ht_ready, NT)
            weights(0)
            n = 0
            for t0, width in [CTX_T] + LAT_T:
                if n >= 4:
                    pe.wait_ge(bank_free, n - 3)
                pe.wait_ge(lo_ready, (t0 + width) // P)
                channels_tile(n % 4, 0, 0, t0, width)
                n += 1
            for half in range(2):
                weights(1 + half)
                for b in range(2):
                    for t0, width in [CTX_T] + LAT_T:
                        pe.wait_ge(bank_free, n - 3)
                        channels_tile(n % 4, (1 + half) % 2, b * P, t0, width)
                        n += 1
            for half in range(2):
                weights(3 + half)
                for t in range(NT):
                    pe.wait_ge(bank_free, n - 3)
                    tokens_tile(n % 4, (3 + half) % 2, slice(t * P, (t + 1) * P))
                    n += 1
            with pe.Fori(0, 4) as g:
                for half in range(2):
                    weights(2 * g + (5 + half))
                    for m in range(8):
                        b, j = divmod(m, 4)
                        m += 8 * half
                        pe.wait_ge(bank_free, B_TILES * g + (Q0 + m - 3))
                        channels_tile((Q0 + m) % 4, (5 + half) % 2, b * P, *LAT_T[j])
            def hidden_sums(layer):
                for j in range(2):
                    cut = slice(j * TILE, (j + 1) * TILE)
                    w, src = (fw2[:, :], hidden[:, cut]) if layer else (fw1[:, :], feats[:, cut])
                    pe.matmul(bank[4 + j][:, :], w, src, start=True, stop=True).then_inc(hid_sum, 1)

            pe.wait_ge(hid_in, 64)
            hidden_sums(0)
            with pe.Fori(0, 2) as g:
                for half in range(2):
                    weights(2 * g + (13 + half))
                    for t in range(NT_LAT):
                        m = half * NT_LAT + t
                        pe.wait_ge(bank_free, A_TILES * g + (O0 + m - 3))
                        tokens_tile((O0 + m) % 4, (13 + half) % 2,
                                    slice(T_CTX + t * P, T_CTX + (t + 1) * P))
            pe.wait_ge(hid_ready, 2)
            hidden_sums(1)
            for half in range(2):
                weights(17 + half)
                for m in range(8):
                    b, j = divmod(m, 4)
                    m += 8 * half
                    pe.wait_ge(bank_free, Z0 + m - 3)
                    channels_tile((Z0 + m) % 4, (17 + half) % 2, b * P, *LAT_T[j])

        @block.scalar
        def _(act):
            act.wait_ge(small_loaded, 16 * 6)
            act.activation(svec[:, :, :], cvec[:, :, :], ACT.Silu).then_inc(svec_ready, 1)

            def square(i, j):
                act.wait_ge(x_loaded[j], 16 * i + 16)
                wait_count(act, rstd_ready, i, X_ROWS, j - X_ROWS + 1)
                act.activation(h_lo[:, :, bass.ts(i * X_ROWS + j, P)], xrow[j].rearrange("p (k t) -> p k t", k=KD),
                               ACT.Square, accum_out=sumsq[:, j:j + 1]).then_inc(ssq_ready, 1)

            def high(i, j):
                act.wait_ge(ht_ready, i * X_ROWS + (j + 1))
                act.copy(h_hi[:, :, bass.ts(i * X_ROWS + j, P)], ht[j % 3]).then_inc(hi_ready, 1)

            def turns(i, last=False):
                for j in range(X_ROWS):
                    for by, stage_of in ((0, high), (3, square)):
                        tile = ahead(i, j, by, last)
                        if tile:
                            stage_of(*tile)

            for j in range(3):
                square(0, j)
            for c in range(4):
                act.wait_ge(mod_used, 2 * c + 2)
                if c >= 2:
                    act.wait_ge(mod_turned, c - 1)
                act.copy(modrow[c % 2], bank[c][0:2, :]).then_inc(mod_rows, 1)
            turns(0)
            with act.Fori(1, NT // X_ROWS - 1) as i:
                turns(i)
            turns(NT // X_ROWS - 1, True)

            def split(item, par, loads, done_tiles, width=SLOT):
                act.wait_ge(w_loaded[par], 16 * loads)
                if done_tiles is not None:
                    act.wait_ge(tile_ready, done_tiles)
                act.copy(w_hi[:, par, :, 0:width], stage[:, par, :, 0:width]).then_inc(w_hi_ready, 1)

            def begin(n, slot, turn):
                act.wait_ge(tile_ready, n + 1)
                if not (isinstance(turn, int) and turn == 0):
                    act.wait_ge(stored[slot], 16 * turn)

            def plain(n, slot, turn, width, func, bias=0.0):
                begin(n, slot, turn)
                act.activation(res[slot][:, 0:width], bank[slot][:, 0:width], func, bias=bias)\
                   .then_inc(bank_free, 1)

            def conv_tile(n, slot, turn, c, r, width, blk, silu):
                begin(n, slot, turn)
                if not (isinstance(c, int) and c < 2):
                    act.wait_ge(tap_both, c - 1)
                act.copy(raw[r][:, 0:width], bank[slot][:, 0:width]).then_inc(raw_ready, 1)
                w_mid, bias = [coef[:, bass.ds(blk, 1), k:k + 1].rearrange("p a b -> p (a b)") for k in (1, 3)]
                act.activation(res[slot][:, 0:width], bank[slot][:, 0:width], ACT.Identity,
                               bias=bias, scale=w_mid).then_inc(bank_free, 1)
                if silu:
                    act.wait_ge(tap_both, c + 1)
                    act.activation(res[slot][:, 0:width], res[slot][:, 0:width], ACT.Silu)\
                       .then_inc(silu_done, 1)

            split(0, 0, 1, None, P)
            split(1, 1, 1, None)
            act.wait_ge(lo_ready, NT)
            for n, (t0, width) in enumerate([CTX_T] + LAT_T):
                plain(n, n % 4, n // 4, width, ACT.Identity, gbias[:, 0:1])
            n, c = K0, 0
            for half in range(2):
                split(2 + half, half, 2, K0 + half * K_TILES // 2)
                for b in range(2):
                    for t0, width in [CTX_T] + LAT_T:
                        conv_tile(n, n % 4, n // 4, c, c % 2, width, 2 * half + b, True)
                        n, c = n + 1, c + 1
            for half in range(2):
                split(4 + half, half, 3, V0 + half * V_TILES // 2)
                for t in range(NT):
                    plain(n, n % 4, n // 4, SLOT, ACT.Copy)
                    n += 1
            for half in range(2):
                split(6 + half, half, 4, Q0 + half * B_TILES // 2)
                for m in range(8 * half, 8 * half + 8):
                    conv_tile(n, n % 4, n // 4, K_TILES + m, m % 2, TILE, 4 + 2 * half + m // 4 % 2, True)
                    n += 1
            with act.Fori(0, 3) as g:
                for half in range(2):
                    split(None, half, g + 5, B_TILES * g + (Q0 + B_TILES + half * B_TILES // 2))
                    for m in range(8 * half, 8 * half + 8):
                        conv_tile(B_TILES * g + (n + m), (n + m) % 4, 4 * g + (n + m) // 4,
                                  B_TILES * g + (K_TILES + B_TILES + m), m % 2, TILE,
                                  4 * g + (8 + m // 4), False)
            def sines(layer):
                for j in range(2):
                    cut = slice(j * TILE, (j + 1) * TILE)
                    act.wait_ge(hid_step[j], 6 * (layer + 1))
                    act.activation(hidden[:, cut], hidden[:, cut], ACT.Sin).then_inc(hid_ready, 1)

            n = O0
            for g, func in enumerate((ACT.Sigmoid, ACT.Silu, ACT.Silu)):
                for half in range(2):
                    if (g, half) != (2, 1):
                        split(None, half, g + 8, n)
                    for t in range(8 if g == 2 else NT_LAT):
                        plain(n, n % 4, n // 4, TILE if g == 2 else SLOT, func)
                        n += 1
                    if half == 0 and g != 1:
                        sines(g // 2)

        @block.gpsimd
        def _(pool):
            def root(i, j):
                pool.wait_ge(ssq_ready, i * X_ROWS + (j + 1))
                wait_count(pool, xhat_ready, i, X_ROWS, j - X_ROWS + 1)
                pool.tensor_tensor(rstd[:, j:j + 1], sumsq[:, j:j + 1], power[:, 1:2], ALU.add)\
                    .then_inc(eps_added, 1)
                pool.wait_ge(eps_added, i * X_ROWS + (j + 1))
                pool.tensor_tensor(rstd[:, j:j + 1], rstd[:, j:j + 1], power[:, 0:1], ALU.pow)\
                    .then_inc(rstd_ready, 1)

            def low(i, j):
                tokens = bass.ts(i * X_ROWS + j, P)
                pool.wait_ge(hi_ready, i * X_ROWS + (j + 1))
                pool.tensor_tensor(h_lo[:, :, tokens], ht[j % 3], h_hi[:, :, tokens].bitcast(F32), ALU.subtract)\
                    .then_inc(lo_ready, 1)

            def turns(i, last=False):
                for j in range(X_ROWS):
                    if j + 3 < X_ROWS or not last:
                        root(i + (j + 3) // X_ROWS, (j + 3) % X_ROWS)
                    low(i, j)

            pool.memset(power[:, 0:1], -0.5).then_inc(power_set, 1)
            pool.memset(power[:, 1:2], D * EPS).then_inc(power_set, 1)
            pool.wait_ge(power_set, 2)
            for j in range(3):
                root(0, j)
            turns(0)
            with pool.Fori(1, NT // X_ROWS - 1) as i:
                turns(i)
            turns(NT // X_ROWS - 1, True)

        @block.vector
        def _(dve):
            dve.wait_ge(small_loaded, 16 * 6)
            dve.wait_ge(mod_turned, 4)
            for col in range(2):
                ins = dve.tensor_tensor(mod[:, :, col], psM[:, :, col], bmod[:, :], ALU.add)
            ins.then_inc(mod_step, 1)
            dve.wait_ge(mod_step, 1)
            for col in range(2):
                ins = dve.scalar_tensor_tensor(gcol[:, :, col], mod[:, KD:2 * KD, col], 1.0, pgain[:, :],
                                               ALU.add, ALU.mult)
            ins.then_inc(mod_step, 1)
            dve.wait_ge(mod_step, 2)
            dve.tensor_scalar(gcol[:, :, :], gcol[:, :, :], ROOT_D, None, ALU.mult).then_inc(mod_step, 1)
            dve.wait_ge(mod_step, 3)

            def normalise(i, j):
                dve.wait_ge(rstd_ready, i * X_ROWS + (j + 1))
                dve.tensor_scalar(xrow[j], xrow[j], rstd[:, j:j + 1], None, ALU.mult).then_inc(xhat_ready, 1)

            def modulate(i, j, stream):
                dve.wait_ge(xt_ready, i * X_ROWS + (j + 1))
                wait_count(dve, lo_ready, i, X_ROWS, j - 2)
                for k in range(KD):
                    ins = dve.tensor_scalar(ht[j % 3][:, k, :],
                                            bank[2 * (j % 3) + k // 4][:, (k % 4) * P:(k % 4 + 1) * P],
                                            gcol[:, k, stream:stream + 1], mod[:, k, stream:stream + 1],
                                            ALU.mult, ALU.add)
                ins.then_inc(ht_ready, 1)

            def tiles(i, streams, last=False):
                for j in range(X_ROWS):
                    modulate(i, j, streams[j])
                    tile = ahead(i, j, 2, last)
                    if tile:
                        normalise(*tile)

            for j in range(2):
                normalise(0, j)
            tiles(0, [1] * NT_CTX + [0] * (X_ROWS - NT_CTX))
            with dve.Fori(1, NT // X_ROWS - 1) as i:
                tiles(i, [0] * X_ROWS)
            tiles(NT // X_ROWS - 1, [0] * X_ROWS, True)

            def split(item, par, done_tiles, width=SLOT):
                dve.wait_ge(w_hi_ready, item + 1)
                if done_tiles is not None:
                    dve.wait_ge(tile_ready, done_tiles)
                dve.tensor_tensor(w_lo[:, par, :, 0:width], stage[:, par, :, 0:width],
                                  w_hi[:, par, :, 0:width].bitcast(F32), ALU.subtract).then_inc(w_lo_ready, 1)

            def taps(n, slot, c, r, width, blk, rows):
                dve.wait_ge(raw_ready, c + 1)
                dve.wait_ge(bank_free, n + 1)
                u = raw[r][:, 0:width].rearrange("p (a b) -> p a b", a=rows)
                y = res[slot][:, 0:width].rearrange("p (a b) -> p a b", a=rows)
                e = width // rows
                w_left, w_right = [coef[:, bass.ds(blk, 1), k:k + 1].rearrange("p a b -> p (a b)") for k in (0, 2)]
                dve.scalar_tensor_tensor(y[:, :, 1:e], u[:, :, 0:e - 1], w_left, y[:, :, 1:e],
                                         ALU.mult, ALU.add).then_inc(tap_first, 1)
                dve.wait_ge(tap_first, c + 1)
                dve.scalar_tensor_tensor(y[:, :, 0:e - 1], u[:, :, 1:e], w_right, y[:, :, 0:e - 1],
                                         ALU.mult, ALU.add).then_inc(tap_both, 1)

            split(0, 0, None, P)
            split(1, 1, None)
            n, c = K0, 0
            for half in range(2):
                split(2 + half, half, K0 + half * K_TILES // 2)
                for b in range(2):
                    for t0, width in [CTX_T] + LAT_T:
                        taps(n, n % 4, c, c % 2, width, 2 * half + b, 1 if width == T_CTX else TILE // ROW)
                        n, c = n + 1, c + 1
            for half in range(2):
                split(4 + half, half, V0 + half * V_TILES // 2)
            with dve.Fori(0, 4) as g:
                for half in range(2):
                    split(2 * g + (6 + half), half, B_TILES * g + (Q0 + half * B_TILES // 2))
                    for m in range(8 * half, 8 * half + 8):
                        taps(B_TILES * g + (Q0 + m), (Q0 + m) % 4, B_TILES * g + (K_TILES + m), m % 2, TILE,
                             4 * g + (4 + m // 4), TILE // ROW)

            def reduced(layer):
                for step in range(6):
                    for j in range(2):
                        cut = slice(j * TILE, (j + 1) * TILE)
                        a, k = hidden[:, cut], whole[:, cut]
                        if step:
                            dve.wait_ge(hid_step[j], 6 * layer + step)
                        else:
                            dve.wait_ge(hid_sum, 2 * layer + j + 1)
                            ins = dve.tensor_scalar(a, bank[4 + j][:, :], fcol[:, 2 * layer:2 * layer + 1],
                                                    fcol[:, 2 * layer + 1:2 * layer + 2], ALU.add, ALU.mult)
                        if step == 1:
                            ins = dve.tensor_scalar(k, a, 1.0 / (2 * math.pi), MAGIC, ALU.mult, ALU.add)
                        elif step == 2:
                            ins = dve.tensor_scalar(k, k, -MAGIC, None, ALU.add)
                        elif step in (3, 4):
                            ins = dve.scalar_tensor_tensor(a, k, -(TWO_PI_A, TWO_PI_B)[step - 3], a, ALU.mult, ALU.add)
                        elif step == 5:
                            ins = dve.tensor_scalar(a, a, PI_DOWN, -PI_DOWN, ALU.min, ALU.max)
                        ins.then_inc(hid_step[j], 1)

            for i in range(5):
                split(14 + i, i % 2, O0 + i * A_TILES // 2)
                if i % 4 == 0:
                    reduced(i // 4)


HC = HEADS * NT
CTX_STEPS = 2 * NT_CTX
V1 = DH + 1


def mlstm(nc, d, s, svec, wo_hi, wo_lo, gate):
    with ExitStack() as ctx:
        sb, ps = mem_makers(nc, ctx)
        sem = sem_maker(nc, ctx)

        ipre = sb("ipre", [HC, 2, P])
        fpre = sb("fpre", [HC, 2, P])
        logf = sb("logf", [HC, 2, P])
        ones = sb("ones", [HC, P])
        bsum = sb("bsum", [HC, 2, P])
        arow = sb("arow", [HC, 2, P])
        mrow = sb("mrow", [HC, 2, P])
        wsrow = sb("wsrow", [HC, 2, P])
        emrow = sb("emrow", [HC, 2, P])
        mprev = sb("mprev", [HC, 2])
        mlast = sb("mlast", [HC, 2])
        nmlast = sb("nmlast", [HC, 2])
        wcol = sb("wcol", [HC, 2])
        logroot = sb("logroot", [HC, 1])
        chain = sb("chain", [HEADS, 2, 2, NT])
        carry = sb("carry", [HEADS, 2, NT])
        mp = sb("mp", [HEADS, 2, NT])
        ident = sb("ident_m", [P, P])
        mask = sb("mask", [P, 2, P])
        gain = sb("gain", [P, CH])
        cols = sb("cols", [P, 2, 3, HC])
        mpb = sb("mpb", [P, 2, HC])
        wc = sb("wc", [P, 2, HC])

        qT = sb("qT", [P, 4, HEADS, P])
        kT = sb("kT", [P, 4, HEADS, P])
        v1 = sb("v1", [P, 4, HEADS, V1])
        mb = sb("mb", [P, 4, HEADS, P])
        wib = sb("wib", [P, 4, HEADS, P])
        E = sb("E", [P, 2, HEADS, P])
        pm = sb("pm", [P, 2, HEADS, P])
        kw = sb("kw", [P, 2, HEADS, P])
        C = sb("C", [P, 2, HEADS, V1])
        den = sb("den", [P, 2, HEADS])
        h = sb("h", [P, 4, HEADS, P])
        other = sb("other", [P, 4, HEADS, P])
        og = sb("og", [P, 4, HEADS, P])
        zg = sb("zg", [P, 4, HEADS, P])
        sq = sb("sq", [P, 2, HEADS, P])
        ssq = sb("ssq", [P, 4, HEADS])
        rinv = sb("rinv", [P, 4, HEADS])
        power = sb("power_m", [P, 2, HEADS])
        yT = sb("yT", [P, 2, HEADS, P])

        stage = sb("stage_o", [P, KD, D])
        sfull = sb("sfull", [P, KD, P])
        bgate, post = [other[:, i:i + 2].rearrange("p j h v -> p (j h v)") for i in (0, 2)]

        psK = ps("psK", [P, HEADS, P])
        psY = ps("psY", [P, HEADS, P])
        psS = [ps(f"psS{i}", [P, HEADS, P]) for i in range(2)]
        psN = ps("psN", [P, 2, 512])[:, :, 0:2 * V1].rearrange("p a (b v) -> p a b v", b=2)
        psU = ps("psU", [P, 2, 512])[:, :, 0:2 * V1].rearrange("p a (b v) -> p a b v", b=2)

        gate_cols_in = sem("gate_cols_in")
        gate_rows_in = sem("gate_rows_in")
        wo_in = sem("wo_in")
        s_spread = sem("s_spread")
        gate_sum = sem("gate_sum")
        gate_step = sem("gate_step")
        wo_high = sem("wo_high")
        wo_low = sem("wo_low")
        rows_in = sem("rows_in")
        act_row = sem("act_row")
        dve_row = sem("dve_row")
        ends_out = sem("ends_out")
        ends_in = sem("ends_in")
        mprev_out = sem("mprev_out")
        mprev_in = sem("mprev_in")
        rows_out = sem("rows_out")
        wc_in = sem("wc_in")
        mpb_in = sem("mpb_in")
        turned = sem("turned")
        cols_ready = sem("cols_ready")
        const_in = sem("const_in")
        const_set = sem("const_set")
        step_in = [sem(f"step_in{i}") for i in range(4)]
        masked = sem("masked")
        wi_ready = sem("wi_ready")
        q_scaled = sem("q_scaled")
        e_ready = sem("e_ready")
        k_turned = sem("k_turned")
        kw_ready = sem("kw_ready")
        s_ready = sem("s_ready")
        p_ready = sem("p_ready")
        num_ready = sem("num_ready")
        den_neg = sem("den_neg")
        den_max = sem("den_max")
        den_inv = sem("den_inv")
        h_ready = sem("h_ready")
        u_ready = sem("u_ready")
        c_ready = sem("c_ready")
        h_out = [sem(f"h_out{i}") for i in range(4)]
        fin_in = [sem(f"fin_in{i}") for i in range(4)]
        gated = sem("gated")
        y_scaled = sem("y_scaled")
        gain_ready = sem("gain_ready")
        ssq_ready = sem("ssq_ready_m")
        guard_added = sem("guard_added")
        rinv_ready = sem("rinv_ready")
        y_ready = sem("y_ready")
        y_turned = sem("y_turned")
        yT_ready = sem("yT_ready")
        y_out = [sem(f"y_out{i}") for i in range(2)]

        CTX = [(0, 0), (1, 1), (0, 1), (1, 0)]
        LOOP = 4
        HALF = NT_LAT // 4

        def chunk_of(it, j):
            i = 2 * it + j // 2
            return i if j % 2 == 0 else i * -1 + (NT_LAT - 1)

        DONE = LOOP * HALF

        def first_body(it):
            return isinstance(it, int) and it == 0

        def earlier(it, j, lag):
            if isinstance(it, int):
                n = LOOP * it + j - lag
                return None if n < DONE or n >= 2 * DONE else divmod(n, LOOP)
            return (it, j - lag) if j >= lag else (it + -1, j - lag + LOOP)

        block = ctx.enter_context(nc.Block())

        @block.sync
        def _(sp):
            for dr in range(2):
                for dst, kind in ((ipre, 0), (fpre, 1)):
                    r0 = 32 * (2 * dr + kind)
                    sp.dma_start(dst[:, dr, :], s["gates"][r0:r0 + HEADS, :].rearrange("h (c t) -> (h c) t", t=P))\
                      .then_inc(rows_in, 16)
            sp.dma_start(ident[:, :], d["ident"]).then_inc(const_in, 16)
            sp.dma_start(mask[:, :, :], d["mask"]).then_inc(const_in, 16)
            sp.dma_start(gain[:, :], spread(d["mh_gain"][0])).then_inc(const_in, 16)

            def load_kv(slot, dr, c):
                sp.dma_start(kT[:, slot, :, :], s["k"][:, :, bass.ts(c, P)].rearrange("h p t -> p h t"))\
                  .then_inc(step_in[slot], 16)
                sp.dma_start(v1[:, slot, :, 0:DH], s["v"][c].rearrange("p (h v) -> p h v", h=HEADS))\
                  .then_inc(step_in[slot], 16)

            sp.wait_ge(const_set, 1)
            for j, (dr, c) in enumerate(CTX):
                load_kv(j, dr, c)

            sp.wait_ge(dve_row, 6)
            for dr in range(2):
                end = P - 1 if dr == 0 else 0
                sp.dma_start(s["small"][dr, 0], bsum[:, dr, end:end + 1]).then_inc(ends_out, 16)
                sp.dma_start(s["small"][dr, 1], mrow[:, dr, end:end + 1]).then_inc(ends_out, 16)
            sp.wait_ge(ends_out, 64)
            for dr in range(2):
                sp.dma_start(chain[:, dr, :, :], s["small"][dr, 0:2].rearrange("w (h c) -> h w c", h=HEADS))\
                  .then_inc(ends_in, 16)
            sp.wait_ge(dve_row, 10)
            for dr in range(2):
                sp.dma_start(s["small"][dr, 2].rearrange("(h c) -> h c", h=HEADS), mp[:, dr, :])\
                  .then_inc(mprev_out, 16)
            sp.wait_ge(mprev_out, 32)
            for dr in range(2):
                sp.dma_start(mprev[:, dr:dr + 1], s["small"][dr, 2]).then_inc(mprev_in, 16)
            sp.wait_ge(dve_row, 13)
            sp.wait_ge(act_row, 6)
            for dr in range(2):
                sp.dma_start(s["rows"][dr], mrow[:, dr, :]).then_inc(rows_out, 16)
                sp.dma_start(s["small"][dr, 3], wcol[:, dr:dr + 1]).then_inc(rows_out, 16)
            sp.wait_ge(rows_out, 64)
            for dr in range(2):
                sp.dma_start(mpb[:, dr, :], spread(s["small"][dr, 2])).then_inc(mpb_in, 16)
                sp.dma_start(wc[:, dr, :], spread(s["small"][dr, 3])).then_inc(wc_in, 16)

            def load_step(it, j):
                dr, t = j % 2, chunk_of(it, j)
                sp.dma_start(qT[:, j, :, :], s["qhy"][0:HEADS, :, bass.ts(t, P)].rearrange("h p t -> p h t"))\
                  .then_inc(step_in[j], 16)
                load_kv(j, dr, t + NT_CTX)
                src = s["rows"][dr].rearrange("(h c) t -> c h t", h=HEADS)
                sp.dma_start(mb[:, j, :, :], spread(src[bass.ds(t + NT_CTX, 1)].rearrange("c h t -> (c h) t")))\
                  .then_inc(step_in[j], 16)

            for j in range(LOOP):
                sp.wait_ge(u_ready, j + 1)
                load_step(0, j)

            def ahead(it, j):
                sp.wait_ge(u_ready, LOOP * it + (CTX_STEPS + j + 1))
                load_step(it + 1, j)

            gate_cols = d["w_mod"][2 * D // SLOT:3 * D // SLOT].rearrange("j p k n -> p k j n")
            for k in range(KD):
                sp.dma_start(stage[:, k, :].rearrange("p (j n) -> p j n", n=SLOT), gate_cols[:, k])\
                  .then_inc(gate_cols_in, 16)
            sp.dma_start(bgate, spread(d["bgate"][0])).then_inc(gate_rows_in, 16)
            sp.dma_start(post, spread(d["post"][0])).then_inc(gate_rows_in, 16)

            def first_half(it):
                for j in range(LOOP):
                    sp.wait_ge(h_ready, LOOP * it + (j + 1))
                    sp.dma_start(s["hf"][chunk_of(it, j)], h[:, j, :, :]).then_inc(h_out[j], 16)
                    ahead(it, j)

            first_half(0)
            sp.wait_ge(gate_sum, 2)
            sp.dma_start(stage[:, :, :], d["w_out"]).then_inc(wo_in, 16)
            with sp.Fori(1, HALF) as it:
                first_half(it)
            for j in range(LOOP):
                sp.wait_ge(h_out[j], 16 * HALF)

            def load_fin(it, j):
                tile = chunk_of(it, j)
                for dst, src in ((other, s["hf"][tile]), (og, s["ozh"][0, tile]), (zg, s["ozh"][1, tile])):
                    sp.dma_start(dst[:, j, :, :].rearrange("p h v -> p (h v)"), src).then_inc(fin_in[j], 16)

            def store_y(it, j):
                wait_count(sp, yT_ready, it, LOOP, j + 1 - DONE)
                sp.dma_start(s["y"][0:HEADS, :, bass.ts(chunk_of(it, j), P)].rearrange("h p t -> p h t"),
                             yT[:, j % 2, :, :]).then_inc(y_out[j % 2], 16)

            def turn(it, j, last=False):
                if not last:
                    ahead(it, j)
                back = earlier(it, j, 2)
                if back and not (last and j >= 2):
                    wait_count(sp, y_ready, back[0], LOOP, back[1] + 1 - DONE)
                    load_fin(*((it, j + 2) if j < 2 else (it + 1, j - 2)))
                back = earlier(it, j, LOOP)
                if back:
                    store_y(*back)

            for j in range(LOOP):
                load_fin(HALF, j)
            for j in range(LOOP):
                turn(HALF, j)
            with sp.Fori(HALF + 1, 2 * HALF - 1) as it:
                for j in range(LOOP):
                    turn(it, j)
            for j in range(LOOP):
                turn(2 * HALF - 1, j, True)
            for j in range(LOOP):
                store_y(2 * HALF - 1, j)
            for j in range(2):
                sp.wait_ge(y_out[j], 16 * 2 * HALF)

        @block.gpsimd
        def _(pool):
            pool.memset(v1[:, :, :, DH:V1], 1.0).then_inc(const_set, 1)
            pool.memset(C[:, :, :, :], 0.0).then_inc(const_set, 1)
            pool.memset(power[:, 0, :], -0.5).then_inc(const_set, 1)
            pool.memset(power[:, 1, :], DH * EPS).then_inc(const_set, 1)
            pool.memset(ones[:, :], 1.0).then_inc(const_set, 1)
            pool.memset(logroot[:, :], 0.5 * math.log(DH)).then_inc(const_set, 1)
            pool.wait_ge(const_set, 6)
            pool.wait_ge(const_in, 48)

            def prepare(it, j):
                wait_count(pool, p_ready, it, LOOP, j - 1)
                pool.wait_ge(step_in[j], 64 * it + (32 + 64))
                pool.tensor_tensor(E[:, j % 2, :, :], mb[:, j, :, :],
                                   mask[:, j % 2:j % 2 + 1, :].to_broadcast([P, HEADS, P]), ALU.add)\
                    .then_inc(masked, 1)
                wait_count(pool, wi_ready, it, LOOP, j + 1)
                pool.tensor_tensor(wib[:, j, :, :], wib[:, j, :, :], qT[:, j, :, :], ALU.mult)\
                    .then_inc(q_scaled, 1)

            def gate(it, j):
                wait_count(pool, fin_in[j], it, 48, 48 * (1 - HALF))
                wait_count(pool, h_ready, it, LOOP, j + 1)
                pool.tensor_tensor(og[:, j, :, :], h[:, j, :, :], og[:, j, :, :], ALU.mult).then_inc(gated, 1)

            def root(it, j):
                wait_count(pool, ssq_ready, it, LOOP, j + 1 - DONE)
                pool.tensor_tensor(rinv[:, j, :], ssq[:, j, :], power[:, 1, :], ALU.add).then_inc(guard_added, 1)
                wait_count(pool, guard_added, it, LOOP, j + 1 - DONE)
                pool.tensor_tensor(rinv[:, j, :], rinv[:, j, :], power[:, 0, :], ALU.pow).then_inc(rinv_ready, 1)

            def turn(it, j, last=False):
                if j < 2:
                    prepare(it, j + 2)
                elif not last:
                    prepare(it + 1, j - 2)
                gate(it, j)
                back = earlier(it, j, 1)
                if back:
                    root(*back)

            for j in range(LOOP):
                prepare(0, j)
            with pool.Fori(1, HALF) as it:
                for j in range(LOOP):
                    prepare(it, j)
            for j in range(2):
                prepare(HALF, j)
            for j in range(LOOP):
                turn(HALF, j)
            with pool.Fori(HALF + 1, 2 * HALF - 1) as it:
                for j in range(LOOP):
                    turn(it, j)
            for j in range(LOOP):
                turn(2 * HALF - 1, j, True)
            root(2 * HALF - 1, LOOP - 1)

        @block.tensor
        def _(pe):
            pe.wait_ge(const_in, 48)

            def turn_k(slot, step, loads, first=False):
                pe.wait_ge(step_in[slot], loads)
                if not first:
                    pe.wait_ge(kw_ready, step)
                for hd in range(HEADS):
                    mm = pe.transpose(psK[:, hd, :], kT[:, slot, hd, :], ident[:, :])
                mm.then_inc(k_turned, 1)

            def state(slot, dr, step, first=False):
                pe.wait_ge(kw_ready, step + 1)
                if not first:
                    pe.wait_ge(c_ready, step)
                for hd in range(HEADS):
                    mm = pe.matmul(psU[:, hd // 2, hd % 2, :], kw[:, dr, hd, :], v1[:, slot, hd, :],
                                   start=True, stop=True)
                mm.then_inc(u_ready, 1)

            pe.wait_ge(act_row, 6)
            for dr in range(2):
                for w, row in enumerate((arow, wsrow, emrow)):
                    mm = pe.transpose(psN[:, dr, :, :].rearrange("p a b -> p (a b)")[:, w * HC:(w + 1) * HC],
                                      row[:, dr, :], ident[0:HC, 0:HC])
                mm.then_inc(turned, 1)

            for j, (dr, c) in enumerate(CTX):
                turn_k(j, j, 32, j == 0)
                state(j, dr, j, j == 0)

            def scores(it, j):
                if j >= 2 or not first_body(it):
                    pe.wait_ge(p_ready, LOOP * it + (j - 1))
                for hd in range(HEADS):
                    mm = pe.matmul(psS[j % 2][:, hd, :], kT[:, j, hd, :], qT[:, j, hd, :], start=True, stop=True)
                mm.then_inc(s_ready, 1)

            def numerators(it, j):
                n = LOOP * it + j
                pe.wait_ge(p_ready, n + 1)
                pe.wait_ge(q_scaled, n + 1)
                pe.wait_ge(c_ready, n + (CTX_STEPS - 1))
                if j or not first_body(it):
                    pe.wait_ge(h_ready, n)
                for hd in range(HEADS):
                    pe.matmul(psN[:, hd // 2, hd % 2, :], pm[:, j % 2, hd, :], v1[:, j, hd, :],
                              start=True, stop=False)
                    mm = pe.matmul(psN[:, hd // 2, hd % 2, :], wib[:, j, hd, :], C[:, j % 2, hd, :],
                                   start=False, stop=True)
                mm.then_inc(num_ready, 1)

            def turn_y(it, j):
                wait_count(pe, y_ready, it, LOOP, j + 1 - DONE)
                wait_count(pe, yT_ready, it, LOOP, j - DONE)
                for hd in range(HEADS):
                    mm = pe.transpose(psY[:, hd, :], h[:, j, hd, :], ident[:, :])
                mm.then_inc(y_turned, 1)

            def front(it, j):
                turn_k(j, LOOP * it + (CTX_STEPS + j), 64 * it + (32 + 64))
                scores(it, j)

            def body(it, final):
                front(it, 0)
                for j in range(LOOP):
                    if j < LOOP - 1:
                        front(it, j + 1)
                    numerators(it, j)
                    state(j, j % 2, LOOP * it + (CTX_STEPS + j))
                    back = final and earlier(it, j, 3)
                    if back:
                        turn_y(*back)

            pe.wait_ge(cols_ready, 2)
            body(0, False)
            pe.wait_ge(s_spread, 1)
            pe.wait_ge(gate_cols_in, 16 * KD)
            for c in range(2):
                if c:
                    pe.wait_ge(gate_step, 1)
                for k in range(KD):
                    mm = pe.matmul(psY[:, :, :], sfull[:, k, :], stage[:, k, c * TILE:(c + 1) * TILE],
                                   start=(k == 0), stop=(k == KD - 1))
                mm.then_inc(gate_sum, 1)
            with pe.Fori(1, HALF) as it:
                body(it, False)
            body(HALF, True)
            with pe.Fori(HALF + 1, 2 * HALF) as it:
                body(it, True)
            for j in range(1, LOOP):
                turn_y(2 * HALF - 1, j)

        @block.scalar
        def _(act):
            act.wait_ge(rows_in, 64)
            act.activation(logf[:, :, :], fpre[:, :, :], ACT.Abs).then_inc(act_row, 1)
            act.wait_ge(act_row, 1)
            act.activation(logf[:, :, :], logf[:, :, :], ACT.Exp, scale=-1.0).then_inc(act_row, 1)
            act.wait_ge(act_row, 2)
            act.wait_ge(const_set, 6)
            act.activation(logf[:, :, :], logf[:, :, :], ACT.Ln, bias=ones[:, 0:1]).then_inc(act_row, 1)

            act.wait_ge(dve_row, 12)
            act.wait_ge(mprev_in, 32)
            for dr in range(2):
                act.activation(wsrow[:, dr, :], arow[:, dr, :], ACT.Exp, bias=nmlast[:, dr:dr + 1])
                act.activation(wcol[:, dr:dr + 1], mlast[:, dr:dr + 1], ACT.Exp, scale=-1.0,
                               bias=mprev[:, dr:dr + 1]).then_inc(act_row, 1)
            act.wait_ge(dve_row, 13)
            act.activation(emrow[:, :, :], emrow[:, :, :], ACT.Exp, scale=-1.0, bias=logroot[:, 0:1])\
               .then_inc(act_row, 1)
            for dr in range(2):
                act.wait_ge(turned, dr + 1)
                act.copy(cols[:, dr, :, :].rearrange("p w r -> p (w r)"),
                         psN[:, dr, :, :].rearrange("p a b -> p (a b)")[:, 0:3 * HC]).then_inc(cols_ready, 1)
            act.wait_ge(cols_ready, 2)

            def column(dr, which, c, hd):
                return cols[:, dr, which, bass.ds(c + hd * NT, 1)]

            def weigh_k(step, dr, c, first=False):
                act.wait_ge(k_turned, step + 1)
                if not first:
                    act.wait_ge(u_ready, step - 1)
                for hd in range(HEADS):
                    ins = act.activation(kw[:, dr, hd, :], psK[:, hd, :], ACT.Copy, scale=column(dr, 1, c, hd))
                ins.then_inc(kw_ready, 1)

            for j, (dr, c) in enumerate(CTX):
                weigh_k(j, dr, c, j < 2)

            def weights(it, j):
                n = LOOP * it + j
                act.wait_ge(masked, n + 1)
                for hd in range(HEADS):
                    ins = act.activation(E[:, j % 2, hd, :], E[:, j % 2, hd, :], ACT.Exp, scale=-1.0,
                                         bias=column(j % 2, 0, chunk_of(it, j) + NT_CTX, hd))
                ins.then_inc(e_ready, 1)

            def inter(it, j):
                act.wait_ge(step_in[j], 64 * it + (32 + 64))
                wait_count(act, num_ready, it, LOOP, j + 1 - LOOP)
                for hd in range(HEADS):
                    m = mpb[:, j % 2, bass.ds(chunk_of(it, j) + (NT_CTX + hd * NT), 1)]
                    ins = act.activation(wib[:, j, hd, :], mb[:, j, hd, :], ACT.Exp, scale=-1.0, bias=m)
                ins.then_inc(wi_ready, 1)

            def inter_ahead(it, j):
                if j < 2:
                    inter(it, j + 2)
                elif not (isinstance(it, int) and it == 2 * HALF - 1):
                    inter(it + 1, j - 2)

            def front(it, j):
                weights(it, j)
                weigh_k(LOOP * it + (CTX_STEPS + j), j % 2, chunk_of(it, j) + NT_CTX)

            def squares(it, j):
                wait_count(act, gated, it, LOOP, j + 1 - DONE)
                for hd in range(HEADS):
                    ins = act.activation(sq[:, j % 2, hd, :], og[:, j, hd, :], ACT.Square,
                                         accum_out=ssq[:, j, hd:hd + 1])
                ins.then_inc(ssq_ready, 1)

            def copy_y(it, j):
                wait_count(act, y_turned, it, LOOP, j + 1 - DONE)
                wait_count(act, y_out[j % 2], it, 32, 16 * (j // 2 - 2 * HALF))
                act.copy(yT[:, j % 2, :, :], psY[:, :, :]).then_inc(yT_ready, 1)

            def body(it, final):
                for j in range(-1, LOOP):
                    if final and j >= 0:
                        inter_ahead(it, j)
                    if j < LOOP - 1:
                        if not final:
                            inter(it, j + 1)
                        front(it, j + 1)
                    if j < 0:
                        continue
                    for lag, stage in ((1, squares), (LOOP, copy_y)):
                        back = final and earlier(it, j, lag)
                        if back:
                            stage(*back)

            def split_wo(it):
                for k in range(2):
                    block_k = bass.ds(2 * it + (k - 2), 1)
                    act.copy(wo_hi[:, block_k, :], stage[:, block_k, :]).then_inc(wo_high, 1)

            act.wait_ge(mpb_in, 32)
            body(0, False)
            with act.Fori(1, HALF) as it:
                body(it, False)
                act.wait_ge(wo_in, 16)
                split_wo(it)
            inter(HALF, 0)
            inter(HALF, 1)
            body(HALF, True)
            split_wo(HALF)
            body(HALF + 1, True)
            with act.Fori(HALF + 2, 2 * HALF - 1) as it:
                body(it, True)
            body(2 * HALF - 1, True)
            squares(2 * HALF - 1, LOOP - 1)
            for j in range(LOOP):
                copy_y(2 * HALF - 1, j)

        @block.vector
        def _(dve):
            dve.tensor_copy(sfull[:, :, :], svec[:, :, 0:1].to_broadcast([P, KD, P])).then_inc(s_spread, 1)
            row = lambda t, dr, back=False: t[:, dr, ::-1] if back else t[:, dr, :]
            dve.wait_ge(rows_in, 64)
            dve.wait_ge(act_row, 3)
            dve.scalar_tensor_tensor(logf[:, :, :], fpre[:, :, :], 0.0, logf[:, :, :], ALU.min, ALU.subtract)\
               .then_inc(dve_row, 1)
            dve.wait_ge(dve_row, 1)
            dve.wait_ge(const_set, 6)
            for dr in range(2):
                dve.tensor_tensor_scan(row(bsum, dr, dr), ones[:, :], row(logf, dr, dr), 0.0,
                                       ALU.mult, ALU.add).then_inc(dve_row, 1)
            dve.wait_ge(dve_row, 3)
            dve.tensor_tensor(arow[:, :, :], ipre[:, :, :], bsum[:, :, :], ALU.subtract).then_inc(dve_row, 1)
            dve.wait_ge(dve_row, 4)
            for dr in range(2):
                dve.tensor_tensor_scan(row(mrow, dr, dr), row(arow, dr, dr), row(arow, dr, dr), -3.0e38,
                                       ALU.max, ALU.max).then_inc(dve_row, 1)
            dve.wait_ge(ends_in, 32)
            dve.tensor_tensor_scan(carry[:, 0, :], chain[:, 0, 1, :], chain[:, 0, 0, :], 0.0,
                                   ALU.max, ALU.add).then_inc(dve_row, 1)
            dve.tensor_tensor_scan(carry[:, 1, 1::-1], chain[:, 1, 1, 1::-1], chain[:, 1, 0, 1::-1], 0.0,
                                   ALU.max, ALU.add).then_inc(dve_row, 1)
            dve.wait_ge(dve_row, 8)
            dve.tensor_tensor_scan(carry[:, 1, NT - 1:1:-1], chain[:, 1, 1, NT - 1:1:-1],
                                   chain[:, 1, 0, NT - 1:1:-1], carry[:, 1, 0:1],
                                   ALU.max, ALU.add).then_inc(dve_row, 1)
            dve.wait_ge(dve_row, 9)
            dve.memset(mp[:, 0, 0:1], 0.0)
            dve.memset(mp[:, 1, 1:2], 0.0)
            dve.tensor_copy(mp[:, 0, 1:NT], carry[:, 0, 0:NT - 1])
            dve.tensor_copy(mp[:, 1, 0:1], carry[:, 1, 1:2])
            dve.tensor_copy(mp[:, 1, NT - 1:NT], carry[:, 1, 0:1])
            dve.tensor_copy(mp[:, 1, 2:NT - 1], carry[:, 1, 3:NT]).then_inc(dve_row, 1)
            dve.wait_ge(mprev_in, 32)
            dve.wait_ge(dve_row, 6)
            dve.wait_ge(ends_out, 64)
            for dr in range(2):
                end = P - 1 if dr == 0 else 0
                dve.tensor_scalar(mlast[:, dr:dr + 1], mrow[:, dr, end:end + 1], mprev[:, dr:dr + 1], None, ALU.max)
                ins = dve.tensor_scalar(nmlast[:, dr:dr + 1], mrow[:, dr, end:end + 1], mprev[:, dr:dr + 1], -1.0,
                                        ALU.max, ALU.mult)
            ins.then_inc(dve_row, 1)
            dve.wait_ge(dve_row, 11)
            for dr in range(2):
                ins = dve.tensor_scalar(mrow[:, dr, :], mrow[:, dr, :], mprev[:, dr:dr + 1], None, ALU.max)
            ins.then_inc(dve_row, 1)
            dve.wait_ge(dve_row, 12)
            dve.tensor_tensor(emrow[:, :, :], bsum[:, :, :], mrow[:, :, :], ALU.add).then_inc(dve_row, 1)

            def update(step, dr, c, first=False):
                dve.wait_ge(u_ready, step + 1)
                if not first:
                    dve.wait_ge(c_ready, step - 1)
                for hd in range(HEADS):
                    ins = dve.scalar_tensor_tensor(C[:, dr, hd, :], C[:, dr, hd, :], wc[:, dr, bass.ds(c + hd * NT, 1)],
                                                   psU[:, hd // 2, hd % 2, :], ALU.mult, ALU.add)
                ins.then_inc(c_ready, 1)

            dve.wait_ge(wc_in, 32)
            for j, (dr, c) in enumerate(CTX):
                update(j, dr, c, j < 2)

            def products(it, j):
                n = LOOP * it + j
                dve.wait_ge(s_ready, n + 1)
                dve.wait_ge(e_ready, n + 1)
                if j >= 2 or not first_body(it):
                    dve.wait_ge(num_ready, n - 1)
                dve.tensor_tensor(pm[:, j % 2, :, :], psS[j % 2][:, :, :], E[:, j % 2, :, :], ALU.mult)\
                   .then_inc(p_ready, 1)

            def normalise(it, j, final):
                n, b = LOOP * it + j, j % 2
                dve.wait_ge(num_ready, n + 1)
                floor = cols[:, b, 2, :].rearrange("p (h c) -> p h c", h=HEADS)[:, :, bass.ds(chunk_of(it, j) + NT_CTX, 1)]
                floor = floor.rearrange("p (a b) c -> p a b c", a=2)[:, :, :, 0]
                size = psN[:, :, :, DH]
                dn = den[:, b, :].rearrange("p (a b) -> p a b", a=2)
                dve.scalar_tensor_tensor(dn, size, -1.0, floor, ALU.mult, ALU.max).then_inc(den_neg, 1)
                dve.wait_ge(den_neg, n + 1)
                dve.tensor_tensor(dn, size, dn, ALU.max).then_inc(den_max, 1)
                dve.wait_ge(den_max, n + 1)
                dve.reciprocal(den[:, b, :], den[:, b, :]).then_inc(den_inv, 1)
                dve.wait_ge(den_inv, n + 1)
                if final:
                    dve.wait_ge(h_out[j], 16 * HALF)
                    if earlier(it, j, LOOP):
                        wait_count(dve, y_turned, it, LOOP, j + 1 - LOOP - DONE)
                elif not first_body(it):
                    dve.wait_ge(h_out[j], 16 * it)
                if final:
                    wait_count(dve, fin_in[j], it, 48, 48 * (1 - HALF))
                    for hd in range(HEADS):
                        ins = dve.scalar_tensor_tensor(h[:, j, hd, :], psN[:, hd // 2, hd % 2, 0:DH],
                                                       den[:, b, hd:hd + 1], other[:, j, hd, :], ALU.mult, ALU.add)
                else:
                    ins = dve.tensor_tensor(h[:, j, :, :].rearrange("p (a b) v -> p a b v", a=2), psN[:, :, :, 0:DH],
                                            dn.unsqueeze(3).to_broadcast([P, 2, 2, DH]), ALU.mult)
                ins.then_inc(h_ready, 1)

            def outputs(it, j):
                wait_count(dve, rinv_ready, it, LOOP, j + 1 - DONE)
                for hd in range(HEADS):
                    ins = dve.scalar_tensor_tensor(h[:, j, hd, :], og[:, j, hd, :], rinv[:, j, hd:hd + 1],
                                                   zg[:, j, hd, :], ALU.mult, ALU.mult)
                ins.then_inc(y_scaled, 1)
                wait_count(dve, y_scaled, it, LOOP, j + 1 - DONE)
                dve.tensor_tensor(h[:, j, :, :], h[:, j, :, :], gain[:, :].rearrange("p (h v) -> p h v", h=HEADS),
                                  ALU.mult).then_inc(y_ready, 1)

            def body(it, final):
                products(it, 0)
                for j in range(LOOP):
                    if j < LOOP - 1:
                        products(it, j + 1)
                    normalise(it, j, final)
                    update(LOOP * it + (CTX_STEPS + j), j % 2, chunk_of(it, j) + NT_CTX)
                    back = final and earlier(it, j, 2)
                    if back:
                        outputs(*back)

            dve.wait_ge(const_in, 48)
            dve.tensor_scalar(gain[:, :], gain[:, :], float(math.sqrt(DH)), None, ALU.mult).then_inc(gain_ready, 1)
            def split_wo(it):
                for k in range(2):
                    block_k = bass.ds(2 * it + (k - 2), 1)
                    dve.wait_ge(wo_high, 2 * it + (k - 1))
                    dve.tensor_tensor(wo_lo[:, block_k, :], stage[:, block_k, :], wo_hi[:, block_k, :].bitcast(F32),
                                      ALU.subtract).then_inc(wo_low, 1)

            body(0, False)
            dve.wait_ge(gate_rows_in, 32)
            for c in range(2):
                cut = slice(c * TILE, (c + 1) * TILE)
                dve.wait_ge(gate_sum, c + 1)
                dve.tensor_tensor(gate[:, cut], psY[:, :, :].rearrange("p h t -> p (h t)"), bgate[:, cut], ALU.add)\
                   .then_inc(gate_step, 1)
            dve.wait_ge(gate_step, 2)
            dve.scalar_tensor_tensor(gate[:, :], gate[:, :], ROOT_D, post, ALU.mult, ALU.mult).then_inc(gate_step, 1)
            with dve.Fori(1, HALF) as it:
                body(it, False)
                split_wo(it)
            dve.wait_ge(gain_ready, 1)
            body(HALF, True)
            split_wo(HALF)
            with dve.Fori(HALF + 1, 2 * HALF) as it:
                body(it, True)
            for j in range(LOOP - 2, LOOP):
                outputs(2 * HALF - 1, j)


GROUPS = CH // P
S_TILES = N2 // 2
Q_TILES = NQ // 4
F_TILES = N2 // 4


PER_UNIT = {"S": 2 * S_TILES + 1, "T": F_TILES + Q_TILES + 2 * F_TILES + Q_TILES,
            "X": F_TILES + Q_TILES + F_TILES + 2 * Q_TILES, "I": Q_TILES}
START = {"S": S_TILES + 1, "T": F_TILES + Q_TILES, "X": F_TILES + 2 * Q_TILES, "I": 0}
NORM_AFTER = 2


def places(start=None):
    return dict(start or START)


def hyena(nc, d, s, hidden):
    with ExitStack() as ctx:
        sb, ps = mem_makers(nc, ctx)
        sem = sem_maker(nc, ctx)
        tables = sb("tables", [P, 5, NQ, P])
        outer = sb("outer", [P, 2 * K1])
        back = sb("back", [K1, 2, P])
        ident = sb("ident_h", [P, P])
        ones = sb("ones_h", [P, P])
        guard = sb("guard_h", [P, 1])
        w3 = sb("w3", [P, 2, 2, P])
        fb = sb("fb", [P, 2, P])
        window = sb("window", [P, N2, P])
        f = sb("f", [P, N2, P])
        Bf = sb("Bf", [P, NQ, 8, N2])
        A2f = sb("A2f", [P, NQ, P])
        sums = sb("sums", [P, P])
        total = sb("total", [P, P])
        H = sb("H", [P, 2, NQ, P])
        xin = sb("xin", [P, T_LAT])
        x2 = sb("x2", [P, T_LAT])
        zh = sb("zh", [P, T_LAT])
        nat = sb("nat", [P, N2, P])
        x1 = sb("x1", [P, N2, P])
        B = sb("B", [P, NQ, 8, N2])
        Bi = B[:, :, :, :].rearrange("p q a n -> p (q a n)").rearrange("p (m q j) -> p m q j", q=NQ, j=4)
        A2 = sb("A2", [P, NQ, P])
        Ai = sb("Ai", [K1, 2, N2, P])
        prod = sb("prod", [P, 2, 2, 4, P])
        sqr = Bf[:, :, :, :].rearrange("p q a n -> p (q a n)")[:, 0:N2 * P].rearrange("p (n c) -> p n c", n=N2)

        psS = [ps(f"psS_h{i}", [P, 2, 8, NQ]) for i in range(2)]
        psT = [ps(f"psT{i}", [P, 4, P]) for i in range(2)]
        psX = [ps(f"psX{i}", [P, 4, P]) for i in range(2)]
        psI = [ps(f"psI{i}", [P, 4, P]) for i in range(2)]
        banks = {"S": psS, "T": psT, "X": psX, "I": psI}

        start_in = sem("start_in")
        filter_in = sem("filter_in")
        const_in = sem("const_in_h")
        const_set = sem("const_set_h")
        group_in = sem("group_in")
        x_in = sem("x_in")
        gates_in = sem("gates_in")
        summed = {r: sem(f"{r}_summed") for r in "STXI"}
        taken = {r: sem(f"{r}_taken") for r in "STXI"}
        squared = sem("squared")
        n2_summed = sem("n2_summed")
        root_ready = sem("root_ready")
        scale_ready = sem("scale_ready")
        f_scaled = sem("f_scaled")
        f_ready = sem("f_ready")
        gated = sem("gated_h")
        y_out = sem("y_out_h")

        block = ctx.enter_context(nc.Block())
        UNIT1 = {r: START[r] + PER_UNIT[r] for r in START}

        @block.sync
        def _(sp):
            def load_group(g):
                sp.dma_start(w3[:, :, :, :], d["fw3"][g]).then_inc(group_in, 16)
                sp.dma_start(window[:, :, :], d["window"][g]).then_inc(group_in, 16)
                sp.dma_start(fb[P // 2:P // 2 + 1, :, :], d["fbias"][g]).then_inc(group_in, 16)

            def load_x(block_row):
                sp.dma_start(xin[:, :], s["qhy"][block_row]).then_inc(x_in, 16)

            def load_gates(g):
                sp.dma_start(x2[:, :], s["qhy"][g + (HEADS + 2 * GROUPS)]).then_inc(gates_in, 16)
                sp.dma_start(zh[:, :], s["zh"][g]).then_inc(gates_in, 16)

            load_group(0)
            sp.dma_start(ident[:, :], d["ident"]).then_inc(start_in, 16)
            load_x(HEADS)
            sp.dma_start(outer[:, :], d["outer"].rearrange("p a k -> p (a k)")).then_inc(start_in, 16)
            sp.dma_start(tables[:, 1:3, :, :], d["tables"][:, 1:3]).then_inc(filter_in, 16)
            for dst, src in ((tables[:, 0, :, :], d["tables"][:, 0]), (tables[:, 3:5, :, :], d["tables"][:, 3:5]),
                             (back[:, :, :], d["back"])):
                sp.dma_start(dst, src).then_inc(const_in, 16)
            sp.wait_ge(summed["T"], F_TILES)
            load_x(HEADS + GROUPS)
            load_gates(0)

            def body(g, last):
                if not last:
                    wait_count(sp, summed["T"], g, 2 * PER_UNIT["T"], START["T"] + F_TILES)
                    load_x(g + (HEADS + 1))
                    wait_count(sp, f_ready, g, 2, 2)
                    load_group(g + 1)
                    wait_count(sp, summed["T"], g, 2 * PER_UNIT["T"], UNIT1["T"] + F_TILES)
                    load_x(g + (HEADS + GROUPS + 1))
                end = UNIT1["X"] + Q_TILES + F_TILES + (0 if last else F_TILES)
                wait_count(sp, taken["X"], g, 2 * PER_UNIT["X"], end)
                sp.dma_start(s["y"][g + HEADS], x2[:, :]).then_inc(y_out, 16)
                wait_count(sp, y_out, g, 16, 16)
                if not last:
                    load_gates(g + 1)

            body(0, False)
            with sp.Fori(1, GROUPS - 1) as g:
                body(g, False)
            body(GROUPS - 1, True)

        @block.gpsimd
        def _(pool):
            pool.memset(ones[:, :], 1.0).then_inc(const_set, 1)
            pool.memset(guard[:, :], EPS).then_inc(const_set, 1)
            with pool.Fori(0, GROUPS) as g:
                pool.wait_ge(gates_in, 32 * g + 32)
                pool.tensor_tensor(x2[:, :], x2[:, :], zh[:, :], ALU.mult).then_inc(gated, 1)

        @block.tensor
        def _(pe):
            def fill(g, at, ring):
                n = at[ring]
                at[ring] += 1
                wait_count(pe, taken[ring], g, 2 * PER_UNIT[ring], n - 1)
                return banks[ring][n % 2]

            def outer_tile(g, at, src, t):
                bank = fill(g, at, "S")
                for i in range(2):
                    mm = pe.matmul(bank[:, i, :, :].rearrange("p a q -> p (a q)"), src[:, 2 * t + i, :], outer[:, :],
                                   start=True, stop=True)
                mm.then_inc(summed["S"], 1)

            def turn_x(g, at):
                for t in range(F_TILES):
                    bank = fill(g, at, "T")
                    for i in range(4):
                        mm = pe.transpose(bank[:, i, :], xin[:, 4 * t + i:T_LAT:N2], ident[:, :])
                    mm.then_inc(summed["T"], 1)

            def to_rows(g, at, src, t):
                bank = fill(g, at, "T")
                for i in range(4):
                    mm = pe.transpose(bank[:, i, :], src[:, 4 * t + i, :, :].rearrange("p a n -> p (a n)"), ident[:, :])
                mm.then_inc(summed["T"], 1)

            def in_time(g, at, o):
                for t in range(F_TILES):
                    bank = fill(g, at, "X")
                    for i in range(2):
                        mm = pe.matmul(bank[:, 2 * i:2 * i + 2, :], hidden[:, 2 * t + i:HALF_T:N2 // 2],
                                       w3[:, o, :, :].rearrange("k e c -> k (e c)"), start=True, stop=True)
                    mm.then_inc(summed["X"], 1)

            def norm(g, at, unit):
                wait_count(pe, n2_summed, g, 2, unit + 1)
                bank = fill(g, at, "S")
                pe.matmul(bank[:, :, :, :].rearrange("p b a q -> p (b a q)")[:, 0:P], ones[:, :], sums[:, :],
                          start=True, stop=True).then_inc(summed["S"], 1)

            def filter_outer(g, at, unit):
                wait_count(pe, f_ready, g, 2, unit + 1)
                for t in range(S_TILES):
                    outer_tile(g, at, f, t)

            def filter_inner(g, at):
                wait_count(pe, taken["S"], g, 2 * PER_UNIT["S"], at["S"])
                for t in range(Q_TILES + 1):
                    if t < Q_TILES:
                        to_rows(g, at, Bf, t)
                    if t:
                        wait_count(pe, taken["T"], g, 2 * PER_UNIT["T"], at["T"] - (t < Q_TILES))
                        for part in range(2):
                            bank = fill(g, at, "X")
                            for i in range(4):
                                q = 4 * (t - 1) + i
                                mm = pe.matmul(bank[:, i, :], tables[:, 1 + part, q, :], A2f[:, q, :],
                                               start=True, stop=True)
                            mm.then_inc(summed["X"], 1)

            pe.wait_ge(const_set, 2)
            pe.wait_ge(group_in, 48)
            at = {"S": 0, "T": 0, "X": 0, "I": 0}
            in_time(0, at, 0)
            pe.wait_ge(start_in, 32)
            pe.wait_ge(x_in, 16)
            turn_x(0, at)
            norm(0, at, 0)
            filter_outer(0, at, 0)
            pe.wait_ge(filter_in, 16)
            filter_inner(0, at)
            pe.wait_ge(const_in, 48)

            def unit(g, at, o, more):
                for t in range(S_TILES):
                    if t % 2 == 0:
                        if o:
                            wait_count(pe, taken["X"], g, 2 * PER_UNIT["X"],
                                       UNIT1["X"] - 2 * Q_TILES - F_TILES + t // 2 + 1)
                        elif isinstance(g, int) and g == 0:
                            pe.wait_ge(taken["T"], t // 2 + 1)
                        else:
                            wait_count(pe, taken["T"], g, 2 * PER_UNIT["T"],
                                       UNIT1["T"] - 2 * PER_UNIT["T"] + t // 2 + 1)
                    outer_tile(g, at, nat, t)
                if more:
                    wait_count(pe, x_in, g, 32, 32 + 16 * o)
                    turn_x(g, at)
                wait_count(pe, taken["S"], g, 2 * PER_UNIT["S"], at["S"])
                rows_at = at["T"]
                for t in range(Q_TILES):
                    to_rows(g, at, B, t)
                if more:
                    wait_count(pe, group_in, g, 48, 48 + 48 * o)
                    in_time(g, at, 1 - o)

                def inverse(t, product_at):
                    wait_count(pe, taken["X"], g, 2 * PER_UNIT["X"], product_at + 1)
                    bank = fill(g, at, "I")
                    for i in range(4):
                        q = 4 * t + i
                        for part in range(2):
                            mm = pe.matmul(bank[:, i, :], prod[:, t % 2, part, i, :], tables[:, 3 + part, q, :],
                                           start=(part == 0), stop=(part == 1))
                    mm.then_inc(summed["I"], 1)

                for t in range(Q_TILES):
                    wait_count(pe, taken["T"], g, 2 * PER_UNIT["T"], rows_at + t + 1)
                    bank = fill(g, at, "X")
                    for i in range(4):
                        mm = pe.matmul(bank[:, i, :], tables[:, 0, 4 * t + i, :], A2[:, 4 * t + i, :],
                                       start=True, stop=True)
                    mm.then_inc(summed["X"], 1)
                    if t:
                        inverse(t - 1, at["X"] - 2)
                    if more and t == NORM_AFTER:
                        norm(g, at, o + 1)
                inverse(Q_TILES - 1, at["X"] - 1)
                if more:
                    filter_outer(g, at, o + 1)
                wait_count(pe, taken["I"], g, 2 * PER_UNIT["I"], at["I"])
                for t in range(F_TILES + 1):
                    if t < F_TILES:
                        for r in range(2):
                            bank = fill(g, at, "T")
                            for i in range(4):
                                mm = pe.transpose(bank[0:K1, i, :], Bi[:, N2 * r + 4 * t + i, :, :].rearrange("c q j -> c (q j)"),
                                                  ident[:, :])
                            mm.then_inc(summed["T"], 1)
                    if t:
                        n2 = 4 * (t - 1)
                        wait_count(pe, taken["T"], g, 2 * PER_UNIT["T"], at["T"] - 2 * (t < F_TILES))
                        bank = fill(g, at, "X")
                        if o == 0:
                            for r in range(2):
                                mm = pe.matmul(bank[:, :, :], back[:, r, :],
                                               Ai[:, r, n2:n2 + 4, :].rearrange("k n c -> k (n c)"),
                                               start=(r == 0), stop=(r == 1))
                        else:
                            for i in range(4):
                                for r in range(2):
                                    mm = pe.matmul(bank[:, i, :], Ai[:, r, n2 + i, :], back[:, r, :],
                                                   start=(r == 0), stop=(r == 1))
                        mm.then_inc(summed["X"], 1)
                if more:
                    filter_inner(g, at)

            def body(g, last):
                at = places()
                unit(g, at, 0, True)
                unit(g, at, 1, not last)

            body(0, False)
            with pe.Fori(1, GROUPS - 1) as g:
                body(g, False)
            body(GROUPS - 1, True)

        @block.scalar
        def _(act):
            def take(g, at, ring, dst, rows=P):
                n = at[ring]
                at[ring] += 1
                wait_count(act, summed[ring], g, 2 * PER_UNIT[ring], n + 1)
                act.copy(dst, banks[ring][n % 2][0:rows]).then_inc(taken[ring], 1)

            def take_outer(g, at, dst):
                for t in range(S_TILES):
                    take(g, at, "S", dst[:, :, :, 2 * t:2 * t + 2].rearrange("p q a n -> p n a q"))

            def take_tiles(g, at, ring, dst, tiles):
                for t in range(tiles):
                    take(g, at, ring, dst[:, 4 * t:4 * t + 4])

            def square(g, x_at):
                wait_count(act, taken["X"], g, 2 * PER_UNIT["X"], x_at)
                act.activation(sqr, f[:, :, :], ACT.Square).then_inc(squared, 1)

            def root(g, at):
                n = at["S"]
                at["S"] += 1
                wait_count(act, summed["S"], g, 2 * PER_UNIT["S"], n + 1)
                act.activation(total[:, :], banks["S"][n % 2][:, :, :, :].rearrange("p b a q -> p (b a q)")[:, 0:P],
                               ACT.Sqrt, bias=guard[:, 0:1]).then_inc(taken["S"], 1)

            act.wait_ge(const_set, 2)
            at = {"S": 0, "T": 0, "X": 0, "I": 0}
            square(0, F_TILES)
            take_tiles(0, at, "T", nat, F_TILES)
            root(0, at)
            take_outer(0, at, Bf)
            take_tiles(0, at, "T", A2f, Q_TILES)

            def unit(g, at, o, more):
                take_outer(g, at, B)
                if more:
                    take_tiles(g, at, "T", nat if o else x1, F_TILES)
                take_tiles(g, at, "T", A2, Q_TILES)
                if more:
                    square(g, (UNIT1 if o else START)["X"] + F_TILES)
                for t in range(Q_TILES):
                    n = at["I"]
                    at["I"] += 1
                    wait_count(act, summed["I"], g, 2 * PER_UNIT["I"], n + 1)
                    act.copy(Bi[:, :, 4 * t:4 * t + 4, :],
                             psI[n % 2][:, :, :].rearrange("p q (m j) -> p m q j", j=4)).then_inc(taken["I"], 1)
                    if more and t == NORM_AFTER - 1:
                        root(g, at)
                if more:
                    take_outer(g, at, Bf)
                for t in range(F_TILES):
                    for r in range(2):
                        take(g, at, "T", Ai[:, r, 4 * t:4 * t + 4, :], K1)
                if more:
                    take_tiles(g, at, "T", A2f, Q_TILES)

            def body(g, last):
                at = places()
                unit(g, at, 0, True)
                unit(g, at, 1, not last)

            body(0, False)
            with act.Fori(1, GROUPS - 1) as g:
                body(g, False)
            body(GROUPS - 1, True)

        @block.vector
        def _(dve):
            def tile_of(g, at, ring):
                n = at[ring]
                at[ring] += 1
                wait_count(dve, summed[ring], g, 2 * PER_UNIT[ring], n + 1)
                return banks[ring][n % 2][:, :, :]

            def weigh(g, at, loads):
                wait_count(dve, group_in, g, 48, 48 * loads)
                for t in range(F_TILES):
                    dve.tensor_tensor(f[:, 4 * t:4 * t + 4, :], tile_of(g, at, "X"), window[:, 4 * t:4 * t + 4, :],
                                      ALU.mult).then_inc(taken["X"], 1)

            def sum_squares(g, unit):
                wait_count(dve, squared, g, 2, unit + 1)
                dve.tensor_reduce(sums[:, :], sqr.rearrange("p n c -> p c n"), AX.X, ALU.add).then_inc(n2_summed, 1)

            def invert(g, at, unit):
                wait_count(dve, taken["S"], g, 2 * PER_UNIT["S"], at["S"] + 1)
                dve.reciprocal(total[:, :], total[:, :]).then_inc(scale_ready, 1)

            def scale(g, unit, half):
                if half == 0:
                    wait_count(dve, scale_ready, g, 2, unit + 1)
                cut = slice(half * N2 // 2, (half + 1) * N2 // 2)
                ins = dve.tensor_tensor(f[:, cut, :], f[:, cut, :],
                                        total[:, :].unsqueeze(1).to_broadcast([P, N2 // 2, P]), ALU.mult)
                if half == 0:
                    ins.then_inc(f_scaled, 1)

            def add_bias(g, unit, o):
                wait_count(dve, f_scaled, g, 2, unit + 1)
                dve.tensor_tensor(f[P // 2:P // 2 + 1, 0, :], f[P // 2:P // 2 + 1, 0, :],
                                  fb[P // 2:P // 2 + 1, o, :], ALU.add).then_inc(f_ready, 1)

            def take_spectrum(g, at):
                for t in range(Q_TILES):
                    for part in range(2):
                        dve.tensor_copy(H[:, part, 4 * t:4 * t + 4, :], tile_of(g, at, "X")).then_inc(taken["X"], 1)

            at = {"S": 0, "T": 0, "X": 0, "I": 0}
            weigh(0, at, 1)
            sum_squares(0, 0)
            invert(0, at, 0)
            scale(0, 0, 0)
            scale(0, 0, 1)
            add_bias(0, 0, 0)
            take_spectrum(0, at)

            def unit(g, at, o, more):
                spectrum_at = at["X"]
                if more:
                    weigh(g, at, 1 + o)
                wait_count(dve, taken["X"], g, 2 * PER_UNIT["X"], spectrum_at)
                for t in range(Q_TILES):
                    wait_count(dve, summed["I"], g, 2 * PER_UNIT["I"], Q_TILES * o + t - 1)
                    tile = tile_of(g, at, "X")
                    for part in range(2):
                        ins = dve.tensor_tensor(prod[:, t % 2, part], tile, H[:, part, 4 * t:4 * t + 4, :], ALU.mult)
                    ins.then_inc(taken["X"], 1)
                    if more and t == NORM_AFTER - 1:
                        sum_squares(g, o + 1)
                    if more and t == Q_TILES - 3:
                        invert(g, {"S": (UNIT1 if o else START)["S"] + S_TILES}, o + 1)
                    if more and t >= Q_TILES - 2:
                        scale(g, o + 1, t - (Q_TILES - 2))
                if more:
                    add_bias(g, o + 1, 1 - o)
                if o:
                    wait_count(dve, gated, g, 1, 1)
                else:
                    wait_count(dve, taken["T"], g, 2 * PER_UNIT["T"], START["T"] + F_TILES)
                for t in range(F_TILES):
                    tile = tile_of(g, at, "X")
                    if o:
                        y = x2[:, :].rearrange("p (t n) -> p n t", n=N2)[:, 4 * t:4 * t + 4, :]
                        ins = dve.tensor_tensor(y, tile, y, ALU.mult)
                    else:
                        ins = dve.tensor_tensor(nat[:, 4 * t:4 * t + 4, :], tile, x1[:, 4 * t:4 * t + 4, :], ALU.mult)
                    ins.then_inc(taken["X"], 1)
                if more:
                    take_spectrum(g, at)

            def body(g, last):
                at = places()
                unit(g, at, 0, True)
                unit(g, at, 1, not last)

            body(0, False)
            with dve.Fori(1, GROUPS - 1) as g:
                body(g, False)
            body(GROUPS - 1, True)


def output(nc, d, s, w_hi, w_lo, gate, out):
    with ExitStack() as ctx:
        sb, ps = mem_makers(nc, ctx)
        sem = sem_maker(nc, ctx)
        y_hi = sb("y_hi", [P, 2, KD, P], F32R)
        y_lo = sb("y_lo", [P, 2, KD, P], F32R)
        y = sb("y", [P, 2, KD, P])
        x = sb("x_o", [P, 2, D])
        z = sb("z_o", [P, 2, D])
        sumsq = sb("sumsq_o", [P, 2, 2])
        rinv = sb("rinv_o", [P, 2])
        power = sb("power_o", [P, 2])

        acc = [[ps(f"acc{i}{c}", [P, TILE]) for c in range(2)] for i in range(2)]

        power_set = sem("power_set_o")
        y_in = [sem(f"y_in{i}") for i in range(2)]
        x_in = [sem(f"xo_in{i}") for i in range(2)]
        hi_ready = sem("yhi_ready")
        lo_ready = sem("ylo_ready")
        acc_ready = sem("acc_ready")
        squared = sem("squared_o")
        rinv_step = sem("rinv_step_o")
        gated = sem("gated_o")
        res_ready = sem("res_ready_o")
        out_done = [sem(f"out_done{i}") for i in range(2)]

        block = ctx.enter_context(nc.Block())

        @block.sync
        def _(sp):
            def load_y(t, b):
                sp.dma_start(y[:, b, :, :], s["y"][:, :, bass.ts(t, P)].rearrange("k p t -> p k t"))\
                  .then_inc(y_in[b], 16)

            def load_x(t, b):
                sp.dma_start(x[:, b, :], d["x"][bass.ts(t, P), :]).then_inc(x_in[b], 16)

            for b in range(2):
                load_y(b, b)
            for b in range(2):
                load_x(b, b)

            sp.wait_ge(lo_ready, 1)
            load_y(2, 0)

            def store(i, b, load_y3=True, load_x2=True):
                if load_y3:
                    sp.wait_ge(lo_ready, 2 * i + (b + 2))
                    load_y(2 * i + (b + 3), 1 - b)
                sp.wait_ge(res_ready, 2 * i + (b + 1))
                sp.dma_start(out[bass.ts(2 * i + b, P), :], z[:, b, :]).then_inc(out_done[b], 16)
                if load_x2:
                    load_x(2 * i + (b + 2), b)

            with sp.Fori(0, NT_LAT // 2 - 2) as i:
                for b in range(2):
                    store(i, b)
            for n in range(NT_LAT - 4, NT_LAT):
                store(n // 2, n % 2, n + 3 < NT_LAT, n + 2 < NT_LAT)
            for b in range(2):
                sp.wait_ge(out_done[b], 16 * (NT_LAT // 2))

        @block.gpsimd
        def _(pool):
            pool.memset(power[:, 0:1], -0.5).then_inc(power_set, 1)
            pool.memset(power[:, 1:2], D * EPS).then_inc(power_set, 1)
            pool.wait_ge(power_set, 2)
            with pool.Fori(0, NT_LAT // 2) as i:
                for b in range(2):
                    n = 2 * i + (b + 1)
                    pool.wait_ge(squared, n)
                    pool.tensor_tensor(rinv[:, b:b + 1], sumsq[:, b, 0:1], sumsq[:, b, 1:2], ALU.add)\
                        .then_inc(rinv_step, 1)
                    pool.wait_ge(rinv_step, 6 * i + (3 * b + 1))
                    pool.tensor_tensor(rinv[:, b:b + 1], rinv[:, b:b + 1], power[:, 1:2], ALU.add)\
                        .then_inc(rinv_step, 1)
                    pool.wait_ge(rinv_step, 6 * i + (3 * b + 2))
                    pool.tensor_tensor(rinv[:, b:b + 1], rinv[:, b:b + 1], power[:, 0:1], ALU.pow)\
                        .then_inc(rinv_step, 1)

        @block.tensor
        def _(pe):
            def tile(i, b, first):
                pe.wait_ge(hi_ready, 2 * i + (b + 1))
                pe.wait_ge(lo_ready, 2 * i + (b + 1))
                if not first:
                    pe.wait_ge(gated, 2 * i + (b - 1))
                for c in range(2):
                    o, cut = acc[b][c][:, :], slice(c * TILE, (c + 1) * TILE)
                    for k in range(KD):
                        pe.matmul(o, y_hi[:, b, k, :], w_hi[:, k, cut], start=(k == 0), stop=False)
                        pe.matmul(o, y_hi[:, b, k, :], w_lo[:, k, cut], start=False, stop=False)
                        mm = pe.matmul(o, y_lo[:, b, k, :], w_hi[:, k, cut], start=False, stop=(k == KD - 1))
                mm.then_inc(acc_ready, 1)

            for b in range(2):
                tile(0, b, True)
            with pe.Fori(1, NT_LAT // 2) as i:
                for b in range(2):
                    tile(i, b, False)

        @block.scalar
        def _(act):
            def high(i, b, first):
                act.wait_ge(y_in[b], 16 * i + 16)
                if not first:
                    act.wait_ge(acc_ready, 2 * i + (b - 1))
                act.copy(y_hi[:, b], y[:, b]).then_inc(hi_ready, 1)

            for b in range(2):
                high(0, b, True)

            def squares(i, b, first):
                act.wait_ge(acc_ready, 2 * i + (b + 1))
                if not first:
                    act.wait_ge(out_done[b], 16 * i)
                for c in range(2):
                    ins = act.activation(z[:, b, c * TILE:(c + 1) * TILE], acc[b][c][:, :], ACT.Square,
                                         accum_out=sumsq[:, b, c:c + 1])
                ins.then_inc(squared, 1)

            def body(i, first, last):
                for b in range(2):
                    squares(i, b, first)
                    if not last:
                        high(i + 1, b, False)

            body(0, True, False)
            with act.Fori(1, NT_LAT // 2 - 1) as i:
                body(i, False, False)
            body(NT_LAT // 2 - 1, False, True)

        @block.vector
        def _(dve):
            def low(i, b):
                dve.wait_ge(hi_ready, 2 * i + (b + 1))
                dve.tensor_tensor(y_lo[:, b], y[:, b], y_hi[:, b].bitcast(F32), ALU.subtract).then_inc(lo_ready, 1)

            for b in range(2):
                low(0, b)
            def finish(i, b):
                n = 2 * i + (b + 1)
                dve.wait_ge(rinv_step, 6 * i + (3 * b + 3))
                for c in range(2):
                    cut = slice(c * TILE, (c + 1) * TILE)
                    ins = dve.scalar_tensor_tensor(z[:, b, cut], acc[b][c][:, :], rinv[:, b:b + 1], gate[:, cut],
                                                   ALU.mult, ALU.mult)
                ins.then_inc(gated, 1)
                dve.wait_ge(gated, n)
                dve.wait_ge(x_in[b], 16 * i + 16)
                dve.tensor_tensor(z[:, b, :], z[:, b, :], x[:, b, :], ALU.add).then_inc(res_ready, 1)

            def body(i, last):
                for b in range(2):
                    if not last:
                        low(i + 1, b)
                    finish(i, b)

            with dve.Fori(0, NT_LAT // 2 - 1) as i:
                body(i, False)
            body(NT_LAT // 2 - 1, True)


def build(nc, d, out, stages=("project", "mlstm", "hyena", "output")):
    scratch = {
        "gates": (P, T_ALL), "k": (HEADS, P, T_ALL), "v": (NT, P, CH), "qhy": (16, P, T_LAT),
        "ozh": (2, NT_LAT, P, CH), "zh": (GROUPS, P, T_LAT), "rows": (2, HEADS * NT, P), "small": (2, 4, HEADS * NT),
        "hf": (NT_LAT, P, CH), "y": (KD, P, T_LAT),
    }
    s = {k: nc.dram_tensor(f"s_{k}", v, F32).ap() for k, v in scratch.items()}
    with ExitStack() as ctx:
        svec = ctx.enter_context(nc.sbuf_tensor("svec", [P, KD, 2], F32))
        with nc.sbuf_tensor("hidden", [P, HALF_T], F32) as hidden:
            project(nc, d, s, svec, hidden)
            if "hyena" in stages:
                hyena(nc, d, s, hidden)
        w_hi = ctx.enter_context(nc.sbuf_tensor("wo_hi", [P, KD, D], F32R))
        w_lo = ctx.enter_context(nc.sbuf_tensor("wo_lo", [P, KD, D], F32R))
        gate = ctx.enter_context(nc.sbuf_tensor("gate", [P, D], F32))
        if "mlstm" in stages:
            mlstm(nc, d, s, svec, w_hi, w_lo, gate)
        if "output" in stages:
            output(nc, d, s, w_hi, w_lo, gate, out)


def columns(v):
    return np.ascontiguousarray(v.reshape(-1, P).T)


def dft_tables():
    n1, k1 = np.arange(P), np.arange(K1)
    n2, k2 = np.arange(N2), np.arange(N2)
    ang = -2 * np.pi * np.outer(n1, k1 + 0.5) / N1
    outer = np.stack([np.cos(ang), np.sin(ang)], 1)
    fwd = np.zeros((NQ, 4, 2, N2, 4, 2, N2))
    inv = np.zeros((NQ, 4, 2, N2, 4, 2, N2))
    for q in range(NQ):
        for j in range(4):
            a = -2 * np.pi * (n2[:, None] * (NQ * j + q + 0.5) / N + n2[:, None] * k2 / N2)
            c, z = np.cos(a), np.sin(a)
            fwd[q, j, 0, :, j, 0, :], fwd[q, j, 1, :, j, 0, :] = c, -z
            fwd[q, j, 0, :, j, 1, :], fwd[q, j, 1, :, j, 1, :] = z, c
            c, z = c.T, -z.T
            inv[q, j, 0, :, j, 0, :], inv[q, j, 1, :, j, 0, :] = c, -z
            inv[q, j, 0, :, j, 1, :], inv[q, j, 1, :, j, 1, :] = z, c
    turned = np.empty_like(inv)
    turned[:, :, 0], turned[:, :, 1] = inv[:, :, 1], -inv[:, :, 0]
    fwd_re, fwd_im = np.empty_like(fwd), np.empty_like(fwd)
    fwd_re[:, :, :, :, :, 0], fwd_re[:, :, :, :, :, 1] = fwd[:, :, :, :, :, 0], fwd[:, :, :, :, :, 0]
    fwd_im[:, :, :, :, :, 0], fwd_im[:, :, :, :, :, 1] = fwd[:, :, :, :, :, 1], fwd[:, :, :, :, :, 1]
    fwd, fwd_re, fwd_im = [a.transpose(0, 2, 1, 3, 4, 5, 6).reshape(NQ, P, P) for a in (fwd, fwd_re, fwd_im)]
    inv, turned = [a.transpose(0, 1, 2, 3, 5, 6, 4).reshape(NQ, P, P) for a in (inv, turned)]
    ang = 2 * np.pi * np.outer(k1 + 0.5, n1 + N1 // 3) / N1
    back = np.stack([np.cos(ang), -np.sin(ang)], 1) * (2.0 / N)
    back = back.reshape(4, NQ, 2, P).transpose(1, 0, 2, 3).reshape(K1, 2, P)
    tables = np.stack([fwd, fwd_re, fwd_im, inv, turned], 0).transpose(2, 0, 1, 3)
    f = lambda a: np.ascontiguousarray(a.astype(np.float32))
    return f(outer), f(tables), f(back)


def filter_tables():
    f = np.float32
    pos = np.arange(T_LAT, dtype=f)
    bands = np.arange(1, 9, dtype=f)
    ang = f(2.0 * math.pi / T_LAT) * pos[:, None] * bands[None, :]
    feats = np.concatenate([(pos / f(T_LAT))[:, None], np.sin(ang), np.cos(ang)], -1).astype(f)
    lo, hi = math.log(1e-2) / 1.5, math.log(1e-2) / 0.3
    rates = np.abs(np.linspace(lo, hi, CH, dtype=f))
    offset = np.abs(pos - T_LAT // 2) / f(T_LAT / 2)
    window = np.exp(-offset[:, None] * rates).astype(f)
    window = window.reshape(P, N2, 4, P).transpose(2, 0, 1, 3)
    feats = feats.T.reshape(17, P, N2 // 2, 2).transpose(3, 0, 1, 2).reshape(2 * 17, T_LAT // 2)
    return np.ascontiguousarray(feats), np.ascontiguousarray(window)


def two_blocks(w):
    out = np.zeros((2 * w.shape[0], 2 * w.shape[1]), np.float32)
    out[:w.shape[0], :w.shape[1]] = w
    out[w.shape[0]:, w.shape[1]:] = w
    return out


def lay_out(a):
    a = {k: np.asarray(v) for k, v in a.items()}
    w = a["w_in"][0]
    cuts = np.cumsum([2 * CH, CH, CH, CH, 4 * HEADS, 3 * CH, CH])
    qk, v, o, zm, g, hy, zh = np.split(w, cuts[:-1], axis=1)
    wide = np.concatenate([qk[:, CH:], v, qk[:, :CH], hy, o, zm, zh], 1)
    w_in = wide.reshape(KD, P, N_SLOTS, SLOT).transpose(2, 1, 0, 3)
    w_gate = np.zeros((P, KD, P), np.float32)
    gbias = np.zeros((P, 1), np.float32)
    for kind in range(4):
        at = slice(32 * kind, 32 * kind + HEADS)
        w_gate[:, :, at] = g[:, kind * HEADS:(kind + 1) * HEADS].reshape(KD, P, HEADS).transpose(1, 0, 2)
        gbias[at, 0] = a["b_gates"][0, kind * HEADS:(kind + 1) * HEADS]
    wm = a["w_mod"][0].reshape(KD, P, 3 * D // SLOT, SLOT).transpose(2, 1, 0, 3)
    taps = np.concatenate([a["conv_qk_w"][0][:, CH:], a["conv_qk_w"][0][:, :CH], a["hy_conv_w"][0]], 1)
    bias = np.concatenate([a["conv_qk_b"][0][CH:], a["conv_qk_b"][0][:CH], a["hy_conv_b"][0]])
    coef = np.concatenate([taps, bias[None]], 0).reshape(4, 20, P).transpose(2, 1, 0)
    w3 = np.zeros((GROUPS, 2, HID, 2, 2, P), np.float32)
    for e in range(2):
        w3[:, e, :, :, e] = a["filt_w3"][0].reshape(HID, 2, GROUPS, P).transpose(2, 0, 1, 3)
    w3 = w3.reshape(GROUPS, P, 2, 2, P)
    outer, tables, back = dft_tables()
    feats, window = filter_tables()
    row = np.arange(P)
    before = row[:, None] <= row[None, :]
    far = np.float32(1e30)
    out = {
        "x": a["x"][0], "ctx": a["ctx"][0],
        "cvec": np.stack([columns(a["c"][0]), columns(a["c_ctx"])], 2),
        "w_mod": wm, "bmod": columns(a["b_mod"][0, :2 * D]), "bgate": a["b_mod"][0, 2 * D:][None],
        "pgain": columns(a["pre_gain"][0]), "post": a["post_gain"][0][None],
        "gbias": gbias, "w_gate": w_gate, "w_in": w_in, "coef": coef,
        "ident": np.eye(P, dtype=np.float32),
        "mask": np.stack([np.where(before, 0, far), np.where(before.T, 0, far)], 1).astype(np.float32),
        "mh_gain": a["mh_gain"][0][None],
        "outer": outer, "tables": tables, "back": back, "feats": feats, "window": window,
        "fw1": two_blocks(a["filt_w1"][0]), "fw2": two_blocks(a["filt_w2"][0]),
        "fw3": w3,
        "fcol": np.tile(np.stack([a["filt_b1"][0], a["filt_freq"][0, 0],
                                  a["filt_b2"][0], a["filt_freq"][0, 1]], 1), (2, 1)),
        "fbias": a["filt_bias"][0].reshape(2, 4, P).transpose(1, 0, 2)[:, None],
        "w_out": a["w_out"][0].reshape(KD, P, D).transpose(1, 0, 2),
    }
    return {k: np.ascontiguousarray(v) for k, v in out.items()}


def kernel(**inputs):
    from concourse import bacc
    from concourse.bass_utils import run_bass_kernel_spmd

    nc = bacc.Bacc("TRN2", target_bir_lowering=False, num_devices=1, dynamic_dma_scratch_size=1024)
    arrays = {f"in_{k}": v for k, v in lay_out(inputs).items()}
    d = {k[3:]: nc.dram_tensor(k, v.shape, mybir.dt.from_np(v.dtype), kind="ExternalInput").ap()
         for k, v in arrays.items()}
    out = nc.dram_tensor("out", (T_LAT, D), F32, kind="ExternalOutput").ap()
    build(nc, d, out)
    r = run_bass_kernel_spmd(nc, [arrays], core_ids=[0])
    return r.results[0]["out"].reshape(1, T_LAT, D)
```
